# Optimizing a Trainium2 kernel written in Bass

```python
import math
import jax, jax.numpy as jnp
from jax import lax
import numpy as np

D_MODEL = 1024
BATCH = 1
SEQ = 1024
DEPTH = 1

N_MLA_HEADS = 4
MLA_NOPE_DIM = 64
MLA_ROPE_DIM = 32
MLA_QK_DIM = MLA_NOPE_DIM + MLA_ROPE_DIM
MLA_V_DIM = 64
MLA_Q_RANK = 384
MLA_KV_RANK = 256
MLA_WIDTH = N_MLA_HEADS * MLA_V_DIM
N_FOX_HEADS = 4
FOX_HEAD_DIM = 64
FOX_WIDTH = N_FOX_HEADS * FOX_HEAD_DIM
FOX_FORGET_BIAS_INIT = 3.0
S5_GROUPS = 16
S5_GROUP_CH = 16
S5_STATE = 64
S5_WIDTH = S5_GROUPS * S5_GROUP_CH
N_BRANCHES = 3
BRANCH_WIDTH = 256
D_FF = 2816
CONV_WIDTH = 3
Q_BLOCK = 128
ROPE_THETA = 10000.0
NORM_EPS = 1e-6
NEG_INF = -1e30
IN_WIDTHS = (MLA_Q_RANK, MLA_KV_RANK, MLA_ROPE_DIM,
             FOX_WIDTH, FOX_WIDTH, FOX_WIDTH, N_FOX_HEADS,
             S5_WIDTH, N_BRANCHES * D_MODEL)
D_IN = sum(IN_WIDTHS)

kernel_name = "hybrid_mla_fox_s5_gated_trunk"

def rms_norm(x, gain):
    x32 = x.astype(jnp.float32)
    y = x32 * lax.rsqrt(jnp.mean(x32 * x32, axis=-1, keepdims=True) + NORM_EPS)
    return (y * gain.astype(jnp.float32)).astype(x.dtype)

def rope_tables(positions):
    inv_freq = ROPE_THETA ** (-jnp.arange(0, MLA_ROPE_DIM, 2, dtype=jnp.float32) / MLA_ROPE_DIM)
    ang = positions.astype(jnp.float32)[..., None] * inv_freq
    return jnp.cos(ang)[:, :, None, :], jnp.sin(ang)[:, :, None, :]

def apply_rope_tail(x, cos, sin):
    x_pass, x_rot = x[..., :MLA_NOPE_DIM], x[..., MLA_NOPE_DIM:]
    x1, x2 = jnp.split(x_rot, 2, axis=-1)
    rot = jnp.concatenate([x1 * cos - x2 * sin, x2 * cos + x1 * sin], axis=-1)
    return jnp.concatenate([x_pass, rot.astype(x.dtype)], axis=-1)

def causal_block_attention(q, k, v, log_forget_cum=None):
    seq = q.shape[1]
    scale = q.shape[-1] ** -0.5
    outs = []
    for i in range(seq // Q_BLOCK):
        q_lo, q_hi = i * Q_BLOCK, (i + 1) * Q_BLOCK
        qb, kb, vb = q[:, q_lo:q_hi], k[:, :q_hi], v[:, :q_hi]
        s = jnp.einsum('bqhd,bkhd->bhqk', qb, kb).astype(jnp.float32) * scale
        if log_forget_cum is not None:
            c_q = jnp.transpose(log_forget_cum[:, q_lo:q_hi], (0, 2, 1))[..., :, None]
            c_k = jnp.transpose(log_forget_cum[:, :q_hi], (0, 2, 1))[..., None, :]
            s = s + (c_q - c_k)
        mask = (q_lo + jnp.arange(Q_BLOCK))[:, None] >= jnp.arange(q_hi)[None, :]
        p = jax.nn.softmax(jnp.where(mask, s, NEG_INF), axis=-1).astype(v.dtype)
        outs.append(jnp.einsum('bhqk,bkhd->bqhd', p, vb))
    return jnp.concatenate(outs, axis=1)

def s5_branch(u, lam_re, lam_im, b_re, b_im, c_re, c_im, d, log_step, w_glu, b_glu):
    bsz, seq, _ = u.shape
    u32 = u.astype(jnp.float32).reshape(bsz, seq, S5_GROUPS, S5_GROUP_CH)
    lam = lax.complex(lam_re.astype(jnp.float32), lam_im.astype(jnp.float32))
    step = jnp.exp(log_step.astype(jnp.float32))[:, None]
    lam_bar = jnp.exp(lam * step)
    b_mat = lax.complex(b_re.astype(jnp.float32), b_im.astype(jnp.float32))
    b_bar = ((lam_bar - 1.0) / lam)[..., None] * b_mat
    bu = jnp.einsum('gph,bsgh->bsgp', b_bar, u32.astype(jnp.complex64))
    a = jnp.broadcast_to(lam_bar, bu.shape)

    def combine(e1, e2):
        a1, x1 = e1
        a2, x2 = e2
        return a1 * a2, a2 * x1 + x2

    _, state = lax.associative_scan(combine, (a, bu), axis=1)
    c_mat = lax.complex(c_re.astype(jnp.float32), c_im.astype(jnp.float32))
    y = jnp.real(jnp.einsum('ghp,bsgp->bsgh', c_mat, state)) + d.astype(jnp.float32) * u32
    y = jax.nn.gelu(y.reshape(bsz, seq, S5_WIDTH))
    y = y * jax.nn.sigmoid(y @ w_glu.astype(jnp.float32) + b_glu.astype(jnp.float32))
    return y.astype(u.dtype)

def causal_depthwise_conv(h, w):
    seq = h.shape[1]
    hp = jnp.pad(h, ((0, 0), (CONV_WIDTH - 1, 0), (0, 0)))
    return sum(w[j] * hp[:, j:j + seq] for j in range(CONV_WIDTH))

def mixer_block(h, cos, sin, w_in, q_lat_norm_g, w_uq, kv_lat_norm_g, w_ukv,
                mla_q_norm_g, mla_k_norm_g, fox_q_norm_g, fox_k_norm_g, fox_f_bias,
                s5_lambda_re, s5_lambda_im, s5_b_re, s5_b_im, s5_c_re, s5_c_im, s5_d,
                s5_log_step, s5_w_glu, s5_b_glu, w_branch, w_out):
    bsz, seq, _ = h.shape
    proj = h @ w_in
    split_points = np.cumsum(IN_WIDTHS)[:-1].tolist()
    c_q, c_kv, k_r, fq, fk, fv, f_logit, u, gate_logits = jnp.split(proj, split_points, axis=-1)

    q = jnp.einsum('bsr,rhd->bshd', rms_norm(c_q, q_lat_norm_g), w_uq)
    kv = jnp.einsum('bsr,rhd->bshd', rms_norm(c_kv, kv_lat_norm_g), w_ukv)
    k_nope, v_mla = kv[..., :MLA_NOPE_DIM], kv[..., MLA_NOPE_DIM:]
    k_rope = jnp.broadcast_to(k_r[:, :, None, :], (bsz, seq, N_MLA_HEADS, MLA_ROPE_DIM))
    k_mla = jnp.concatenate([k_nope, k_rope], axis=-1)
    q_mla = apply_rope_tail(rms_norm(q, mla_q_norm_g), cos, sin)
    k_mla = apply_rope_tail(rms_norm(k_mla, mla_k_norm_g), cos, sin)
    o_mla = causal_block_attention(q_mla, k_mla, v_mla).reshape(bsz, seq, MLA_WIDTH)

    q_fox = rms_norm(fq.reshape(bsz, seq, N_FOX_HEADS, FOX_HEAD_DIM), fox_q_norm_g)
    k_fox = rms_norm(fk.reshape(bsz, seq, N_FOX_HEADS, FOX_HEAD_DIM), fox_k_norm_g)
    v_fox = fv.reshape(bsz, seq, N_FOX_HEADS, FOX_HEAD_DIM)
    log_f = jax.nn.log_sigmoid((f_logit + fox_f_bias).astype(jnp.float32))
    cum_log_f = lax.cumsum(log_f, axis=1)
    o_fox = causal_block_attention(q_fox, k_fox, v_fox, cum_log_f).reshape(bsz, seq, FOX_WIDTH)

    o_s5 = s5_branch(u, s5_lambda_re, s5_lambda_im, s5_b_re, s5_b_im, s5_c_re, s5_c_im,
                     s5_d, s5_log_step, s5_w_glu, s5_b_glu)

    branches = jnp.stack([o_mla, o_fox, o_s5], axis=2)
    gates = jax.nn.sigmoid(gate_logits.reshape(bsz, seq, N_BRANCHES, D_MODEL))
    projected = jnp.einsum('bsnw,nwd->bsnd', branches, w_branch)
    merged = jnp.einsum('bsnd,bsnd->bsd', gates, projected)
    return merged @ w_out

def conv_gated_ffn(h, w_up, conv_w, w_down):
    up = causal_depthwise_conv(h @ w_up, conv_w)
    gate, val = jnp.split(up, 2, axis=-1)
    return (jax.nn.silu(gate) * val) @ w_down

def setup_inputs(seed: int = 0) -> dict:
    key = jax.random.key(seed)
    ks = iter(jax.random.split(key, 40))
    f32 = jnp.float32
    L = DEPTH

    def nrm(shape, scale):
        return scale * jax.random.normal(next(ks), shape, f32)

    def gain(shape):
        return 1.0 + nrm(shape, 0.02)

    x = nrm((BATCH, SEQ, D_MODEL), 1.0)
    offset = jax.random.randint(next(ks), (BATCH, 1), 0, 4096, dtype=jnp.int32)
    positions = offset + jnp.arange(SEQ, dtype=jnp.int32)[None, :]

    attn_norm_g = gain((L, D_MODEL))
    w_in = nrm((L, D_MODEL, D_IN), D_MODEL ** -0.5)
    q_lat_norm_g = gain((L, MLA_Q_RANK))
    w_uq = nrm((L, MLA_Q_RANK, N_MLA_HEADS, MLA_QK_DIM), MLA_Q_RANK ** -0.5)
    kv_lat_norm_g = gain((L, MLA_KV_RANK))
    w_ukv = nrm((L, MLA_KV_RANK, N_MLA_HEADS, MLA_NOPE_DIM + MLA_V_DIM), MLA_KV_RANK ** -0.5)
    mla_q_norm_g = gain((L, MLA_QK_DIM))
    mla_k_norm_g = gain((L, MLA_QK_DIM))
    fox_q_norm_g = gain((L, FOX_HEAD_DIM))
    fox_k_norm_g = gain((L, FOX_HEAD_DIM))
    fox_f_bias = FOX_FORGET_BIAS_INIT + nrm((L, N_FOX_HEADS), 0.5)
    s5_lambda_re = -0.5 + nrm((L, S5_GROUPS, S5_STATE), 0.01)
    s5_lambda_im = math.pi * jnp.arange(S5_STATE, dtype=f32) + nrm((L, S5_GROUPS, S5_STATE), 0.01)
    s5_b_re = nrm((L, S5_GROUPS, S5_STATE, S5_GROUP_CH), (2 * S5_GROUP_CH) ** -0.5)
    s5_b_im = nrm((L, S5_GROUPS, S5_STATE, S5_GROUP_CH), (2 * S5_GROUP_CH) ** -0.5)
    s5_c_re = nrm((L, S5_GROUPS, S5_GROUP_CH, S5_STATE), (2 * S5_STATE) ** -0.5)
    s5_c_im = nrm((L, S5_GROUPS, S5_GROUP_CH, S5_STATE), (2 * S5_STATE) ** -0.5)
    s5_d = nrm((L, S5_GROUPS, S5_GROUP_CH), 0.5)
    s5_log_step = jnp.log(jax.random.uniform(next(ks), (L, S5_GROUPS), f32, minval=0.001, maxval=0.1))
    s5_w_glu = nrm((L, S5_WIDTH, S5_WIDTH), S5_WIDTH ** -0.5)
    s5_b_glu = nrm((L, S5_WIDTH), 0.02)
    w_branch = nrm((L, N_BRANCHES, BRANCH_WIDTH, D_MODEL), BRANCH_WIDTH ** -0.5)
    w_out = nrm((L, D_MODEL, D_MODEL), D_MODEL ** -0.5)
    ffn_norm_g = gain((L, D_MODEL))
    w_up = nrm((L, D_MODEL, 2 * D_FF), D_MODEL ** -0.5)
    ffn_conv_w = nrm((L, CONV_WIDTH, 2 * D_FF), 0.2).at[:, CONV_WIDTH - 1].add(1.0)
    w_down = nrm((L, D_FF, D_MODEL), D_FF ** -0.5)
    return {"x": x, "positions": positions, "attn_norm_g": attn_norm_g, "w_in": w_in,
            "q_lat_norm_g": q_lat_norm_g, "w_uq": w_uq, "kv_lat_norm_g": kv_lat_norm_g,
            "w_ukv": w_ukv, "mla_q_norm_g": mla_q_norm_g, "mla_k_norm_g": mla_k_norm_g,
            "fox_q_norm_g": fox_q_norm_g, "fox_k_norm_g": fox_k_norm_g, "fox_f_bias": fox_f_bias,
            "s5_lambda_re": s5_lambda_re, "s5_lambda_im": s5_lambda_im, "s5_b_re": s5_b_re,
            "s5_b_im": s5_b_im, "s5_c_re": s5_c_re, "s5_c_im": s5_c_im, "s5_d": s5_d,
            "s5_log_step": s5_log_step, "s5_w_glu": s5_w_glu, "s5_b_glu": s5_b_glu,
            "w_branch": w_branch, "w_out": w_out, "ffn_norm_g": ffn_norm_g, "w_up": w_up,
            "ffn_conv_w": ffn_conv_w, "w_down": w_down}

def reference(x, positions, attn_norm_g, w_in, q_lat_norm_g, w_uq, kv_lat_norm_g, w_ukv,
              mla_q_norm_g, mla_k_norm_g, fox_q_norm_g, fox_k_norm_g, fox_f_bias,
              s5_lambda_re, s5_lambda_im, s5_b_re, s5_b_im, s5_c_re, s5_c_im, s5_d,
              s5_log_step, s5_w_glu, s5_b_glu, w_branch, w_out, ffn_norm_g, w_up,
              ffn_conv_w, w_down):
    cos, sin = rope_tables(positions)
    for l in range(DEPTH):
        h = rms_norm(x, attn_norm_g[l])
        x = x + mixer_block(h, cos, sin, w_in[l], q_lat_norm_g[l], w_uq[l], kv_lat_norm_g[l],
                            w_ukv[l], mla_q_norm_g[l], mla_k_norm_g[l], fox_q_norm_g[l],
                            fox_k_norm_g[l], fox_f_bias[l], s5_lambda_re[l], s5_lambda_im[l],
                            s5_b_re[l], s5_b_im[l], s5_c_re[l], s5_c_im[l], s5_d[l],
                            s5_log_step[l], s5_w_glu[l], s5_b_glu[l], w_branch[l], w_out[l])
        h = rms_norm(x, ffn_norm_g[l])
        x = x + conv_gated_ffn(h, w_up[l], ffn_conv_w[l], w_down[l])
    return x


_drawn_inputs = setup_inputs


def setup_inputs(seed=0):
    import zlib

    import numpy as np

    out = dict(_drawn_inputs(seed))
    spreads = {}
    factors = {'attn_norm_g': 8.0,
     'q_lat_norm_g': 8.0,
     'kv_lat_norm_g': 8.0,
     'mla_q_norm_g': 8.0,
     'mla_k_norm_g': 8.0,
     'fox_q_norm_g': 8.0,
     'fox_k_norm_g': 8.0,
     's5_lambda_re': 64.0,
     's5_lambda_im': 29.736,
     's5_b_re': 41.776,
     's5_b_im': 41.576,
     's5_c_re': 42.2,
     's5_c_im': 42.256,
     's5_log_step': 32.51,
     's5_w_glu': 3.739,
     's5_b_glu': 64.0,
     'ffn_norm_g': 3.5}
    for name, (base, spread) in spreads.items():
        noise = np.random.default_rng([zlib.crc32(name.encode()), seed]).standard_normal(out[name].shape)
        drawn = base * np.exp(spread * noise) if base else spread * noise
        out[name] = __import__('jax').numpy.asarray(drawn.astype(out[name].dtype))
    for name, factor in factors.items():
        out[name] = (out[name] * factor).astype(out[name].dtype)
    return out
```

```python
from contextlib import ExitStack
import math
import numpy as np

import concourse.bass as bass
from concourse import mybir

F32 = mybir.dt.float32
F32R = mybir.dt.float32r
BF16 = mybir.dt.bfloat16
I32 = mybir.dt.int32
ALU = mybir.AluOpType
ACT = mybir.ActivationFunctionType
AX = mybir.AxisListType

P = 128
T, D, KD = 1024, 1024, 8
TT = T // P
BANK = 512
Q_RANK, KV_RANK = 384, 256
H, NOPE, ROPE = 4, 64, 32
QK = NOPE + ROPE
VD = 64
FH, FD = 4, 64
GR, GC, ST = 16, 16, 64
CH = 8
NCH = T // CH
FF, CONV = 2816, 3
EPS = 1e-6
NEG = -1e30
C_Q, C_KV, C_KR = 0, Q_RANK, Q_RANK + KV_RANK
C_FQ = C_KR + ROPE
C_FK, C_FV = C_FQ + 256, C_FQ + 512
C_F = C_FQ + 768
C_U = C_F + FH
C_G = C_U + 256

RW = 132 * 256
FW = 70 * 256


class Chain:

    def __init__(self, sem):
        self.sem, self.n = sem, 0

    def on(self, eng, base=None):
        self.eng, self.base = eng, base
        return self

    def __call__(self, ins):
        ins.then_inc(self.sem, 1)
        self.n += 1
        self.eng.wait_ge(self.sem, self.n if self.base is None else self.base + self.n)
        return ins


class Memory:
    pass


class Programs:

    def __init__(self, scalar, vector, tensor, gpsimd=None, sync=None, done=None):
        self.scalar, self.vector, self.tensor = scalar, vector, tensor
        self.gpsimd, self.sync, self.done = gpsimd, sync, done


def cols(tensor, off, *dims):
    n = math.prod(dims)
    ap = tensor[:, off:off + n]
    if len(dims) == 1:
        return ap
    names = "abcd"[:len(dims)]
    return ap.rearrange(f"p ({' '.join(names)}) -> p {' '.join(names)}",
                        **{k: v for k, v in zip(names[1:], dims[1:])})


def setup(nc, ctx, ins):
    m = Memory()
    m.nc, m.ctx, m.ins = nc, ctx, ins
    m.sb = lambda name, shape, dt=F32: ctx.enter_context(nc.sbuf_tensor(name, shape, dt))
    m.scope, m.held = ctx.enter_context(ExitStack()), []

    def sem(name):
        m.held.append(m.scope.enter_context(nc.semaphore(name)))
        return m.held[-1]
    m.sem = sem
    m.R = m.sb("split_arena", [P, RW], F32R)
    m.F = m.sb("plain_arena", [P, FW], F32)
    m.ident = m.sb("ident", [P, P])
    m.identb = m.sb("identb", [P, P], BF16)
    m.maskb = m.sb("maskb", [P, P], BF16)
    m.vecs = m.sb("vecs", [P, 3 * P])
    m.colv = m.sb("colv", [P, 160])
    m.conv_w = m.colv[:, 0:132].rearrange("p (j f) -> p j f", j=CONV)
    m.g_attn, m.g_ffn = m.colv[:, 132:140], m.colv[:, 140:148]
    m.g_qlat, m.g_kvlat, m.b_glu = m.colv[:, 148:151], m.colv[:, 151:153], m.colv[:, 153:155]
    m.rowg = m.sb("rowg", [P, 2 * QK + 2 * FD + FH])
    m.stat = m.sb("stat", [P, 64])
    m.statb = m.sb("statb", [P, 64])
    m.cidx = m.sb("cidx", [P, P])
    m.ps = ctx.enter_context(nc.psum_tensor("ps", [P, 8, BANK], F32))
    m.h_hi = cols(m.R, 0, KD, T)
    m.h_lo = cols(m.R, KD * T, KD, T)
    m.dve_step, m.pool_step = (Chain(ctx.enter_context(nc.semaphore(n))) for n in ("dve_step", "pool_step"))
    m.scr_u = nc.dram_tensor("scr_u", (P, 8 * 256), F32, kind="Internal").ap()
    m.scr_lat = nc.dram_tensor("scr_lat", (P, TT * 672), F32, kind="Internal").ap()
    return m


def reuse_semaphores(m):
    with m.nc.Block() as block:
        @block.sync
        def _(sp):
            for s in m.held:
                sp.sem_clear(s)
    m.scope.close()
    m.scope, m.held = m.ctx.enter_context(ExitStack()), []


def f32(ap):
    return ap.bitcast(F32)


def norm_and_turn(m, tag, src_dma, gain, before=None, pool_first=None):
    nc = m.nc
    rows = cols(m.F, 0, TT, D)
    loaded = [m.sem(f"{tag}_loaded{i}") for i in range(TT)] if src_dma is not None else None
    sq_done, ms_done, rstd_done = m.sem(f"{tag}_sq"), m.sem(f"{tag}_ms"), m.sem(f"{tag}_rstd")
    scaled, turned, hi_done, lo_done = (m.sem(f"{tag}_{n}") for n in ("scaled", "turned", "hi", "lo"))
    scaled_to = cols(m.F, 0, TT, D) if src_dma is not None else m.rows_scaled
    ssq = m.stat[:, 0:TT]
    rstd = m.stat[:, 8:8 + TT]
    expo = m.stat[:, 16:16 + TT]

    def sync(sp):
        if src_dma is not None:
            for i in range(TT):
                sp.dma_start(rows[:, i, :], src_dma[i * P:(i + 1) * P, :]).then_inc(loaded[i], 16)

    def scalar(act):
        for i in range(TT):
            if loaded:
                act.wait_ge(loaded[i], 16)
            nc.scalar.activation(m.ps[:, 6:8, :].rearrange("p a b -> p (a b)"), rows[:, i, :], ACT.Square,
                                 accum_out=ssq[:, i:i + 1]).then_inc(sq_done, 1)
            act.wait_ge(sq_done, i + 1)
        n = 0
        for half in range(2):
            for k in range(KD):
                act.wait_ge(turned, n + 1)
                nc.scalar.activation(m.h_hi[:, k, half * BANK:(half + 1) * BANK], m.ps[:, n % 4, :],
                                     ACT.Copy, scale=gain[:, k:k + 1]).then_inc(hi_done, 1)
                n += 1

    def vector(dve):
        for i in range(TT):
            dve.wait_ge(sq_done, i + 1)
            nc.vector.tensor_scalar(ssq[:, i:i + 1], ssq[:, i:i + 1], 1.0 / D, EPS, ALU.mult, ALU.add).then_inc(ms_done, 1)
        for i in range(TT):
            dve.wait_ge(rstd_done, i + 1)
            nc.vector.tensor_scalar(scaled_to[:, i, :], rows[:, i, :], rstd[:, i:i + 1], None, ALU.mult).then_inc(scaled, 1)
        n = 0
        for half in range(2):
            for k in range(KD):
                dve.wait_ge(hi_done, n + 1)
                cut = slice(half * BANK, (half + 1) * BANK)
                nc.vector.scalar_tensor_tensor(out=m.h_lo[:, k, cut], in0=m.ps[:, n % 4, :], scalar=gain[:, k:k + 1],
                                               in1=f32(m.h_hi[:, k, cut]), op0=ALU.mult, op1=ALU.subtract).then_inc(lo_done, 1)
                n += 1

    def gpsimd(pool):
        m.pool_step.on(pool)
        m.pool_step(nc.gpsimd.memset(expo, -0.5))
        for i in range(TT):
            pool.wait_ge(ms_done, i + 1)
            nc.gpsimd.tensor_tensor(rstd[:, i:i + 1], ssq[:, i:i + 1], expo[:, i:i + 1], ALU.pow).then_inc(rstd_done, 1)

    def tensor(pe):
        n = 0
        for half in range(2):
            for k in range(KD):
                if n == 0:
                    pe.wait_ge(scaled, 4)
                if n == KD:
                    pe.wait_ge(scaled, 8)
                if n >= 4:
                    pe.wait_ge(lo_done, n - 3)
                for j in range(4):
                    t = nc.tensor.transpose(m.ps[:, n % 4, j * P:(j + 1) * P],
                                            scaled_to[:, 4 * half + j, k * P:(k + 1) * P], m.ident[:])
                t.then_inc(turned, 1)
                n += 1
    return Programs(scalar, vector, tensor, gpsimd, sync, lo_done)


def stage_load_norm_project(m):
    nc = m.nc
    vec_in, row_in, vec_turned, vec_done, const = (m.sem(n) for n in ("vec_in", "row_in", "vec_turned", "vec_done", "const"))
    nrm = norm_and_turn(m, "attn", m.ins["x"].rearrange("b t d -> (b t) d"), m.g_attn)

    chunks = [(0, 192), (192, 192), (C_KV, 288), (C_FQ, 256), (C_FK, 256), (C_FV, 260), (C_U, 256)]
    NW = 288
    m.lat = cols(m.F, 0, TT, 672)
    m.fqk = cols(m.F, 5376, TT, 512)
    m.fvf = cols(m.F, 5376 + 4096, TT, 260)
    m.u = cols(m.F, 11552, GR, CH, GC)
    raw = [cols(m.F, 13600 + i * 4 * NW, 4, NW) for i in range(2)]
    W0 = 2 * KD * T
    w_hi = [cols(m.R, W0 + i * 2 * KD * NW, KD, NW) for i in range(2)]
    w_lo = [cols(m.R, W0 + (2 * i + 1) * KD * NW, KD, NW) for i in range(2)]
    raw_in = [m.sem(f"pw_in{i}") for i in range(2)]
    w_hi_done, w_lo_done, prod, out_act, out_dve = (m.sem(n) for n in ("pw_hi", "pw_lo", "p_prod", "p_act", "p_dve"))
    spill = m.sem("spill")
    w_src = m.ins["w_in"][0].rearrange("(k p) n -> p k n", p=P)

    def dest(c, t):
        first, n = chunks[c]
        if first < C_FQ:
            return m.lat[:, t, first:first + n]
        if first < C_FV:
            return m.fqk[:, t, first - C_FQ:first - C_FQ + n]
        if first == C_FV:
            return m.fvf[:, t, :]
        return m.u[:, :, 7 - t, :]

    def made(n):
        width = chunks[n // TT][1]
        src = m.ps[:, n % 4, 0:width]
        return src.rearrange("p (g h) -> p g h", h=GC) if chunks[n // TT][0] == C_U else src

    nch = len(chunks)
    with nc.Block() as block:
        @block.sync
        def _(sp):
            nrm.sync(sp)
            cw = m.ins["ffn_conv_w"][0]
            sp.dma_start(m.vecs[0:44, :].rearrange("f (j c) -> f j c", j=CONV),
                         cw.rearrange("j (f c) -> f j c", c=P)).then_inc(vec_in, 16)
            at = 44
            for v in (m.ins["attn_norm_g"], m.ins["ffn_norm_g"], m.ins["q_lat_norm_g"], m.ins["kv_lat_norm_g"], m.ins["s5_b_glu"]):
                n = v.shape[1] // P
                sp.dma_start(m.vecs[at:at + n, 0:P], v[0].rearrange("(r c) -> r c", c=P)).then_inc(vec_in, 16)
                at += n
            at = 0
            for v in (m.ins["mla_q_norm_g"], m.ins["mla_k_norm_g"], m.ins["fox_q_norm_g"], m.ins["fox_k_norm_g"], m.ins["fox_f_bias"]):
                n = v.shape[1]
                sp.dma_start(m.rowg[:, at:at + n], v[0].partition_broadcast(P)).then_inc(row_in, 16)
                at += n
            for c, (first, n) in enumerate(chunks):
                for half in range(2):
                    if c >= 1:
                        sp.wait_ge(w_lo_done, 2 * (c - 1) + half + 1)
                    sp.dma_start(raw[half][:, :, 0:n], w_src[:, 4 * half:4 * half + 4, first:first + n]).then_inc(raw_in[half], 16)
            sp.wait_ge(out_act, 3 * TT // 2)
            sp.wait_ge(out_dve, 3 * TT // 2)
            sp.dma_start(m.scr_lat, m.lat.rearrange("p a b -> p (a b)")).then_inc(spill, 16)
            sp.wait_ge(out_act, nch * TT // 2)
            sp.wait_ge(out_dve, nch * TT // 2)
            sp.dma_start(m.scr_u, m.u.rearrange("p g s h -> p (g s h)")).then_inc(spill, 16)
            sp.wait_ge(spill, 32)

        @block.gpsimd
        def _(pool):
            m.pool_step.on(pool)
            m.pool_step(nc.gpsimd.memset(m.ident[:], 0.0))
            m.pool_step(nc.gpsimd.affine_select(out=m.ident[:], in_=m.ident[:], compare_op=ALU.not_equal, fill=1.0,
                                                base=0, pattern=[[-1, P]], channel_multiplier=1))
            m.pool_step(nc.gpsimd.tensor_copy(m.identb[:], m.ident[:]))
            m.pool_step(nc.gpsimd.memset(m.maskb[:], 0.0))
            nc.gpsimd.affine_select(out=m.maskb[:], in_=m.maskb[:], compare_op=ALU.is_ge, fill=NEG,
                                    base=0, pattern=[[-1, P]], channel_multiplier=1).then_inc(const, 1)
            pool.wait_ge(const, 1)
            nrm.gpsimd(pool)

        @block.tensor
        def _(pe):
            pe.wait_ge(const, 1)
            pe.wait_ge(vec_in, 96)
            for j in range(CONV):
                nc.tensor.transpose(m.ps[:, 5, j * P:j * P + 44], m.vecs[0:44, j * P:(j + 1) * P], m.ident[0:44, 0:44])
            nc.tensor.transpose(m.ps[:, 5, 3 * P:3 * P + 67], m.vecs[0:67, 0:P], m.ident[0:67, 0:67]).then_inc(vec_turned, 1)
            nrm.tensor(pe)
            pe.wait_ge(nrm.done, 2 * KD)
            n = 0
            for c, (first, width) in enumerate(chunks):
                pe.wait_ge(w_lo_done, 2 * c + 2)
                for t in range(TT):
                    bank = n % 4
                    if n >= 4:
                        pe.wait_ge(out_act if n % 2 == 0 else out_dve, n // 2 - 1)
                    for k in range(KD):
                        if first == C_U:
                            hi, lo = (a[:, k, :].rearrange("p (c s) -> p c s", s=8)[:, :, t] for a in (m.h_hi, m.h_lo))
                        else:
                            hi, lo = (a[:, k, t * P:(t + 1) * P] for a in (m.h_hi, m.h_lo))
                        wh, wl = w_hi[c % 2][:, k, 0:width], w_lo[c % 2][:, k, 0:width]
                        o = m.ps[:, bank, 0:width]
                        nc.tensor.matmul(o, hi, wh, start=(k == 0), stop=False)
                        nc.tensor.matmul(o, hi, wl, start=False, stop=False)
                        mm = nc.tensor.matmul(o, lo, wh, start=False, stop=(k == KD - 1))
                    mm.then_inc(prod, 1)
                    n += 1

        @block.scalar
        def _(act):
            act.wait_ge(vec_turned, 1)
            act.wait_ge(vec_done, 2)
            nrm.scalar(act)

            def split(c, half):
                n = chunks[c][1]
                act.wait_ge(raw_in[half], 16 * (c + 1))
                if c >= 2:
                    act.wait_ge(prod, (c - 1) * TT)
                nc.scalar.activation(w_hi[c % 2][:, 4 * half:4 * half + 4, 0:n], raw[half][:, :, 0:n], ACT.Copy).then_inc(w_hi_done, 1)
            for c in range(2):
                split(c, 0), split(c, 1)
            for n in range(nch * TT):
                if n % 2 == 0:
                    act.wait_ge(prod, n + 1)
                    nc.scalar.activation(dest(n // TT, n % TT), made(n), ACT.Copy).then_inc(out_act, 1)
                if n % TT == TT - 1 and n // TT + 2 < nch:
                    split(n // TT + 2, 0), split(n // TT + 2, 1)

        @block.vector
        def _(dve):
            dve.wait_ge(vec_turned, 1)
            nc.vector.tensor_copy(m.conv_w, m.ps[:, 5, 0:3 * P].rearrange("p (j c) -> p j c", j=CONV)[:, :, 0:44]).then_inc(vec_done, 1)
            nc.vector.tensor_copy(m.colv[:, 132:155], m.ps[:, 5, 3 * P + 44:3 * P + 67]).then_inc(vec_done, 1)
            dve.wait_ge(vec_done, 2)
            nrm.vector(dve)

            def split(c, half):
                n = chunks[c][1]
                dve.wait_ge(w_hi_done, 2 * c + half + 1)
                hi = w_hi[c % 2][:, 4 * half:4 * half + 4, 0:n]
                nc.vector.tensor_tensor(w_lo[c % 2][:, 4 * half:4 * half + 4, 0:n], raw[half][:, :, 0:n], f32(hi),
                                        ALU.subtract).then_inc(w_lo_done, 1)
            for c in range(2):
                split(c, 0), split(c, 1)
            for n in range(nch * TT):
                if n % 2 == 1:
                    dve.wait_ge(prod, n + 1)
                    nc.vector.tensor_copy(dest(n // TT, n % TT), made(n)).then_inc(out_dve, 1)
                if n % TT == TT - 1 and n // TT + 2 < nch:
                    split(n // TT + 2, 0), split(n // TT + 2, 1)
            dve.wait_ge(row_in, 80)


ATT_STEPS = H * TT


def attention(m, tag, kd, q_of, k_of, v_of, q_t, k_t, p_buf, pt_buf, branch, ready):
    nc, ps = m.nc, m.ps
    scores, negmax, exped, normed, filled, copied, pv, o_hi, o_lo, rs = (
        m.sem(f"{tag}_{n}") for n in ("scores", "negmax", "exp", "norm", "filled", "copied", "pv", "o_hi", "o_lo", "recip"))
    nmax, rsum, rinv = m.stat[:, 0:2], m.stat[:, 2:4], m.stat[:, 4:6]
    S = [m.ps[:, 0:2, :].rearrange("p b n -> p (b n)"), m.ps[:, 2:4, :].rearrange("p b n -> p (b n)")]

    fills, after_turn = [], {}
    order = []
    order.append(("qk", 0))
    for s in range(ATT_STEPS + 2):
        if s < ATT_STEPS:
            order.append(("s", s))
        if 1 <= s <= ATT_STEPS:
            order.append(("t", s - 1))
        if s >= 2:
            order.append(("v", s - 2))
        if s % TT == 5 and s // TT + 1 < H:
            order.append(("qk", s // TT + 1))
    qk_until, t_until = {}, {}
    for what, n in order:
        if what == "qk":
            fills += [("qk", n, w, half) for w in range(2) for half in range(2)]
            qk_until[n] = len(fills)
        elif what == "t":
            tiles = n % TT + 1
            fills += [("p", n, a, min(4, tiles - a)) for a in range(0, tiles, 4)]
            t_until[n] = len(fills)

    def tensor(pe):
        ready(pe)
        f = 0
        for what, n in order:
            h, i = divmod(n, TT)
            if what == "qk":
                h = n
                for w, (src, _) in enumerate(((q_of, q_t), (k_of, k_t))):
                    for half in range(2):
                        if f >= 2:
                            pe.wait_ge(copied, f - 1)
                        for j in range(4):
                            tr = nc.tensor.transpose(ps[0:kd, 4 + f % 2, j * P:(j + 1) * P], src(h, 4 * half + j), m.ident[:])
                        tr.then_inc(filled, 1)
                        f += 1
            elif what == "s":
                if i == 0:
                    pe.wait_ge(copied, qk_until[h])
                if n >= 2:
                    pe.wait_ge(exped, n - 1)
                keys = (i + 1) * P
                for a in range(0, keys, BANK):
                    b = min(keys, a + BANK)
                    diag = b == keys
                    mm = nc.tensor.matmul(S[n % 2][:, a:b], q_t[h % 2][0:kd, i * P:(i + 1) * P], k_t[h % 2][0:kd, a:b],
                                          start=True, stop=not diag)
                mm = nc.tensor.matmul(S[n % 2][:, keys - P:keys], m.identb[:], m.maskb[:], start=False, stop=True)
                mm.then_inc(scores, 1)
            elif what == "t":
                pe.wait_ge(normed, n + 1)
                for a in range(0, i + 1, 4):
                    pe.wait_ge(copied, f - 1)
                    for j in range(a, min(a + 4, i + 1)):
                        tr = nc.tensor.transpose(ps[:, 4 + f % 2, (j - a) * P:(j - a + 1) * P],
                                                 p_buf[n % 2][:, j * P:(j + 1) * P], m.ident[:])
                    tr.then_inc(filled, 1)
                    f += 1
            else:
                pe.wait_ge(copied, t_until[n])
                g = n // 4
                if i % 4 == 0 and g >= 2:
                    pe.wait_ge(o_lo, g - 1)
                rows = slice(64 * (h % 2), 64 * (h % 2) + 64)
                for j in range(i + 1):
                    mm = nc.tensor.matmul(ps[rows, 6 + g % 2, (i % 4) * P:(i % 4 + 1) * P], v_of(h, j),
                                          pt_buf[n % 2][:, j * P:(j + 1) * P], start=(j == 0), stop=(j == i))
                mm.then_inc(pv, 1)

    def out_rows(g):
        h, half = divmod(g, 2)
        rows = slice(64 * (h % 2), 64 * (h % 2) + 64)
        k = 2 * branch + h // 2
        return rows, k, slice(half * BANK, (half + 1) * BANK)

    def scalar(act):
        f = 0
        for what, n in order:
            if what == "s":
                keys = (n % TT + 1) * P
                act.wait_ge(negmax, n + 1)
                if n >= 2:
                    act.wait_ge(filled, t_until[n - 2])
                    act.wait_ge(rs, n - 1)
                nc.scalar.activation(p_buf[n % 2][:, 0:keys], S[n % 2][:, 0:keys], ACT.Exp, bias=nmax[:, n % 2:n % 2 + 1],
                                     accum_out=rsum[:, n % 2:n % 2 + 1]).then_inc(exped, 1)
                continue
            if what in ("qk", "t"):
                while f < len(fills) and fills[f][0] == ("qk" if what == "qk" else "p") and fills[f][1] == n:
                    act.wait_ge(filled, f + 1)
                    if what == "qk":
                        _, h, w, half = fills[f]
                        if half == 0 and w == 0 and h >= 2:
                            act.wait_ge(scores, (h - 1) * TT)
                        dst = (q_t, k_t)[w][h % 2][0:kd, half * BANK:(half + 1) * BANK]
                        nc.scalar.activation(dst, ps[0:kd, 4 + f % 2, :], ACT.Copy).then_inc(copied, 1)
                    else:
                        _, s, a, c = fills[f]
                        if a == 0 and s >= 2:
                            act.wait_ge(pv, s - 1)
                        nc.scalar.activation(pt_buf[s % 2][:, a * P:(a + c) * P], ps[:, 4 + f % 2, 0:c * P], ACT.Copy).then_inc(copied, 1)
                    f += 1
            if what == "v" and n % 4 == 3:
                g = n // 4
                rows, k, cut = out_rows(g)
                act.wait_ge(pv, n + 1)
                nc.scalar.activation(m.br_hi[rows, k, cut], ps[rows, 6 + g % 2, :], ACT.Copy).then_inc(o_hi, 1)

    def vector(dve):
        for what, n in order:
            if what == "s":
                keys = (n % TT + 1) * P
                dve.wait_ge(scores, n + 1)
                if n >= 2:
                    dve.wait_ge(exped, n - 1)
                nc.vector.tensor_reduce(nmax[:, n % 2:n % 2 + 1], S[n % 2][:, 0:keys], AX.X, ALU.max, negate=True).then_inc(negmax, 1)
            elif what == "t":
                keys = (n % TT + 1) * P
                dve.wait_ge(exped, n + 1)
                nc.vector.reciprocal(rinv[:, n % 2:n % 2 + 1], rsum[:, n % 2:n % 2 + 1]).then_inc(rs, 1)
                dve.wait_ge(rs, n + 1)
                nc.vector.tensor_scalar(p_buf[n % 2][:, 0:keys], p_buf[n % 2][:, 0:keys], rinv[:, n % 2:n % 2 + 1], None,
                                        ALU.mult).then_inc(normed, 1)
            elif what == "v" and n % 4 == 3:
                g = n // 4
                rows, k, cut = out_rows(g)
                dve.wait_ge(o_hi, g + 1)
                nc.vector.tensor_tensor(m.br_lo[rows, k, cut], ps[rows, 6 + g % 2, :], f32(m.br_hi[rows, k, cut]),
                                        ALU.subtract).then_inc(o_lo, 1)
    return Programs(scalar, vector, tensor)


def stage_fox(m):
    nc = m.nc
    ndim = 2 * TT * FH
    qk = m.fqk.rearrange("p t (g d) -> p (t g) d", d=FD)
    KA = FD + 2
    aug = cols(m.F, 0, TT, 2 * FH, KA)
    sq = cols(m.F, 11552, ndim, FD)
    ssq, rstd, expo = m.stat[:, 0:ndim], m.statb[:, 0:ndim], cols(m.F, 15648, ndim)
    small = [cols(m.F, 15712 + 32 * i, TT, FH) for i in range(12)]
    z, e, den, s1, s2, acc, tot, pre, cum, ez, one_c, _ = small
    ones = cols(m.F, 16128, P)
    upper = cols(m.F, 16256, P)
    q_t = [cols(m.F, 5376 + i * T, T) for i in range(2)]
    k_t = [cols(m.F, 5376 + (2 + i) * T, T) for i in range(2)]
    p_buf = [cols(m.F, 11552 + i * T, T) for i in range(2)]
    pt_buf = [cols(m.F, 11552 + (2 + i) * T, T) for i in range(2)]
    W0 = 2 * KD * T
    m.br_hi = cols(m.R, W0, 6, T)
    m.br_lo = cols(m.R, W0 + 6 * T, 6, T)
    sq_done, ms_done, rstd_done, const, z_done, e_done, log_done, sum_done, prep = (
        m.sem(f"fox_{n}") for n in ("sq", "ms", "rstd", "const", "z", "e", "log", "sum", "prep"))
    gq, gk, fb = m.rowg[:, 192:256], m.rowg[:, 256:320], m.rowg[:, 320:324]

    def ready(pe):
        pe.wait_ge(prep, 1)
    att = attention(m, "fox", KA, lambda h, t: aug[:, t, h, :], lambda h, t: aug[:, t, FH + h, :],
                    lambda h, j: m.fvf[:, j, h * FD:(h + 1) * FD], q_t, k_t, p_buf, pt_buf, 1, ready)

    with nc.Block() as block:
        @block.gpsimd
        def _(pool):
            m.pool_step.on(pool)
            nc.gpsimd.memset(expo, -0.5).then_inc(const, 1)
            nc.gpsimd.memset(ones, 1.0).then_inc(const, 1)
            pool.wait_ge(const, 2)
            nc.gpsimd.affine_select(out=upper, in_=ones, compare_op=ALU.is_ge, fill=0.0, base=0,
                                    pattern=[[1, P]], channel_multiplier=-1).then_inc(const, 1)
            pool.wait_ge(ms_done, 1)
            nc.gpsimd.tensor_tensor(rstd, ssq, expo, ALU.pow).then_inc(rstd_done, 1)

        @block.scalar
        def _(act):
            act.wait_ge(z_done, 1)
            nc.scalar.activation(e, ez, ACT.Exp).then_inc(e_done, 1)
            nc.scalar.activation(sq, qk, ACT.Square).then_inc(sq_done, 1)
            att.scalar(act)

        @block.tensor
        def _(pe):
            pe.wait_ge(const, 3)
            pe.wait_ge(log_done, 1)
            nc.tensor.matmul(m.ps[:, 7, 0:32], upper, z.rearrange("p t h -> p (t h)"), start=True, stop=True)
            nc.tensor.matmul(m.ps[:, 7, 32:64], ones, z.rearrange("p t h -> p (t h)"), start=True, stop=True).then_inc(sum_done, 1)
            att.tensor(pe)

        @block.vector
        def _(dve):
            step = m.dve_step.on(dve)
            V = nc.vector
            step(V.tensor_tensor(z, m.fvf[:, :, 256:260], fb.unsqueeze(1).to_broadcast([P, TT, FH]), ALU.add))
            V.scalar_tensor_tensor(out=ez, in0=z, scalar=-1.0, in1=z, op0=ALU.mult, op1=ALU.min).then_inc(z_done, 1)
            step(V.tensor_scalar(gq, gq, float(FD) ** -0.5, None, ALU.mult))
            dve.wait_ge(e_done, 1)
            step(V.tensor_scalar(den, e, 2.0, None, ALU.add))
            step(V.reciprocal(den, den))
            step(V.tensor_tensor(s1, e, den, ALU.mult))
            step(V.tensor_tensor(s2, s1, s1, ALU.mult))
            step(V.tensor_scalar(acc, s2, 2.0 / 17, 2.0 / 15, ALU.mult, ALU.add))
            for k in (13, 11, 9, 7, 5, 3, 1):
                step(V.tensor_tensor(acc, acc, s2, ALU.mult))
                step(V.tensor_scalar(acc, acc, 2.0 / k, None, ALU.add))
            step(V.tensor_tensor(acc, acc, s1, ALU.mult))
            V.scalar_tensor_tensor(out=z, in0=z, scalar=0.0, in1=acc, op0=ALU.min, op1=ALU.subtract).then_inc(log_done, 1)
            dve.wait_ge(sq_done, 1)
            step(V.tensor_reduce(ssq, sq, AX.X, ALU.add))
            V.tensor_scalar(ssq, ssq, 1.0 / FD, EPS, ALU.mult, ALU.add).then_inc(ms_done, 1)
            dve.wait_ge(sum_done, 1)
            step(V.tensor_copy(tot.rearrange("p t h -> p (t h)"), m.ps[:, 7, 32:64]))
            step(V.memset(pre[:, 0, :], 0.0))
            for t in range(1, TT):
                step(V.tensor_tensor(pre[:, t, :], pre[:, t - 1, :], tot[:, t - 1, :], ALU.add))
            step(V.tensor_tensor(cum, m.ps[:, 7, 0:32].rearrange("p (t h) -> p t h", h=FH), pre, ALU.add))
            step(V.memset(aug[:, :, 0:FH, FD:FD + 1], 1.0))
            step(V.tensor_copy(aug[:, :, 0:FH, FD + 1], cum))
            step(V.tensor_scalar(aug[:, :, FH:2 * FH, FD], cum, -1.0, None, ALU.mult))
            step(V.memset(aug[:, :, FH:2 * FH, FD + 1:FD + 2], 1.0))
            dve.wait_ge(rstd_done, 1)
            step(V.tensor_tensor(sq, qk, rstd.unsqueeze(2).to_broadcast([P, ndim, FD]), ALU.mult))
            sqv = sq.rearrange("p (t g) d -> p t g d", g=2 * FH)
            step(V.tensor_tensor(aug[:, :, 0:FH, 0:FD], sqv[:, :, 0:FH, :],
                                 gq.unsqueeze(1).unsqueeze(1).to_broadcast([P, TT, FH, FD]), ALU.mult))
            V.tensor_tensor(aug[:, :, FH:2 * FH, 0:FD], sqv[:, :, FH:2 * FH, :],
                            gk.unsqueeze(1).unsqueeze(1).to_broadcast([P, TT, FH, FD]), ALU.mult).then_inc(prep, 1)
            att.vector(dve)


INV_FREQ = [float(f) for f in (np.float32(10000.0) ** (-np.arange(0, ROPE, 2, dtype=np.float32) / np.float32(ROPE)))]
TWO_PI = 2 * math.pi
PI_A = 6.28125
PI_B = float(np.float32(round((TWO_PI - PI_A) * 2 ** 22) / 2 ** 22))
PI_C = TWO_PI - PI_A - PI_B
ROUND = 1.5 * 2 ** 23
PI32 = 3.1415925


def reduced(nc, step, ang, turns, absang):
    V = nc.vector
    step(V.tensor_scalar(turns, ang, 1.0 / TWO_PI, ROUND, ALU.mult, ALU.add))
    step(V.tensor_scalar(turns, turns, ROUND, None, ALU.subtract))
    for part in (PI_A, PI_B, PI_C):
        step(V.scalar_tensor_tensor(out=ang, in0=turns, scalar=-part, in1=ang, op0=ALU.mult, op1=ALU.add))
    step(V.tensor_scalar(ang, ang, PI32, -PI32, ALU.min, ALU.max))
    step(V.scalar_tensor_tensor(out=absang, in0=ang, scalar=-1.0, in1=ang, op0=ALU.mult, op1=ALU.min))
    return V.tensor_scalar(absang, absang, math.pi / 2, None, ALU.add)


def stage_mla(m):
    nc = m.nc
    lat = cols(m.F, 0, TT, 672)
    lat_t = cols(m.F, 5376, 5, T)
    w_uq = cols(m.F, 10496, 3, H * QK)
    w_ukv = cols(m.F, 11648, 2, H * 2 * NOPE)
    q = cols(m.F, 12672, TT, H, QK)
    kr = cols(m.F, 15744, TT, ROPE)
    kv = cols(m.F, 0, TT, H, 2 * NOPE)
    k = cols(m.F, 5376, TT, H, QK)
    v = cols(m.F, 10496, TT, H, VD)
    lsq = cols(m.F, 12672, TT, Q_RANK)
    sq = cols(m.F, 0, TT * H, QK)
    ang = cols(m.F, 17024, TT, ROPE // 2)
    sin, cos, turns, t1 = (cols(m.F, 17152 + i * 128, TT, ROPE // 2) for i in range(4))
    pos_f, inv_freq, pos_i, pos8 = (cols(m.F, 17792, TT), cols(m.F, 17800, ROPE // 2), cols(m.F, 16000, P), cols(m.F, 16128, P))
    tmp = [cols(m.F, 16000 + i * 512, TT, H, ROPE // 2) for i in range(2)]
    q_t = [cols(m.F, i * T, T) for i in range(2)]
    k_t = [cols(m.F, (2 + i) * T, T) for i in range(2)]
    p_buf = [cols(m.F, 4096, T), cols(m.F, 16000, T)]
    pt_buf = [cols(m.F, 8448 + i * T, T) for i in range(2)]
    ssq, rstd, expo = m.stat[:, 0:48], m.statb[:, 0:48], cols(m.F, 17824, 48)
    gq, gk = m.rowg[:, 0:QK], m.rowg[:, QK:2 * QK]

    lat_in, w_in, pos_in, const, pos_t, sq_done, ms_done, rstd_done, ang_done, rope_done, scaled, filled, copied, q_prod, kv_prod, q_out, kv_out, prep = (
        m.sem(f"mla_{n}") for n in ("lat_in", "w_in", "pos_in", "const", "pos_t", "sq", "ms", "rstd", "ang", "sincos", "scaled",
                                    "filled", "copied", "q_prod", "kv_prod", "q_out", "kv_out", "prep"))

    pos_t_done = m.sem("mla_pos_t_done")

    def ready(pe):
        pe.wait_ge(prep, 1)
    att = attention(m, "mlaa", QK, lambda h, t: q[:, t, h, :], lambda h, t: k[:, t, h, :],
                    lambda h, j: v[:, j, h, :], q_t, k_t, p_buf, pt_buf, 0, ready)
    NQF = 3 * 2
    with nc.Block() as block:
        @block.sync
        def _(sp):
            sp.dma_start(lat.rearrange("p a b -> p (a b)"), m.scr_lat).then_inc(lat_in, 16)
            sp.dma_start(w_uq, m.ins["w_uq"][0].rearrange("(k p) h d -> p k (h d)", p=P)).then_inc(w_in, 16)
            sp.dma_start(w_ukv, m.ins["w_ukv"][0].rearrange("(k p) h d -> p k (h d)", p=P)).then_inc(w_in, 16)
            sp.dma_start(pos_i.bitcast(I32)[0:TT, :], m.ins["positions"][0].rearrange("(i p) -> i p", p=P)).then_inc(pos_in, 16)

        @block.gpsimd
        def _(pool):
            nc.gpsimd.memset(expo, -0.5).then_inc(const, 1)
            for j, f in enumerate(INV_FREQ):
                nc.gpsimd.memset(inv_freq[:, j:j + 1], f).then_inc(const, 1)
            pool.wait_ge(const, 1 + len(INV_FREQ))
            for n, (a, b) in enumerate(((0, 16), (16, 48), (16, 48))):
                pool.wait_ge(ms_done, n + 1)
                if n == 2:
                    a, b = 16, 48
                nc.gpsimd.tensor_tensor(rstd[:, a:b], ssq[:, a:b], expo[:, a:b], ALU.pow).then_inc(rstd_done, 1)

        @block.scalar
        def _(act):
            act.wait_ge(ang_done, 1)
            nc.scalar.activation(sin, ang, ACT.Sin).then_inc(rope_done, 1)
            nc.scalar.activation(cos, turns, ACT.Sin).then_inc(rope_done, 1)
            for f in range(10):
                act.wait_ge(filled, f + 1)
                r, half = divmod(f, 2)
                g = m.g_qlat[:, r:r + 1] if r < 3 else m.g_kvlat[:, r - 3:r - 2]
                nc.scalar.activation(lat_t[:, r, half * BANK:(half + 1) * BANK], m.ps[:, f % 4, :], ACT.Copy, scale=g).then_inc(copied, 1)
            for t in range(TT):
                act.wait_ge(q_prod, t + 1)
                nc.scalar.activation(q[:, t].rearrange("p h d -> p (h d)"), m.ps[:, t % 4, 0:H * QK], ACT.Copy).then_inc(q_out, 1)
            att.scalar(act)

        @block.tensor
        def _(pe):
            pe.wait_ge(pos_t, 1)
            nc.tensor.transpose(m.ps[:, 7, 0:TT], pos8[0:TT, :], m.ident[0:TT, 0:TT]).then_inc(pos_t_done, 1)
            pe.wait_ge(scaled, 2)
            f = 0
            for r in range(5):
                for half in range(2):
                    if f >= 4:
                        pe.wait_ge(copied, f - 3)
                    for j in range(4):
                        tr = nc.tensor.transpose(m.ps[:, f % 4, j * P:(j + 1) * P], lat[:, 4 * half + j, r * P:(r + 1) * P], m.ident[:])
                    tr.then_inc(filled, 1)
                    f += 1
            pe.wait_ge(copied, 10)
            pe.wait_ge(w_in, 32)
            for t in range(TT):
                if t >= 4:
                    pe.wait_ge(q_out, t - 3)
                for r in range(3):
                    mm = nc.tensor.matmul(m.ps[:, t % 4, 0:H * QK], lat_t[:, r, t * P:(t + 1) * P], w_uq[:, r, :], start=(r == 0), stop=(r == 2))
                mm.then_inc(q_prod, 1)
                if t >= 2:
                    pe.wait_ge(kv_out, t - 1)
                for r in range(2):
                    mm = nc.tensor.matmul(m.ps[:, 4 + t % 2, :], lat_t[:, 3 + r, t * P:(t + 1) * P], w_ukv[:, r, :], start=(r == 0), stop=(r == 1))
                mm.then_inc(kv_prod, 1)
            att.tensor(pe)

        @block.vector
        def _(dve):
            step = m.dve_step.on(dve)
            V = nc.vector
            dve.wait_ge(pos_in, 16)
            V.tensor_copy(pos8[0:TT, :], pos_i.bitcast(I32)[0:TT, :]).then_inc(pos_t, 1)
            step(V.tensor_scalar(gq, gq, float(QK) ** -0.5, None, ALU.mult))
            dve.wait_ge(lat_in, 16)
            for n, (a, b) in enumerate(((0, Q_RANK), (Q_RANK, Q_RANK + KV_RANK))):
                part = lsq[:, :, 0:b - a]
                step(V.tensor_tensor(part, lat[:, :, a:b], lat[:, :, a:b], ALU.mult))
                step(V.tensor_reduce(ssq[:, 8 * n:8 * n + 8], part, AX.X, ALU.add))
                ins = V.tensor_scalar(ssq[:, 8 * n:8 * n + 8], ssq[:, 8 * n:8 * n + 8], 1.0 / (b - a), EPS, ALU.mult, ALU.add)
                ins.then_inc(ms_done, 1) if n else step(ins)
            dve.wait_ge(pos_t_done, 1)
            step(V.tensor_copy(pos_f, m.ps[:, 7, 0:TT]))
            dve.wait_ge(const, 1 + len(INV_FREQ))
            step(V.tensor_copy(t1, pos_f.unsqueeze(2).to_broadcast([P, TT, ROPE // 2])))
            step(V.tensor_tensor(ang, t1, inv_freq.unsqueeze(1).to_broadcast([P, TT, ROPE // 2]), ALU.mult))
            reduced(nc, step, ang, t1, turns).then_inc(ang_done, 1)
            dve.wait_ge(rstd_done, 1)
            for n, (a, b) in enumerate(((0, Q_RANK), (Q_RANK, Q_RANK + KV_RANK))):
                V.tensor_tensor(lat[:, :, a:b], lat[:, :, a:b], rstd[:, 8 * n:8 * n + 8].unsqueeze(2).to_broadcast([P, TT, b - a]),
                                ALU.mult).then_inc(scaled, 1)
            step(V.tensor_copy(kr, lat[:, :, C_KR:C_KR + ROPE]))
            for t in range(TT):
                dve.wait_ge(kv_prod, t + 1)
                V.tensor_copy(kv[:, t].rearrange("p h d -> p (h d)"), m.ps[:, 4 + t % 2, :]).then_inc(kv_out, 1)
            dve.wait_ge(kv_out, TT)
            step(V.tensor_copy(k[:, :, :, 0:NOPE], kv[:, :, :, 0:NOPE]))
            step(V.tensor_copy(k[:, :, :, NOPE:QK], kr.unsqueeze(2).to_broadcast([P, TT, H, ROPE])))
            step(V.tensor_copy(v, kv[:, :, :, NOPE:]))
            dve.wait_ge(q_out, TT)
            dve.wait_ge(rope_done, 2)
            for n, (a, g) in enumerate(((k, gk), (q, gq))):
                flat = a.rearrange("p t h d -> p (t h) d")
                step(V.tensor_tensor(sq, flat, flat, ALU.mult))
                step(V.tensor_reduce(ssq[:, 16:48], sq, AX.X, ALU.add))
                V.tensor_scalar(ssq[:, 16:48], ssq[:, 16:48], 1.0 / QK, EPS, ALU.mult, ALU.add).then_inc(ms_done, 1)
                dve.wait_ge(rstd_done, 2 + n)
                step(V.tensor_tensor(sq, flat, rstd[:, 16:48].unsqueeze(2).to_broadcast([P, TT * H, QK]), ALU.mult))
                step(V.tensor_tensor(flat, sq, g.unsqueeze(1).to_broadcast([P, TT * H, QK]), ALU.mult))
                x1, x2 = a[:, :, :, NOPE:NOPE + ROPE // 2], a[:, :, :, NOPE + ROPE // 2:QK]
                sb, cb = (z.unsqueeze(2).to_broadcast([P, TT, H, ROPE // 2]) for z in (sin, cos))
                step(V.tensor_tensor(tmp[0], x1, sb, ALU.mult))
                step(V.tensor_tensor(tmp[1], x2, sb, ALU.mult))
                step(V.tensor_tensor(x1, x1, cb, ALU.mult))
                step(V.tensor_tensor(x2, x2, cb, ALU.mult))
                step(V.tensor_tensor(x1, x1, tmp[1], ALU.subtract))
                last = V.tensor_tensor(x2, x2, tmp[0], ALU.add)
                step(last) if n == 0 else last.then_inc(prep, 1)
            att.vector(dve)


def stage_s5(m):
    nc = m.nc
    J = GR // 2
    u = cols(m.F, 0, GR, CH, GC)
    u_t = cols(m.F, 2048, GR, NCH)
    m_re = cols(m.F, 4096, J, 2, 9, GC)
    m_im = cols(m.F, 6400, J, 2, 9, GC)
    b_rep = [cols(m.F, 8704 + i * 1024, J, CH, GC) for i in range(2)]
    w = [cols(m.F, 10752 + i * 1024, J, CH, GC) for i in range(2)]
    w_t = [cols(m.F, 12800 + i * 1024, J, P) for i in range(2)]
    kk = cols(m.F, 14848, GR, CH * GC)
    toep = cols(m.F, 10752, GR, CH * GC)
    tab = [cols(m.F, 8704 + i * 1024, J, NCH) for i in range(2)]
    z_in = [cols(m.F, 14848 + i * 1024, J, NCH) for i in range(2)]
    z = [cols(m.F, 12800 + i * 1024, J, NCH) for i in range(2)]
    s_prev = [cols(m.F, 14848 + i * 1024, J, NCH) for i in range(2)]
    tmp, rho = cols(m.F, 0, J, NCH), cols(m.F, 1024, J, NCH)
    y = cols(m.F, 12800, CH, GR, GC)
    y_t = cols(m.F, 8704, 2, NCH, CH)
    w_glu = cols(m.F, 0, 2, GR * GC)
    sg = [cols(m.F, 512 + i * BANK, BANK) for i in range(2)]
    at = [16896]

    def small(*dims):
        n = math.prod(dims)
        at[0] += n
        assert at[0] <= FW
        return cols(m.F, at[0] - n, *dims)
    b = [small(J, GC), small(J, GC)]
    p9, a9, t9, e9, l_re, l_im = (small(J, 9) for _ in range(6))
    lre, lim, stp, a1, th, tt, ta, q_re, q_im, den, t8 = (small(J) for _ in range(11))
    ki, mask16 = small(9), small(GC)
    crow = [m.vecs[:, i * P:(i + 1) * P] for i in range(2)]
    rows = cols(m.F, 14848, 3 * P)
    bb = [cols(m.F, 15232 + i * 128, J, GC) for i in range(2)]
    cc = [cols(m.F, 15488 + i * 128, J, GC) for i in range(2)]
    d_row = cols(m.F, 15744, GR, GC)
    cidx = cols(m.F, 16000, NCH)
    pq = [cols(m.F, 16128 + i * 128, J, GC) for i in range(4)]
    names = ("u_in", "p_in", "r_in", "c_in", "step_b", "row_t", "row_c", "exp1", "cst", "ang9", "sc9", "w_rdy", "b_rdy", "w_ps",
             "w_cp", "u_ps", "u_cp", "k_ps", "k_cp", "toep_in", "x_ps", "tab_a", "tab_s", "s_rdy", "y_ps", "y_cp", "yt_ps", "yt_cp",
             "zero", "glu_in", "g_ps", "g_sg", "g_y", "g_hi", "g_lo", "cidx", "rho")
    s = {n: m.sem(f"s5_{n}") for n in names}
    ps = m.ps
    cidx_keep = m.cidx[:]

    def y_out(f):
        return cols(m.F, 1536 + f * BANK, BANK)

    with nc.Block() as block:
        @block.sync
        def _(sp):
            for i, v in enumerate((m.ins["s5_lambda_re"], m.ins["s5_lambda_im"])):
                sp.dma_start(rows[0:J, i * P:(i + 1) * P], v[0].rearrange("(j g) p -> j (g p)", g=2)).then_inc(s["r_in"], 16)
            sp.dma_start(stp[0:J, 0:2], m.ins["s5_log_step"][0].rearrange("(j g) -> j g", g=2)).then_inc(s["r_in"], 16)
            for i, v in enumerate((m.ins["s5_c_re"], m.ins["s5_c_im"])):
                vj = v[0].rearrange("(j g) h p -> g j h p", g=2)
                for g in range(2):
                    for j in range(J):
                        sp.dma_start(crow[i][j * GC:(j + 1) * GC, g * ST:(g + 1) * ST], vj[g, j]).then_inc(s["c_in"], 16)
            for i, v in enumerate((m.ins["s5_b_re"], m.ins["s5_b_im"])):
                vj = v[0].rearrange("(j g) p h -> g p j h", g=2)
                for g in range(2):
                    sp.dma_start(b[i][g * ST:(g + 1) * ST], vj[g]).then_inc(s["p_in"], 16)
            sp.dma_start(d_row.rearrange("p g h -> p (g h)"), m.ins["s5_d"][0].rearrange("g h -> (g h)").partition_broadcast(P)).then_inc(s["p_in"], 16)
            sp.dma_start(u.rearrange("p g s h -> p (g s h)"), m.scr_u).then_inc(s["u_in"], 16)
            sp.wait_ge(s["k_cp"], 4)
            sp.wait_ge(s["zero"], 1)
            for kap in range(CH):
                lag = (CH - 1 - kap) * GC
                r = slice(kap * GC, (kap + 1) * GC)
                sp.dma_start(toep[r, :, lag:], kk[r, :, 0:CH * GC - lag]).then_inc(s["toep_in"], 16)
            sp.wait_ge(s["s_rdy"], 1)
            sp.dma_start(w_glu, m.ins["s5_w_glu"][0].rearrange("(k p) n -> p k n", p=P)).then_inc(s["glu_in"], 16)

        @block.gpsimd
        def _(pool):
            nc.gpsimd.iota(ki.bitcast(I32), pattern=[[1, 9]], base=0, channel_multiplier=0).then_inc(s["cst"], 1)
            nc.gpsimd.iota(cidx.bitcast(I32), pattern=[[1, NCH]], base=0, channel_multiplier=0).then_inc(s["cst"], 1)
            nc.gpsimd.memset(m_re.rearrange("p a b c d -> p (a b c d)"), 0.0).then_inc(s["cst"], 1)
            nc.gpsimd.memset(m_im.rearrange("p a b c d -> p (a b c d)"), 0.0).then_inc(s["cst"], 1)

        @block.scalar
        def _(act):
            A = nc.scalar.activation
            act.wait_ge(s["row_c"], 3)
            A(stp, stp, ACT.Exp).then_inc(s["exp1"], 1)
            act.wait_ge(s["ang9"], 2)
            A(e9, a9, ACT.Exp).then_inc(s["sc9"], 1)
            A(l_im, p9, ACT.Sin).then_inc(s["sc9"], 1)
            A(l_re, t9, ACT.Sin).then_inc(s["sc9"], 1)
            for f in range(4):
                act.wait_ge(s["u_ps"], f + 1)
                A(u_t[:, 4 * f:4 * f + 4, :].rearrange("p g c -> p (g c)"), ps[:, f, :], ACT.Copy).then_inc(s["u_cp"], 1)
            for f in range(4):
                act.wait_ge(s["w_ps"], f + 1)
                A(w_t[f // 2][:, 4 * (f % 2):4 * (f % 2) + 4, :].rearrange("p j c -> p (j c)"), ps[:, 4 + f, :], ACT.Copy).then_inc(s["w_cp"], 1)
            act.wait_ge(s["tab_a"], 1)
            A(tab[1], tab[1], ACT.Sin).then_inc(s["tab_s"], 1)
            A(tab[0], tab[0], ACT.Sin).then_inc(s["tab_s"], 1)
            for f in range(4):
                act.wait_ge(s["y_ps"], f + 1)
                dst = y[:, :, 4 * f:4 * f + 4, :].rearrange("p s g h -> p g s h")
                A(dst, ps[:, 4 + f, :].rearrange("p (g s h) -> p g s h", g=4, s=CH), ACT.Gelu_apprx_tanh).then_inc(s["y_cp"], 1)
            for f in range(4):
                act.wait_ge(s["g_ps"], f + 1)
                mt, half = divmod(f, 2)
                if f >= 2:
                    act.wait_ge(s["g_y"], f - 1)
                A(sg[f % 2], ps[:, 4 + f, :], ACT.Sigmoid, bias=m.b_glu[:, mt:mt + 1]).then_inc(s["g_sg"], 1)
                act.wait_ge(s["g_y"], f + 1)
                A(m.br_hi[:, 4 + mt, half * BANK:(half + 1) * BANK], y_out(f), ACT.Copy).then_inc(s["g_hi"], 1)

        @block.tensor
        def _(pe):
            I = m.ident
            pe.wait_ge(s["step_b"], 1)
            pe.wait_ge(s["r_in"], 48)
            for i in range(3):
                tr = nc.tensor.transpose(ps[:, 7, i * J:(i + 1) * J], rows[0:J, i * P:(i + 1) * P], I[0:J, 0:J])
            tr.then_inc(s["row_t"], 1)
            pe.wait_ge(s["c_in"], 16 * 4 * J)
            nc.tensor.transpose(ps[:, 6, 0:P], crow[0], I[:])
            nc.tensor.transpose(ps[:, 6, P:2 * P], crow[1], I[:]).then_inc(s["row_t"], 1)
            pe.wait_ge(s["u_in"], 16)
            for g in range(GR):
                tr = nc.tensor.transpose(ps[:, g // 4, (g % 4) * P:(g % 4 + 1) * P], u[:, g].rearrange("p s h -> p (s h)"), I[:])
                if g % 4 == 3:
                    tr.then_inc(s["u_ps"], 1)
            pe.wait_ge(s["w_rdy"], 1)
            for n in range(2 * J):
                i, j = divmod(n, J)
                tr = nc.tensor.transpose(ps[:, 4 + n // 4, (n % 4) * P:(n % 4 + 1) * P], w[i][:, j].rearrange("p s h -> p (s h)"), I[:])
                if n % 4 == 3:
                    tr.then_inc(s["w_ps"], 1)
            pe.wait_ge(s["u_cp"], 4)
            pe.wait_ge(s["b_rdy"], 1)
            pe.wait_ge(s["w_cp"], 4)
            for g in range(GR):
                j, g2 = divmod(g, 2)
                o = ps[:, g // 4, (g % 4) * P:(g % 4 + 1) * P]
                nc.tensor.matmul(o, b_rep[0][:, j].rearrange("p s h -> p (s h)"), m_re[:, j, g2, 0:8, :].rearrange("p k h -> p (k h)"), start=True, stop=False)
                mm = nc.tensor.matmul(o, b_rep[1][:, j].rearrange("p s h -> p (s h)"), m_im[:, j, g2, 0:8, :].rearrange("p k h -> p (k h)"), start=False, stop=True)
                if g % 4 == 3:
                    mm.then_inc(s["k_ps"], 1)
            for i in range(2):
                for j in range(J):
                    for g2 in range(2):
                        mm = nc.tensor.matmul(ps[g2 * ST:(g2 + 1) * ST, 4 + 2 * i + j // 4, (j % 4) * P:(j % 4 + 1) * P],
                                              w_t[i][:, j, g2 * ST:(g2 + 1) * ST], u_t[:, 2 * j + g2, :], start=True, stop=True)
                mm.then_inc(s["x_ps"], 1)
            pe.wait_ge(s["toep_in"], 16 * CH)
            pe.wait_ge(s["s_rdy"], 1)
            for g in range(GR):
                j, g2 = divmod(g, 2)
                o = ps[:, 4 + g // 4, (g % 4) * P:(g % 4 + 1) * P]
                nc.tensor.matmul(o, u_t[:, g, :], toep[:, g, :], start=True, stop=False)
                nc.tensor.matmul(o, s_prev[0][:, j, :], m_re[:, j, g2, 1:9, :].rearrange("p k h -> p (k h)"), start=False, stop=False)
                mm = nc.tensor.matmul(o, s_prev[1][:, j, :], m_im[:, j, g2, 1:9, :].rearrange("p k h -> p (k h)"), start=False, stop=True)
                if g % 4 == 3:
                    mm.then_inc(s["y_ps"], 1)
            pe.wait_ge(s["y_cp"], 4)
            for f in range(4):
                mt, half = divmod(f, 2)
                for q in range(4):
                    st = 4 * half + q
                    tr = nc.tensor.transpose(ps[:, f, q * P:(q + 1) * P], y[:, st, 8 * mt:8 * mt + 8, :].rearrange("p g h -> p (g h)"), I[:])
                tr.then_inc(s["yt_ps"], 1)
            pe.wait_ge(s["yt_cp"], 4)
            pe.wait_ge(s["glu_in"], 16)
            for f in range(4):
                mt, half = divmod(f, 2)
                for k in range(2):
                    rhs = y_t[:, k].rearrange("p c s -> p (c s)")[:, half * BANK:(half + 1) * BANK]
                    mm = nc.tensor.matmul(ps[:, 4 + f, :], w_glu[:, k, mt * P:(mt + 1) * P], rhs, start=(k == 0), stop=(k == 1))
                mm.then_inc(s["g_ps"], 1)

        @block.vector
        def _(dve):
            step = m.dve_step.on(dve)
            V = nc.vector
            TTo, TS, STT = V.tensor_tensor, V.tensor_scalar, V.scalar_tensor_tensor
            dve.wait_ge(s["r_in"], 48)
            V.tensor_copy(rows[0:J, 2 * P:3 * P].rearrange("j (g p) -> j g p", g=2),
                          stp[0:J, 0:2].unsqueeze(2).to_broadcast([J, 2, ST])).then_inc(s["step_b"], 1)
            dve.wait_ge(s["row_t"], 1)
            for i, dst in enumerate((lre, lim, stp)):
                V.tensor_copy(dst, ps[:, 7, i * J:(i + 1) * J]).then_inc(s["row_c"], 1)
            dve.wait_ge(s["row_c"], 3)
            dve.wait_ge(s["row_t"], 2)
            for i in range(2):
                step(V.tensor_copy(cc[i].rearrange("p j h -> p (j h)"), ps[:, 6, i * P:(i + 1) * P]))
            dve.wait_ge(s["cst"], 4)
            step(V.tensor_copy(ki, ki.bitcast(I32)))
            step(V.tensor_copy(cidx_keep, cidx.bitcast(I32)))
            dve.wait_ge(s["exp1"], 1)
            step(TTo(a1, lre, stp, ALU.mult))
            step(TTo(th, lim, stp, ALU.mult))
            step(reduced(nc, step, th, tt, ta))
            kb = ki.unsqueeze(1).to_broadcast([P, J, 9])
            step(TTo(a9, kb, a1.unsqueeze(2).to_broadcast([P, J, 9]), ALU.mult))
            step(TTo(p9, kb, th.unsqueeze(2).to_broadcast([P, J, 9]), ALU.mult))
            reduced(nc, step, p9, e9, t9).then_inc(s["ang9"], 1)
            dve.wait_ge(s["ang9"], 1)
            V.tensor_copy(t8, p9[:, :, 8]).then_inc(s["ang9"], 1)
            dve.wait_ge(s["sc9"], 3)
            step(TTo(l_re, l_re, e9, ALU.mult))
            step(TTo(l_im, l_im, e9, ALU.mult))
            step(TTo(den, lre, lre, ALU.mult))
            step(TTo(tt, lim, lim, ALU.mult))
            step(TTo(den, den, tt, ALU.add))
            step(V.reciprocal(den, den))
            step(TS(ta, l_re[:, :, 1], -1.0, None, ALU.add))
            step(TTo(q_re, ta, lre, ALU.mult))
            step(TTo(tt, l_im[:, :, 1], lim, ALU.mult))
            step(TTo(q_re, q_re, tt, ALU.add))
            step(TTo(q_re, q_re, den, ALU.mult))
            step(TTo(q_im, l_im[:, :, 1], lre, ALU.mult))
            step(TTo(tt, ta, lim, ALU.mult))
            step(TTo(q_im, q_im, tt, ALU.subtract))
            step(TTo(q_im, q_im, den, ALU.mult))
            dve.wait_ge(s["p_in"], 80)

            def cmul(o_re, o_im, xr, xi, yr, yi, t0, t1, neg_im=False):
                step(TTo(t0, xr, yr, ALU.mult))
                step(TTo(t1, xi, yi, ALU.mult))
                step(TTo(o_re, t0, t1, ALU.subtract))
                step(TTo(t0, xr, yi, ALU.mult))
                step(TTo(t1, xi, yr, ALU.mult))
                if neg_im:
                    step(STT(out=o_im, in0=t0, scalar=-1.0, in1=t1, op0=ALU.mult, op1=ALU.subtract))
                else:
                    step(TTo(o_im, t0, t1, ALU.add))

            def over(a, n):
                return a.unsqueeze(2).to_broadcast([P, J, n])
            cmul(bb[0], bb[1], over(q_re, GC), over(q_im, GC), b[0], b[1], pq[0], pq[1])
            nine = [J, 9, GC]
            t0, t1 = cols(m.F, 10752, J, 9, GC), cols(m.F, 11904, J, 9, GC)
            lr, li = (a.unsqueeze(3).to_broadcast([P] + nine) for a in (l_re, l_im))
            cr, ci = (a.unsqueeze(2).to_broadcast([P] + nine) for a in cc)
            step(TTo(t0, lr, cr, ALU.mult))
            step(TTo(t1, li, ci, ALU.mult))
            for g2 in range(2):
                r = slice(g2 * ST, (g2 + 1) * ST)
                step(TTo(m_re[r, :, g2], t0[r], t1[r], ALU.subtract))
            step(TTo(t0, lr, ci, ALU.mult))
            step(TTo(t1, li, cr, ALU.mult))
            step(TTo(t0, t0, t1, ALU.add))
            for g2 in range(2):
                r = slice(g2 * ST, (g2 + 1) * ST)
                ins = TS(m_im[r, :, g2], t0[r], -1.0, None, ALU.mult)
                step(ins) if g2 == 0 else ins.then_inc(s["b_rdy"], 1)
            four = [P, J, CH, GC]
            lr, li = (a[:, :, 0:CH].unsqueeze(3).to_broadcast(four) for a in (l_re, l_im))
            br, bi = (a.unsqueeze(2).to_broadcast(four) for a in bb)
            cmul(w[0], w[1], lr, li, br, bi, b_rep[0], b_rep[1])
            step(V.tensor_copy(b_rep[0], br))
            V.tensor_copy(b_rep[1], bi).then_inc(s["w_rdy"], 1)
            step(V.tensor_reduce(mask16, m.ident[:].rearrange("p (a h) -> p h a", h=GC), AX.X, ALU.add))
            dmat = m.vecs[:, 0:GR * GC].rearrange("p (g h) -> p g h", h=GC)
            dve.wait_ge(s["b_rdy"], 1)
            step(TTo(dmat, d_row, mask16.unsqueeze(1).to_broadcast([P, GR, GC]), ALU.mult))
            dve.wait_ge(s["w_ps"], 4)
            V.memset(toep, 0.0).then_inc(s["zero"], 1)
            for f in range(4):
                dve.wait_ge(s["k_ps"], f + 1)
                o = kk[:, 4 * f:4 * f + 4, :]
                src = ps[:, f, :].rearrange("p (g n) -> p g n", g=4)
                step(V.tensor_copy(o[:, :, GC:], src[:, :, GC:]))
                TTo(o[:, :, 0:GC], src[:, :, 0:GC], dmat[:, 4 * f:4 * f + 4, :], ALU.add).then_inc(s["k_cp"], 1)
            step(TTo(tab[1], t8.unsqueeze(2).to_broadcast([P, J, NCH]), cidx_keep.unsqueeze(1).to_broadcast([P, J, NCH]), ALU.mult))
            reduced(nc, step, tab[1], rho, tab[0]).then_inc(s["tab_a"], 1)
            dve.wait_ge(s["tab_a"], 1)
            step(V.tensor_copy(rho, e9[:, :, 8:9].to_broadcast([P, J, NCH])))
            step(V.memset(rho[:, :, 0:1], 0.0))
            dve.wait_ge(s["tab_s"], 2)
            dve.wait_ge(s["x_ps"], 2)
            dve.wait_ge(s["toep_in"], 16 * CH)
            x = [ps[:, 4 + 2 * i:6 + 2 * i, :].rearrange("p b (j c) -> p (b j) c", c=NCH) for i in range(2)]
            step(TTo(z_in[0], x[0], tab[0], ALU.mult))
            step(TTo(tmp, x[1], tab[1], ALU.mult))
            step(TTo(z_in[0], z_in[0], tmp, ALU.add))
            step(TTo(z_in[1], x[1], tab[0], ALU.mult))
            step(TTo(tmp, x[0], tab[1], ALU.mult))
            step(TTo(z_in[1], z_in[1], tmp, ALU.subtract))
            for i in range(2):
                flat = (a.rearrange("p j c -> p (j c)") for a in (z[i], rho, z_in[i]))
                o, d0, d1 = flat
                step(V.tensor_tensor_scan(o, d0, d1, 0.0, ALU.mult, ALU.add))
            n1 = NCH - 1
            zc = [a[:, :, 0:n1] for a in z]
            cs, sn = tab[0][:, :, 0:n1], tab[1][:, :, 0:n1]
            o_re, o_im = (a[:, :, 1:] for a in s_prev)
            step(V.memset(s_prev[0][:, :, 0:1], 0.0))
            step(V.memset(s_prev[1][:, :, 0:1], 0.0))
            step(TTo(o_re, zc[0], cs, ALU.mult))
            step(TTo(tmp[:, :, 0:n1], zc[1], sn, ALU.mult))
            step(TTo(o_re, o_re, tmp[:, :, 0:n1], ALU.subtract))
            step(TTo(o_im, zc[0], sn, ALU.mult))
            step(TTo(tmp[:, :, 0:n1], zc[1], cs, ALU.mult))
            TTo(o_im, o_im, tmp[:, :, 0:n1], ALU.add).then_inc(s["s_rdy"], 1)
            for f in range(4):
                mt, half = divmod(f, 2)
                dve.wait_ge(s["yt_ps"], f + 1)
                V.tensor_copy(y_t[:, mt, :, 4 * half:4 * half + 4].rearrange("p c s -> p s c"),
                              ps[:, f, :].rearrange("p (s c) -> p s c", s=4)).then_inc(s["yt_cp"], 1)
            dve.wait_ge(s["yt_cp"], 4)
            for f in range(4):
                mt, half = divmod(f, 2)
                cut = slice(half * BANK, (half + 1) * BANK)
                dve.wait_ge(s["g_sg"], f + 1)
                TTo(y_out(f), y_t[:, mt].rearrange("p c s -> p (c s)")[:, cut], sg[f % 2], ALU.mult).then_inc(s["g_y"], 1)
                dve.wait_ge(s["g_hi"], f + 1)
                TTo(m.br_lo[:, 4 + mt, cut], y_out(f), f32(m.br_hi[:, 4 + mt, cut]), ALU.subtract).then_inc(s["g_lo"], 1)


def after(eng, sem, value):
    if isinstance(value, int) and value <= 0:
        return
    eng.wait_ge(sem, value)


def looped(eng, first, last, body):
    body(0)
    with eng.Fori(first, last) as i:
        body(i)


def stage_gates(m):
    nc, ps = m.nc, m.ps
    NB = 3
    UNITS = 2 * NB
    ITERS = KD // 2
    WC = (KD + 2) * P
    W0 = 2 * KD * T + 12 * T
    w_hi = [cols(m.R, W0 + 2 * i * WC, KD + 2, P) for i in range(2)]
    w_lo = [cols(m.R, W0 + (2 * i + 1) * WC, KD + 2, P) for i in range(2)]
    merged = cols(m.F, 0, KD * T)
    raw = [cols(m.F, KD * T + i * WC, KD + 2, P) for i in range(2)]
    sg = [cols(m.F, KD * T + 2 * WC + i * T, T) for i in range(2)]
    part = [cols(m.F, KD * T + 2 * WC + (2 + i) * T, T) for i in range(NB)]
    w_in = [m.sem(f"gate_w_in{i}") for i in range(2)]
    b_in = [m.sem(f"branch_w_in{i}") for i in range(2)]
    hi_done, lo_done, gate_mm, proj_mm, sig_done, mul_done, add_done, sum_done = (
        m.sem(f"gates_{n}") for n in ("hi", "lo", "gate", "proj", "sigmoid", "mul", "add", "sum"))
    gate_src = m.ins["w_in"][0].rearrange("(k p) n -> p k n", p=P)
    branch_src = m.ins["w_branch"][0].rearrange("b (k p) n -> b p k n", p=P)
    gate_ps = [ps[:, 4 * i:4 * i + 2, :].rearrange("p b n -> p (b n)") for i in range(2)]
    proj_ps = [ps[:, 4 * i + 2:4 * i + 4, :].rearrange("p b n -> p (b n)") for i in range(2)]

    def tile_of(it, u):
        return it * 2 + u // NB, u % NB

    with nc.Block() as block:
        @block.sync
        def _(sp):
            def body(it):
                for u in range(UNITS):
                    d, n = tile_of(it, u)
                    after(sp, lo_done, it * UNITS + u - 1)
                    sp.dma_start(raw[u % 2][:, 0:KD, :], gate_src[:, :, bass.ds(d * P + (C_G + n * D), P)]).then_inc(w_in[u % 2], 16)
                    sp.dma_start(raw[u % 2][:, KD:, :], branch_src[n][:, :, bass.ds(d * P, P)]).then_inc(b_in[u % 2], 16)
            looped(sp, 1, ITERS, body)

        @block.scalar
        def _(act):
            def split(it, u):
                if u >= UNITS:
                    it, u = it + 1, u - UNITS
                after(act, w_in[u % 2], (it * (UNITS // 2) + u // 2 + 1) * 16)
                after(act, b_in[u % 2], (it * (UNITS // 2) + u // 2 + 1) * 16)
                after(act, proj_mm, it * UNITS + u - 1)
                nc.scalar.activation(w_hi[u % 2], raw[u % 2], ACT.Copy).then_inc(hi_done, 1)

            def body(it, last=False):
                for u in range(UNITS):
                    if not (last and u == UNITS - 1):
                        split(it, u + 1)
                    after(act, gate_mm, it * UNITS + u + 1)
                    after(act, mul_done, it * UNITS + u - 1)
                    nc.scalar.activation(sg[u % 2], gate_ps[u % 2], ACT.Sigmoid).then_inc(sig_done, 1)
            split(0, 0)
            body(0)
            with act.Fori(1, ITERS - 1) as it:
                body(it)
            body(ITERS - 1, last=True)

        @block.vector
        def _(dve):
            def split(it, u):
                if u >= UNITS:
                    it, u = it + 1, u - UNITS
                after(dve, hi_done, it * UNITS + u + 1)
                nc.vector.tensor_tensor(w_lo[u % 2], raw[u % 2], f32(w_hi[u % 2]), ALU.subtract).then_inc(lo_done, 1)

            def body(it, last=False):
                for u in range(UNITS):
                    if not (last and u == UNITS - 1):
                        split(it, u + 1)
                    d, n = tile_of(it, u)
                    after(dve, proj_mm, it * UNITS + u + 1)
                    after(dve, sig_done, it * UNITS + u + 1)
                    if n == 0:
                        after(dve, sum_done, it * 2 + u // NB)
                    nc.vector.tensor_tensor(part[n], proj_ps[u % 2], sg[u % 2], ALU.mult).then_inc(mul_done, 1)
                    if n == NB - 1:
                        after(dve, mul_done, it * UNITS + u + 1)
                        after(dve, add_done, it * 2 + u // NB + 1)
                        nc.vector.tensor_tensor(merged[:, bass.ds(d * T, T)], part[0], part[2], ALU.add).then_inc(sum_done, 1)
            split(0, 0)
            body(0)
            with dve.Fori(1, ITERS - 1) as it:
                body(it)
            body(ITERS - 1, last=True)

        @block.gpsimd
        def _(pool):
            def body(it):
                for u in (1, NB + 1):
                    after(pool, mul_done, it * UNITS + u + 1)
                    nc.gpsimd.tensor_tensor(part[0], part[0], part[1], ALU.add).then_inc(add_done, 1)
            looped(pool, 1, ITERS, body)

        @block.tensor
        def _(pe):
            def body(it):
                for u in range(UNITS):
                    n = u % NB
                    hi, lo = w_hi[u % 2], w_lo[u % 2]
                    after(pe, lo_done, it * UNITS + u + 1)
                    after(pe, sig_done, it * UNITS + u - 1)
                    after(pe, mul_done, it * UNITS + u - 1)

                    def product(out, k, wk, src_hi, src_lo, sk, first, last):
                        for half in range(2):
                            cut = slice(half * BANK, (half + 1) * BANK)
                            o = out[:, cut]
                            nc.tensor.matmul(o, hi[:, wk, :], src_hi[:, sk, cut], start=first, stop=False, skip_group_check=True)
                            nc.tensor.matmul(o, hi[:, wk, :], src_lo[:, sk, cut], start=False, stop=False, skip_group_check=True)
                        for half in range(2):
                            cut = slice(half * BANK, (half + 1) * BANK)
                            mm = nc.tensor.matmul(out[:, cut], lo[:, wk, :], src_hi[:, sk, cut], start=False, stop=last, skip_group_check=True)
                        return mm
                    for k in range(KD):
                        mm = product(gate_ps[u % 2], k, k, m.h_hi, m.h_lo, k, k == 0, k == KD - 1)
                    mm.then_inc(gate_mm, 1)
                    for k in range(2):
                        mm = product(proj_ps[u % 2], k, KD + k, m.br_hi, m.br_lo, 2 * n + k, k == 0, k == 1)
                    mm.then_inc(proj_mm, 1)
            looped(pe, 1, ITERS, body)


def stage_out(m):
    nc, ps = m.nc, m.ps
    W0 = 2 * KD * T
    merged = cols(m.F, 0, KD, T)
    rows = cols(m.F, 0, TT, D)
    raw = [cols(m.F, KD * T + i * D, D) for i in range(4)]
    w_hi, w_lo = cols(m.R, W0, KD, D), cols(m.R, W0 + KD * D, KD, D)
    w_in = [m.sem(f"out_w_in{i}") for i in range(4)]
    mg_hi, mg_lo, hi_done, lo_done, mm_done, add_done, x_in = (m.sem(f"out_{n}") for n in ("mg_hi", "mg_lo", "hi", "lo", "mm", "add", "x_in"))
    with nc.Block() as block:
        @block.sync
        def _(sp):
            for k in range(KD):
                after(sp, lo_done, k - 3)
                sp.dma_start(raw[k % 4], m.ins["w_out"][0, k * P:(k + 1) * P, :]).then_inc(w_in[k % 4], 16)
            sp.wait_ge(mg_lo, KD)
            sp.dma_start(rows, m.ins["x"][0].rearrange("(i p) d -> p i d", p=P)).then_inc(x_in, 16)

        @block.scalar
        def _(act):
            for k in range(KD):
                nc.scalar.activation(m.h_hi[:, k, :], merged[:, k, :], ACT.Copy).then_inc(mg_hi, 1)
                act.wait_ge(w_in[k % 4], 16 * (k // 4 + 1))
                nc.scalar.activation(w_hi[:, k, :], raw[k % 4], ACT.Copy).then_inc(hi_done, 1)

        @block.vector
        def _(dve):
            for k in range(KD):
                dve.wait_ge(mg_hi, k + 1)
                nc.vector.tensor_tensor(m.h_lo[:, k, :], merged[:, k, :], f32(m.h_hi[:, k, :]), ALU.subtract).then_inc(mg_lo, 1)
                dve.wait_ge(hi_done, k + 1)
                nc.vector.tensor_tensor(w_lo[:, k, :], raw[k % 4], f32(w_hi[:, k, :]), ALU.subtract).then_inc(lo_done, 1)
            dve.wait_ge(x_in, 16)
            for n in range(2 * TT):
                t, half = divmod(n, 2)
                dve.wait_ge(mm_done, n + 1)
                r = rows[:, t, half * BANK:(half + 1) * BANK]
                nc.vector.tensor_tensor(r, ps[:, n % 8, :], r, ALU.add).then_inc(add_done, 1)

        @block.tensor
        def _(pe):
            for base in (0, 4):
                for k in range(KD):
                    if base == 0:
                        pe.wait_ge(mg_lo, k + 1)
                        pe.wait_ge(lo_done, k + 1)
                    for n in range(2 * base, 2 * base + 8):
                        t, half = divmod(n, 2)
                        if k == 0 and n >= 8:
                            pe.wait_ge(add_done, n - 7)
                        o, cut = ps[:, n % 8, :], slice(half * BANK, (half + 1) * BANK)
                        hi, lo = (a[:, k, t * P:(t + 1) * P] for a in (m.h_hi, m.h_lo))
                        nc.tensor.matmul(o, hi, w_hi[:, k, cut], start=(k == 0), stop=False)
                        nc.tensor.matmul(o, hi, w_lo[:, k, cut], start=False, stop=False)
                        mm = nc.tensor.matmul(o, lo, w_hi[:, k, cut], start=False, stop=(k == KD - 1))
                        if k == KD - 1:
                            mm.then_inc(mm_done, 1)


def stage_ffn_norm(m):
    m.rows_scaled = cols(m.F, TT * D, TT, D)
    nrm = norm_and_turn(m, "ffnn", None, m.g_ffn)
    with m.nc.Block() as block:
        @block.scalar
        def _(act):
            nrm.scalar(act)

        @block.vector
        def _(dve):
            nrm.vector(dve)

        @block.gpsimd
        def _(pool):
            nrm.gpsimd(pool)

        @block.tensor
        def _(pe):
            nrm.tensor(pe)


def stage_ffn(m):
    nc, ps = m.nc, m.ps
    FT = FF // P
    GROUPS = FT // 2
    rows = cols(m.F, 0, TT, D)
    raw = [cols(m.F, 8192 + i * T, KD, P) for i in range(4)]
    wd_raw = [cols(m.F, 12288 + i * D, D) for i in range(2)]
    conv = [cols(m.F, 14336 + i * T, T) for i in range(2)]
    gated = cols(m.F, 16384, T)
    W0 = 2 * KD * T
    w_hi = [cols(m.R, W0 + 2 * i * T, KD, P) for i in range(4)]
    w_lo = [cols(m.R, W0 + (2 * i + 1) * T, KD, P) for i in range(4)]
    a_hi, a_lo = cols(m.R, W0 + 8 * T, 2, T), cols(m.R, W0 + 10 * T, 2, T)
    d_hi, d_lo = cols(m.R, W0 + 12 * T, 2, D), cols(m.R, W0 + 14 * T, 2, D)
    w_in = [m.sem(f"up_in{i}") for i in range(4)]
    wd_in = [m.sem(f"down_in{i}") for i in range(2)]
    (hi_done, lo_done, up_mm, scaled, conv_mid, conv_done, silu_done, gated_done, a_hi_done, a_lo_done, d_hi_done, d_lo_done,
     down_mm, add_done, stored) = (m.sem(f"ffn_{n}") for n in (
         "w_hi", "w_lo", "up", "scaled", "conv_mid", "conv", "silu", "gated", "a_hi", "a_lo", "d_hi", "d_lo", "down", "add", "stored"))
    up_src = m.ins["w_up"][0].rearrange("(k p) n -> p k n", p=P)
    ups = [ps[:, 2 * i:2 * i + 2, :].rearrange("p b n -> p (b n)") for i in range(2)]
    ND = 2 * TT

    def feature(it, n):
        return it * (2 * P) + ((n // 2) * P + (n % 2) * FF)

    with nc.Block() as block:
        @block.sync
        def _(sp):
            def body(it):
                for n in range(4):
                    after(sp, lo_done, it * 4 + n - 3)
                    sp.dma_start(raw[n], up_src[:, :, bass.ds(feature(it, n), P)]).then_inc(w_in[n], 16)
                    if n % 2 == 1:
                        f = n // 2
                        after(sp, d_lo_done, it * 2 + f - 1)
                        sp.dma_start(wd_raw[f], m.ins["w_down"][0][bass.ds(it * (2 * P) + f * P, P), :]).then_inc(wd_in[f], 16)
            looped(sp, 1, GROUPS, body)
            for t in range(TT):
                sp.wait_ge(add_done, GROUPS * ND + 2 * t + 2)
                sp.dma_start(m.ins["out"][0, t * P:(t + 1) * P, :], rows[:, t, :]).then_inc(stored, 16)
            sp.wait_ge(stored, 16 * TT)

        def ahead(it, n, by=2):
            return (it, n + by) if n + by < 4 else (it + 1, n + by - 4)

        @block.scalar
        def _(act):
            def split(it, n):
                after(act, w_in[n], it * 16 + 16)
                after(act, up_mm, it * 4 + n - 3)
                nc.scalar.activation(w_hi[n], raw[n], ACT.Copy).then_inc(hi_done, 1)

            def body(it, last=False):
                for n in range(4):
                    f = n // 2
                    if not (last and n >= 2):
                        split(*ahead(it, n))
                    after(act, up_mm, it * 4 + n + 1)
                    after(act, gated_done, it * 2 + f)
                    nc.scalar.activation(conv[n % 2], ups[n % 2], ACT.Copy,
                                         scale=m.colv[:, bass.ds(2 * 44 + it * 2 + f + (n % 2) * FT, 1)]).then_inc(scaled, 1)
                    if n % 2 == 1:
                        after(act, conv_done, it * 4 + n)
                        nc.scalar.activation(conv[0], conv[0], ACT.Silu).then_inc(silu_done, 1)
                        after(act, wd_in[f], it * 16 + 16)
                        after(act, down_mm, it * ND)
                        nc.scalar.activation(d_hi[:, f, :], wd_raw[f], ACT.Copy).then_inc(d_hi_done, 1)
                        after(act, gated_done, it * 2 + f + 1)
                        nc.scalar.activation(a_hi[:, f, :], gated, ACT.Copy).then_inc(a_hi_done, 1)
            split(0, 0)
            split(0, 1)
            body(0)
            with act.Fori(1, GROUPS - 1) as it:
                body(it)
            body(GROUPS - 1, last=True)

        @block.vector
        def _(dve):
            V = nc.vector

            def split(it, n):
                after(dve, hi_done, it * 4 + n + 1)
                V.tensor_tensor(w_lo[n], raw[n], f32(w_hi[n]), ALU.subtract).then_inc(lo_done, 1)

            def adds(it):
                for n in range(ND):
                    t, half = divmod(n, 2)
                    after(dve, down_mm, it * ND + n + 1)
                    r = rows[:, t, half * BANK:(half + 1) * BANK]
                    after(dve, add_done, it * ND + n + 1)
                    V.tensor_tensor(r, ps[:, 4 + n % 4, :], r, ALU.add).then_inc(add_done, 1)

            def body(it, last=False, first=False):
                for n in range(4):
                    f = n // 2
                    if not (last and n >= 2):
                        split(*ahead(it, n))
                    after(dve, scaled, it * 4 + n + 1)
                    up, c = ups[n % 2], conv[n % 2]
                    V.scalar_tensor_tensor(out=c[:, 1:], in0=up[:, 0:T - 1], scalar=m.colv[:, bass.ds(44 + it * 2 + f + (n % 2) * FT, 1)],
                                           in1=c[:, 1:], op0=ALU.mult, op1=ALU.add).then_inc(conv_mid, 1)
                    after(dve, conv_mid, it * 4 + n + 1)
                    V.scalar_tensor_tensor(out=c[:, 2:], in0=up[:, 0:T - 2], scalar=m.colv[:, bass.ds(it * 2 + f + (n % 2) * FT, 1)],
                                           in1=c[:, 2:], op0=ALU.mult, op1=ALU.add).then_inc(conv_done, 1)
                    if n == 0 and not first:
                        adds(it - 1)
                    if n % 2 == 1:
                        after(dve, silu_done, it * 2 + f + 1)
                        after(dve, conv_done, it * 4 + n + 1)
                        after(dve, a_lo_done, it * 2 + f)
                        V.tensor_tensor(gated, conv[0], conv[1], ALU.mult).then_inc(gated_done, 1)
                        after(dve, d_hi_done, it * 2 + f + 1)
                        V.tensor_tensor(d_lo[:, f, :], wd_raw[f], f32(d_hi[:, f, :]), ALU.subtract).then_inc(d_lo_done, 1)
                        after(dve, a_hi_done, it * 2 + f + 1)
                        V.tensor_tensor(a_lo[:, f, :], gated, f32(a_hi[:, f, :]), ALU.subtract).then_inc(a_lo_done, 1)
            dve.sem_inc(add_done, ND)
            split(0, 0)
            split(0, 1)
            body(0, first=True)
            with dve.Fori(1, GROUPS - 1) as it:
                body(it)
            body(GROUPS - 1, last=True)
            adds(GROUPS - 1)

        @block.tensor
        def _(pe):
            def up(it, n):
                after(pe, lo_done, it * 4 + n + 1)
                after(pe, conv_done, it * 4 + n - 1)
                for k in range(KD):
                    for w, src in ((w_hi[n], m.h_hi), (w_hi[n], m.h_lo), (w_lo[n], m.h_hi)):
                        for half in range(2):
                            cut = slice(half * BANK, (half + 1) * BANK)
                            mm = nc.tensor.matmul(ups[n % 2][:, cut], w[:, k, :], src[:, k, cut], start=(k == 0 and w is w_hi[n] and src is m.h_hi),
                                                  stop=(k == KD - 1 and w is w_lo[n]), skip_group_check=True)
                mm.then_inc(up_mm, 1)

            def down(it):
                after(pe, a_lo_done, it * 2 + 2)
                after(pe, d_lo_done, it * 2 + 2)
                for n in range(ND):
                    t, half = divmod(n, 2)
                    after(pe, add_done, it * ND + ND + n - 3)
                    cut = slice(half * BANK, (half + 1) * BANK)
                    for f in range(2):
                        hi, lo = (a[:, f, t * P:(t + 1) * P] for a in (a_hi, a_lo))
                        o = ps[:, 4 + n % 4, :]
                        nc.tensor.matmul(o, hi, d_hi[:, f, cut], start=(f == 0), stop=False)
                        nc.tensor.matmul(o, hi, d_lo[:, f, cut], start=False, stop=False)
                        mm = nc.tensor.matmul(o, lo, d_hi[:, f, cut], start=False, stop=(f == 1))
                    mm.then_inc(down_mm, 1)

            def body(it, first=False):
                up(it, 0)
                if not first:
                    down(it - 1)
                for n in range(1, 4):
                    up(it, n)
            body(0, first=True)
            with pe.Fori(1, GROUPS) as it:
                body(it)
            down(GROUPS - 1)


def hybrid_trunk(nc, ins):
    with ExitStack() as ctx:
        m = setup(nc, ctx, ins)
        stage_load_norm_project(m)
        stage_fox(m)
        stage_mla(m)
        stage_s5(m)
        reuse_semaphores(m)
        stage_gates(m)
        stage_out(m)
        stage_ffn_norm(m)
        stage_ffn(m)


_INS = ["x", "positions", "attn_norm_g", "w_in", "q_lat_norm_g", "w_uq", "kv_lat_norm_g", "w_ukv", "mla_q_norm_g", "mla_k_norm_g",
        "fox_q_norm_g", "fox_k_norm_g", "fox_f_bias", "s5_lambda_re", "s5_lambda_im", "s5_b_re", "s5_b_im", "s5_c_re", "s5_c_im",
        "s5_d", "s5_log_step", "s5_w_glu", "s5_b_glu", "w_branch", "w_out", "ffn_norm_g", "w_up", "ffn_conv_w", "w_down"]


def kernel(**inputs):
    import concourse.bacc as _bacc
    from concourse.bass_utils import run_bass_kernel_spmd as _run

    nc = _bacc.Bacc("TRN2", target_bir_lowering=False, num_devices=1)
    arrays, args = {}, {}
    for name in _INS:
        a = np.ascontiguousarray(inputs[name])
        arrays[f"in_{name}"] = a
        args[name] = nc.dram_tensor(f"in_{name}", a.shape, mybir.dt.from_np(a.dtype), kind="ExternalInput").ap()
    args["out"] = nc.dram_tensor("out_x", (1, T, D), F32, kind="ExternalOutput").ap()
    hybrid_trunk(nc, args)
    r = _run(nc, [arrays], core_ids=[0])
    return r.results[0]["out_x"]
```

```python
from contextlib import ExitStack
import math
import numpy as np

import concourse.bass as bass
from concourse import mybir

F32 = mybir.dt.float32
F32R = mybir.dt.float32r
BF16 = mybir.dt.bfloat16
I32 = mybir.dt.int32
ALU = mybir.AluOpType
ACT = mybir.ActivationFunctionType
AX = mybir.AxisListType

P = 128
T, D, KD = 1024, 1024, 8
TT = T // P
BANK = 512
Q_RANK, KV_RANK = 384, 256
H, NOPE, ROPE = 4, 64, 32
QK = NOPE + ROPE
VD = 64
FH, FD = 4, 64
GR, GC, ST = 16, 16, 64
CH = 8
NCH = T // CH
FF, CONV = 2816, 3
EPS = 1e-6
NEG = -1e30
C_Q, C_KV, C_KR = 0, Q_RANK, Q_RANK + KV_RANK
C_FQ = C_KR + ROPE
C_FK, C_FV = C_FQ + 256, C_FQ + 512
C_F = C_FQ + 768
C_U = C_F + FH
C_G = C_U + 256

RW = 132 * 256
FW = 70 * 256


class Chain:

    def __init__(self, sem):
        self.sem, self.n = sem, 0

    def on(self, eng, base=None):
        self.eng, self.base = eng, base
        return self

    def __call__(self, ins):
        ins.then_inc(self.sem, 1)
        self.n += 1
        self.eng.wait_ge(self.sem, self.n if self.base is None else self.base + self.n)
        return ins


class Memory:
    pass


class Programs:

    def __init__(self, scalar, vector, tensor, gpsimd=None, sync=None, done=None):
        self.scalar, self.vector, self.tensor = scalar, vector, tensor
        self.gpsimd, self.sync, self.done = gpsimd, sync, done


def cols(tensor, off, *dims):
    n = math.prod(dims)
    ap = tensor[:, off:off + n]
    if len(dims) == 1:
        return ap
    names = "abcd"[:len(dims)]
    return ap.rearrange(f"p ({' '.join(names)}) -> p {' '.join(names)}",
                        **{k: v for k, v in zip(names[1:], dims[1:])})


def setup(nc, ctx, ins):
    m = Memory()
    m.nc, m.ctx, m.ins = nc, ctx, ins
    m.sb = lambda name, shape, dt=F32: ctx.enter_context(nc.sbuf_tensor(name, shape, dt))
    m.scope, m.held = ctx.enter_context(ExitStack()), []

    def sem(name):
        m.held.append(m.scope.enter_context(nc.semaphore(name)))
        return m.held[-1]
    m.sem = sem
    m.R = m.sb("split_arena", [P, RW], F32R)
    m.F = m.sb("plain_arena", [P, FW], F32)
    m.ident = m.sb("ident", [P, P])
    m.identb = m.sb("identb", [P, P], BF16)
    m.maskb = m.sb("maskb", [P, P], BF16)
    m.vecs = m.sb("vecs", [P, 3 * P])
    m.colv = m.sb("colv", [P, 160])
    m.conv_w = m.colv[:, 0:132].rearrange("p (j f) -> p j f", j=CONV)
    m.g_attn, m.g_ffn = m.colv[:, 132:140], m.colv[:, 140:148]
    m.g_qlat, m.g_kvlat, m.b_glu = m.colv[:, 148:151], m.colv[:, 151:153], m.colv[:, 153:155]
    m.rowg = m.sb("rowg", [P, 2 * QK + 2 * FD + FH])
    m.stat = m.sb("stat", [P, 64])
    m.statb = m.sb("statb", [P, 64])
    m.cidx = m.sb("cidx", [P, P])
    m.ps = ctx.enter_context(nc.psum_tensor("ps", [P, 8, BANK], F32))
    m.h_hi = cols(m.R, 0, KD, T)
    m.h_lo = cols(m.R, KD * T, KD, T)
    m.dve_step, m.pool_step = (Chain(ctx.enter_context(nc.semaphore(n))) for n in ("dve_step", "pool_step"))
    m.scr_u = nc.dram_tensor("scr_u", (P, 8 * 256), F32, kind="Internal").ap()
    m.scr_gate = nc.dram_tensor("scr_gate", (3 * KD, P, T), F32, kind="Internal").ap()
    m.scr_lat = nc.dram_tensor("scr_lat", (P, TT * 672), F32, kind="Internal").ap()
    return m


def reuse_semaphores(m):
    with m.nc.Block() as block:
        @block.sync
        def _(sp):
            for s in m.held:
                sp.sem_clear(s)
    m.scope.close()
    m.scope, m.held = m.ctx.enter_context(ExitStack()), []


def f32(ap):
    return ap.bitcast(F32)


class NormAndTurn:

    def __init__(self, m, tag, gain, squares_to, scaled_to):
        self.m, self.gain, self.squares_to, self.scaled_to = m, gain, squares_to, scaled_to
        self.rows = cols(m.F, 0, TT, D)
        self.sq_done, self.ms_done, self.rstd_done, self.scaled, self.turned, self.hi_done, self.done = (
            m.sem(f"{tag}_{n}") for n in ("sq", "ms", "rstd", "scaled", "turned", "hi", "lo"))
        self.ssq, self.rstd, self.expo = m.stat[:, 0:TT], m.stat[:, 8:8 + TT], m.stat[:, 16:16 + TT]

    def square(self, act, i):
        self.m.nc.scalar.activation(self.squares_to(i), self.rows[:, i, :], ACT.Square,
                                    accum_out=self.ssq[:, i:i + 1]).then_inc(self.sq_done, 1)
        act.wait_ge(self.sq_done, i + 1)

    def mean(self, dve, i):
        dve.wait_ge(self.sq_done, i + 1)
        self.m.nc.vector.tensor_scalar(self.ssq[:, i:i + 1], self.ssq[:, i:i + 1], 1.0 / D, EPS, ALU.mult, ALU.add).then_inc(self.ms_done, 1)

    def powers(self, pool):
        m = self.m
        m.pool_step.on(pool)
        m.pool_step(m.nc.gpsimd.memset(self.expo, -0.5))
        for i in range(TT):
            pool.wait_ge(self.ms_done, i + 1)
            m.nc.gpsimd.tensor_tensor(self.rstd[:, i:i + 1], self.ssq[:, i:i + 1], self.expo[:, i:i + 1], ALU.pow).then_inc(self.rstd_done, 1)

    def scale(self, dve, i):
        dve.wait_ge(self.rstd_done, i + 1)
        self.m.nc.vector.tensor_scalar(self.scaled_to[:, i, :], self.rows[:, i, :], self.rstd[:, i:i + 1], None, ALU.mult).then_inc(self.scaled, 1)

    def turn(self, pe, half):
        for n in range(half * KD, half * KD + KD):
            k = n % KD
            if k == 0:
                pe.wait_ge(self.scaled, 4 * half + 4)
            if n >= 4:
                pe.wait_ge(self.done, n - 3)
            for j in range(4):
                t = self.m.nc.tensor.transpose(self.m.ps[:, n % 4, j * P:(j + 1) * P],
                                               self.scaled_to[:, 4 * half + j, k * P:(k + 1) * P], self.m.ident[:])
            t.then_inc(self.turned, 1)

    def hi(self, act, half):
        for n in range(half * KD, half * KD + KD):
            k = n % KD
            act.wait_ge(self.turned, n + 1)
            self.m.nc.scalar.activation(self.m.h_hi[:, k, half * BANK:(half + 1) * BANK], self.m.ps[:, n % 4, :],
                                        ACT.Copy, scale=self.gain[:, k:k + 1]).then_inc(self.hi_done, 1)

    def lo(self, dve, half):
        for n in range(half * KD, half * KD + KD):
            k, cut = n % KD, slice(half * BANK, (half + 1) * BANK)
            dve.wait_ge(self.hi_done, n + 1)
            self.m.nc.vector.scalar_tensor_tensor(out=self.m.h_lo[:, k, cut], in0=self.m.ps[:, n % 4, :], scalar=self.gain[:, k:k + 1],
                                                  in1=f32(self.m.h_hi[:, k, cut]), op0=ALU.mult, op1=ALU.subtract).then_inc(self.done, 1)


def stage_load_norm_project(m):
    nc = m.nc
    vec_in, row_in, vec_turned, vec_done, const = (m.sem(n) for n in ("vec_in", "row_in", "vec_turned", "vec_done", "const"))
    nrm = NormAndTurn(m, "attn", m.g_attn, lambda i: m.ps[:, 6:8, :].rearrange("p a b -> p (a b)"), cols(m.F, 0, TT, D))
    x_in = [m.sem(f"x_in{i}") for i in range(TT)]

    chunks = [(0, 192), (192, 192), (C_KV, 288), (C_FQ, 256), (C_FK, 256), (C_FV, 260), (C_U, 256)]
    NW = 288
    m.lat = cols(m.F, 0, TT, 672)
    m.fqk = cols(m.F, 5376, TT, 512)
    m.fvf = cols(m.F, 5376 + 4096, TT, 260)
    m.u = cols(m.F, 11552, GR, CH, GC)
    raw = [cols(m.F, 13600 + i * 4 * NW, 4, NW) for i in range(2)]
    W0 = 2 * KD * T
    w_hi = [cols(m.R, W0 + i * 2 * KD * NW, KD, NW) for i in range(2)]
    w_lo = [cols(m.R, W0 + (2 * i + 1) * KD * NW, KD, NW) for i in range(2)]
    raw_in = [m.sem(f"pw_in{i}") for i in range(2)]
    w_hi_done, w_lo_done, prod, out_act, out_dve = (m.sem(n) for n in ("pw_hi", "pw_lo", "p_prod", "p_act", "p_dve"))
    spill = m.sem("spill")
    w_src = m.ins["w_in"][0].rearrange("(k p) n -> p k n", p=P)

    def dest(c, t):
        first, n = chunks[c]
        if first < C_FQ:
            return m.lat[:, t, first:first + n]
        if first < C_FV:
            return m.fqk[:, t, first - C_FQ:first - C_FQ + n]
        if first == C_FV:
            return m.fvf[:, t, :]
        return m.u[:, :, 7 - t, :]

    def made(n):
        width = chunks[n // TT][1]
        src = m.ps[:, n % 4, 0:width]
        return src.rearrange("p (g h) -> p g h", h=GC) if chunks[n // TT][0] == C_U else src

    nch = len(chunks)
    with nc.Block() as block:
        @block.sync
        def _(sp):
            for i in range(TT):
                sp.dma_start(nrm.rows[:, i, :], m.ins["x"][0, i * P:(i + 1) * P, :]).then_inc(x_in[i], 16)
            cw = m.ins["ffn_conv_w"][0]
            sp.dma_start(m.vecs[0:44, :].rearrange("f (j c) -> f j c", j=CONV),
                         cw.rearrange("j (f c) -> f j c", c=P)).then_inc(vec_in, 16)
            at = 44
            for v in (m.ins["attn_norm_g"], m.ins["ffn_norm_g"], m.ins["q_lat_norm_g"], m.ins["kv_lat_norm_g"], m.ins["s5_b_glu"]):
                n = v.shape[1] // P
                sp.dma_start(m.vecs[at:at + n, 0:P], v[0].rearrange("(r c) -> r c", c=P)).then_inc(vec_in, 16)
                at += n
            at = 0
            for v in (m.ins["mla_q_norm_g"], m.ins["mla_k_norm_g"], m.ins["fox_q_norm_g"], m.ins["fox_k_norm_g"], m.ins["fox_f_bias"]):
                n = v.shape[1]
                sp.dma_start(m.rowg[:, at:at + n], v[0].partition_broadcast(P)).then_inc(row_in, 16)
                at += n
            for c, (first, n) in enumerate(chunks):
                for half in range(2):
                    if c >= 1:
                        sp.wait_ge(w_lo_done, 2 * (c - 1) + half + 1)
                    sp.dma_start(raw[half][:, :, 0:n], w_src[:, 4 * half:4 * half + 4, first:first + n]).then_inc(raw_in[half], 16)
            sp.wait_ge(out_act, 3 * TT // 2)
            sp.wait_ge(out_dve, 3 * TT // 2)
            sp.dma_start(m.scr_lat, m.lat.rearrange("p a b -> p (a b)")).then_inc(spill, 16)
            sp.wait_ge(out_act, nch * TT // 2)
            sp.wait_ge(out_dve, nch * TT // 2)
            sp.dma_start(m.scr_u, m.u.rearrange("p g s h -> p (g s h)")).then_inc(spill, 16)
            sp.wait_ge(spill, 32)

        @block.gpsimd
        def _(pool):
            m.pool_step.on(pool)
            m.pool_step(nc.gpsimd.memset(m.ident[:], 0.0))
            m.pool_step(nc.gpsimd.affine_select(out=m.ident[:], in_=m.ident[:], compare_op=ALU.not_equal, fill=1.0,
                                                base=0, pattern=[[-1, P]], channel_multiplier=1))
            m.pool_step(nc.gpsimd.tensor_copy(m.identb[:], m.ident[:]))
            m.pool_step(nc.gpsimd.memset(m.maskb[:], 0.0))
            nc.gpsimd.affine_select(out=m.maskb[:], in_=m.maskb[:], compare_op=ALU.is_ge, fill=NEG,
                                    base=0, pattern=[[-1, P]], channel_multiplier=1).then_inc(const, 1)
            pool.wait_ge(const, 1)
            nrm.powers(pool)

        @block.tensor
        def _(pe):
            pe.wait_ge(const, 1)
            pe.wait_ge(vec_in, 96)
            for j in range(CONV):
                nc.tensor.transpose(m.ps[:, 5, j * P:j * P + 44], m.vecs[0:44, j * P:(j + 1) * P], m.ident[0:44, 0:44])
            nc.tensor.transpose(m.ps[:, 5, 3 * P:3 * P + 67], m.vecs[0:67, 0:P], m.ident[0:67, 0:67]).then_inc(vec_turned, 1)
            nrm.turn(pe, 0)
            nrm.turn(pe, 1)
            pe.wait_ge(nrm.done, 2 * KD)
            n = 0
            for c, (first, width) in enumerate(chunks):
                pe.wait_ge(w_lo_done, 2 * c + 2)
                for t in range(TT):
                    bank = n % 4
                    if n >= 4:
                        pe.wait_ge(out_act if n % 2 == 0 else out_dve, n // 2 - 1)
                    for k in range(KD):
                        if first == C_U:
                            hi, lo = (a[:, k, :].rearrange("p (c s) -> p c s", s=8)[:, :, t] for a in (m.h_hi, m.h_lo))
                        else:
                            hi, lo = (a[:, k, t * P:(t + 1) * P] for a in (m.h_hi, m.h_lo))
                        wh, wl = w_hi[c % 2][:, k, 0:width], w_lo[c % 2][:, k, 0:width]
                        o = m.ps[:, bank, 0:width]
                        nc.tensor.matmul(o, hi, wh, start=(k == 0), stop=False)
                        nc.tensor.matmul(o, hi, wl, start=False, stop=False)
                        mm = nc.tensor.matmul(o, lo, wh, start=False, stop=(k == KD - 1))
                    mm.then_inc(prod, 1)
                    n += 1

        @block.scalar
        def _(act):
            for i in range(TT):
                act.wait_ge(x_in[i], 16)
                nrm.square(act, i)
            act.wait_ge(vec_done, 2)
            nrm.hi(act, 0)
            nrm.hi(act, 1)

            def split(c, half):
                n = chunks[c][1]
                act.wait_ge(raw_in[half], 16 * (c + 1))
                if c >= 2:
                    act.wait_ge(prod, (c - 1) * TT)
                nc.scalar.activation(w_hi[c % 2][:, 4 * half:4 * half + 4, 0:n], raw[half][:, :, 0:n], ACT.Copy).then_inc(w_hi_done, 1)
            for c in range(2):
                split(c, 0), split(c, 1)
            for n in range(nch * TT):
                if n % 2 == 0:
                    act.wait_ge(prod, n + 1)
                    nc.scalar.activation(dest(n // TT, n % TT), made(n), ACT.Copy).then_inc(out_act, 1)
                if n % TT == TT - 1 and n // TT + 2 < nch:
                    split(n // TT + 2, 0), split(n // TT + 2, 1)

        @block.vector
        def _(dve):
            dve.wait_ge(vec_turned, 1)
            nc.vector.tensor_copy(m.conv_w, m.ps[:, 5, 0:3 * P].rearrange("p (j c) -> p j c", j=CONV)[:, :, 0:44]).then_inc(vec_done, 1)
            nc.vector.tensor_copy(m.colv[:, 132:155], m.ps[:, 5, 3 * P + 44:3 * P + 67]).then_inc(vec_done, 1)
            dve.wait_ge(vec_done, 2)
            nrm.mean(dve, 0)
            for i in range(TT):
                if i + 1 < TT:
                    nrm.mean(dve, i + 1)
                nrm.scale(dve, i)
            nrm.lo(dve, 0)
            nrm.lo(dve, 1)

            def split(c, half):
                n = chunks[c][1]
                dve.wait_ge(w_hi_done, 2 * c + half + 1)
                hi = w_hi[c % 2][:, 4 * half:4 * half + 4, 0:n]
                nc.vector.tensor_tensor(w_lo[c % 2][:, 4 * half:4 * half + 4, 0:n], raw[half][:, :, 0:n], f32(hi),
                                        ALU.subtract).then_inc(w_lo_done, 1)
            for c in range(2):
                split(c, 0), split(c, 1)
            for n in range(nch * TT):
                if n % 2 == 1:
                    dve.wait_ge(prod, n + 1)
                    nc.vector.tensor_copy(dest(n // TT, n % TT), made(n)).then_inc(out_dve, 1)
                if n % TT == TT - 1 and n // TT + 2 < nch:
                    split(n // TT + 2, 0), split(n // TT + 2, 1)
            dve.wait_ge(row_in, 80)


class GateFill:

    PER_HALF = 3 * KD

    def __init__(self, m, tag, first, count, early):
        self.m, self.first, self.total = m, first, count * 2 * self.PER_HALF
        self.count, self.early = count, 2 * early
        self.raw, self.stage = cols(m.F, 16384, KD, P), cols(m.F, 17408, BANK)
        at = 2 * KD * T + 12 * T
        self.w_hi = [cols(m.R, at + 2 * i * T, KD, P) for i in range(2)]
        self.w_lo = [cols(m.R, at + (2 * i + 1) * T, KD, P) for i in range(2)]
        self.w_in, self.hi, self.lo, self.half_mm, self.out, self.stored = (
            m.sem(f"{tag}_gate_{n}") for n in ("w_in", "hi", "lo", "mm", "out", "stored"))
        self.at = {"pe": 0, "act": 0, "dve": 0}
        self.copied = 0
        self.w_src = m.ins["w_in"][0].rearrange("(k p) n -> p k n", p=P)

    def bank(self, half):
        return 6 if half < self.early and half % 2 == 0 else 7

    def load(self, sp, u):
        if u < self.count:
            d, n = divmod(self.first + u, 3)
            if u:
                sp.wait_ge(self.lo, u)
            sp.dma_start(self.raw, self.w_src[:, :, C_G + n * D + d * P:C_G + n * D + (d + 1) * P]).then_inc(self.w_in, 16)

    def sync(self, sp):
        self.load(sp, 0)
        self.load(sp, 1)
        for u in range(self.count):
            self.load(sp, u + 2)
            for half in range(2):
                sp.wait_ge(self.out, 2 * u + half + 1)
                sp.dma_start(self.m.scr_gate[self.first + u][:, half * BANK:(half + 1) * BANK], self.stage).then_inc(self.stored, 16)
        sp.wait_ge(self.stored, 32 * self.count)

    def tensor(self, pe, n):
        m, nc = self.m, self.m.nc
        for i in range(self.at["pe"], self.at["pe"] + n):
            half, j = divmod(i, self.PER_HALF)
            u, h = divmod(half, 2)
            k, which = divmod(j, 3)
            if j == 0:
                pe.wait_ge(self.lo, u + 1)
                if half > (half < self.early):
                    pe.wait_ge(self.out, half - (half < self.early))
            w = (self.w_hi, self.w_hi, self.w_lo)[which][u % 2]
            src = (m.h_hi, m.h_lo, m.h_hi)[which]
            mm = nc.tensor.matmul(m.ps[:, self.bank(half), :], w[:, k, :], src[:, k, h * BANK:(h + 1) * BANK], start=(j == 0), stop=(j == self.PER_HALF - 1))
            if j == self.PER_HALF - 1:
                mm.then_inc(self.half_mm, 1)
        self.at["pe"] += n

    def events(self, name, n):
        out = []
        for i in range(self.at[name], self.at[name] + n):
            half, j = divmod(i, self.PER_HALF)
            if j == 0:
                if half and name == "act" and ("copy", half - 1) not in out and self.copied < half:
                    out.append(("copy", half - 1))
                if half == 0:
                    out.append(("split", 0))
                if half % 2 == 0 and half // 2 + 1 < self.count:
                    out.append(("split", half // 2 + 1))
        self.at[name] += n
        return out

    def scalar(self, act, n):
        m, nc = self.m, self.m.nc
        for what, u in self.events("act", n):
            if what == "copy":
                self.copy_out(act)
                continue
            act.wait_ge(self.w_in, 16 * (u + 1))
            if u >= 2:
                act.wait_ge(self.half_mm, 2 * (u - 1))
            nc.scalar.activation(self.w_hi[u % 2], self.raw, ACT.Copy).then_inc(self.hi, 1)

    def copy_made(self, act):
        while (self.copied + 1) * self.PER_HALF <= self.at["act"]:
            self.copy_out(act)

    def copy_out(self, act):
        act.wait_ge(self.half_mm, self.copied + 1)
        if self.copied:
            act.wait_ge(self.stored, 16 * self.copied)
        self.m.nc.scalar.activation(self.stage, self.m.ps[:, self.bank(self.copied), :], ACT.Copy).then_inc(self.out, 1)
        self.copied += 1

    def vector(self, dve, n):
        for _, u in self.events("dve", n):
            dve.wait_ge(self.hi, u + 1)
            self.m.nc.vector.tensor_tensor(self.w_lo[u % 2], self.raw, f32(self.w_hi[u % 2]), ALU.subtract).then_inc(self.lo, 1)

    def finish(self, act):
        while self.copied < 2 * self.count:
            self.copy_out(act)
        assert set(self.at.values()) <= {self.total, self.at["pe"]}


ATT_STEPS = H * TT


def attention(m, tag, kd, q_of, k_of, v_of, q_t, k_t, p_buf, pt_buf, branch, ready, fill, n_fill):
    nc, ps = m.nc, m.ps
    scores, negmax, exped, normed, filled, copied, pv, o_hi, o_lo, rs = (
        m.sem(f"{tag}_{n}") for n in ("scores", "negmax", "exp", "norm", "filled", "copied", "pv", "o_hi", "o_lo", "recip"))
    nmax, rsum, rinv = m.stat[:, 0:2], m.stat[:, 2:4], m.stat[:, 4:6]
    S = [m.ps[:, 0:2, :].rearrange("p b n -> p (b n)"), m.ps[:, 2:4, :].rearrange("p b n -> p (b n)")]

    fills, after_turn = [], {}
    order = []
    if q_of is not None:
        order.append(("qk", 0))
    nb = len(q_t)
    for s in range(ATT_STEPS + 2):
        if s < ATT_STEPS:
            order.append(("s", s))
        if 1 <= s <= ATT_STEPS:
            order.append(("t", s - 1))
        if s < ATT_STEPS:
            order.append(("f", (s + 1) * n_fill // ATT_STEPS - s * n_fill // ATT_STEPS))
        if s >= 2:
            order.append(("v", s - 2))
        if q_of is not None and s % TT == 5 and s // TT + 1 < H:
            order.append(("qk", s // TT + 1))
    qk_until, t_until = {}, {}
    for what, n in order:
        if what == "qk":
            fills += [("qk", n, w, half) for w in range(2) for half in range(2)]
            qk_until[n] = len(fills)
        elif what == "t":
            tiles = n % TT + 1
            fills += [("p", n, a, min(4, tiles - a)) for a in range(0, tiles, 4)]
            t_until[n] = len(fills)

    def tensor(pe):
        ready(pe)
        f = 0
        for what, n in order:
            h, i = divmod(n, TT)
            if what == "f":
                fill.tensor(pe, n)
            elif what == "qk":
                h = n
                for w, (src, _) in enumerate(((q_of, q_t), (k_of, k_t))):
                    for half in range(2):
                        if f >= 2:
                            pe.wait_ge(copied, f - 1)
                        for j in range(4):
                            tr = nc.tensor.transpose(ps[0:kd, 4 + f % 2, j * P:(j + 1) * P], src(h, 4 * half + j), m.ident[:])
                        tr.then_inc(filled, 1)
                        f += 1
            elif what == "s":
                if i == 0 and q_of is not None:
                    pe.wait_ge(copied, qk_until[h])
                if n >= 2:
                    pe.wait_ge(exped, n - 1)
                keys = (i + 1) * P
                for a in range(0, keys, BANK):
                    b = min(keys, a + BANK)
                    diag = b == keys
                    mm = nc.tensor.matmul(S[n % 2][:, a:b], q_t[h % nb][0:kd, i * P:(i + 1) * P], k_t[h % nb][0:kd, a:b],
                                          start=True, stop=not diag)
                mm = nc.tensor.matmul(S[n % 2][:, keys - P:keys], m.identb[:], m.maskb[:], start=False, stop=True)
                mm.then_inc(scores, 1)
            elif what == "t":
                pe.wait_ge(normed, n + 1)
                for a in range(0, i + 1, 4):
                    if f >= 2:
                        pe.wait_ge(copied, f - 1)
                    for j in range(a, min(a + 4, i + 1)):
                        tr = nc.tensor.transpose(ps[:, 4 + f % 2, (j - a) * P:(j - a + 1) * P],
                                                 p_buf[n % 2][:, j * P:(j + 1) * P], m.ident[:])
                    tr.then_inc(filled, 1)
                    f += 1
            else:
                pe.wait_ge(copied, t_until[n])
                g = n // 4
                if i % 4 == 0 and g >= 1:
                    pe.wait_ge(o_lo, g)
                rows = slice(64 * (h % 2), 64 * (h % 2) + 64)
                for j in range(i + 1):
                    mm = nc.tensor.matmul(ps[rows, 6, (i % 4) * P:(i % 4 + 1) * P], v_of(h, j),
                                          pt_buf[n % 2][:, j * P:(j + 1) * P], start=(j == 0), stop=(j == i))
                mm.then_inc(pv, 1)

    def out_rows(g):
        h, half = divmod(g, 2)
        rows = slice(64 * (h % 2), 64 * (h % 2) + 64)
        k = 2 * branch + h // 2
        return rows, k, slice(half * BANK, (half + 1) * BANK)

    def scalar(act):
        f = 0
        for what, n in order:
            if what == "f":
                fill.scalar(act, n)
                continue
            if what == "s":
                keys = (n % TT + 1) * P
                fill.copy_made(act)
                act.wait_ge(negmax, n + 1)
                if n >= 2:
                    act.wait_ge(filled, t_until[n - 2])
                    act.wait_ge(rs, n - 1)
                nc.scalar.activation(p_buf[n % 2][:, 0:keys], S[n % 2][:, 0:keys], ACT.Exp, bias=nmax[:, n % 2:n % 2 + 1],
                                     accum_out=rsum[:, n % 2:n % 2 + 1]).then_inc(exped, 1)
                continue
            if what in ("qk", "t"):
                while f < len(fills) and fills[f][0] == ("qk" if what == "qk" else "p") and fills[f][1] == n:
                    act.wait_ge(filled, f + 1)
                    if what == "qk":
                        _, h, w, half = fills[f]
                        if half == 0 and w == 0 and h >= 2:
                            act.wait_ge(scores, (h - 1) * TT)
                        dst = (q_t, k_t)[w][h % 2][0:kd, half * BANK:(half + 1) * BANK]
                        nc.scalar.activation(dst, ps[0:kd, 4 + f % 2, :], ACT.Copy).then_inc(copied, 1)
                    else:
                        _, s, a, c = fills[f]
                        if a == 0 and s >= 2:
                            act.wait_ge(pv, s - 1)
                        nc.scalar.activation(pt_buf[s % 2][:, a * P:(a + c) * P], ps[:, 4 + f % 2, 0:c * P], ACT.Copy).then_inc(copied, 1)
                    f += 1
            if what == "v" and n % 4 == 3:
                g = n // 4
                rows, k, cut = out_rows(g)
                act.wait_ge(pv, n + 1)
                nc.scalar.activation(m.br_hi[rows, k, cut], ps[rows, 6, :], ACT.Copy).then_inc(o_hi, 1)

    def vector(dve):
        for what, n in order:
            if what == "f":
                fill.vector(dve, n)
            elif what == "s":
                keys = (n % TT + 1) * P
                dve.wait_ge(scores, n + 1)
                if n >= 2:
                    dve.wait_ge(exped, n - 1)
                nc.vector.tensor_reduce(nmax[:, n % 2:n % 2 + 1], S[n % 2][:, 0:keys], AX.X, ALU.max, negate=True).then_inc(negmax, 1)
                dve.wait_ge(exped, n + 1)
                nc.vector.reciprocal(rinv[:, n % 2:n % 2 + 1], rsum[:, n % 2:n % 2 + 1]).then_inc(rs, 1)
                dve.wait_ge(rs, n + 1)
                nc.vector.tensor_scalar(p_buf[n % 2][:, 0:keys], p_buf[n % 2][:, 0:keys], rinv[:, n % 2:n % 2 + 1], None,
                                        ALU.mult).then_inc(normed, 1)
            elif what == "v" and n % 4 == 3:
                g = n // 4
                rows, k, cut = out_rows(g)
                dve.wait_ge(o_hi, g + 1)
                nc.vector.tensor_tensor(m.br_lo[rows, k, cut], ps[rows, 6, :], f32(m.br_hi[rows, k, cut]),
                                        ALU.subtract).then_inc(o_lo, 1)
    return Programs(scalar, vector, tensor)


FOX_UNITS = 11
MLA_UNITS = 3 * KD - FOX_UNITS
MLA_PREP_UNITS = 5


def stage_fox(m):
    nc = m.nc
    ndim = 2 * TT * FH
    qk = m.fqk.rearrange("p t (g d) -> p (t g) d", d=FD)
    KA = FD + 2
    aug = cols(m.F, 0, TT, 2 * FH, KA)
    sq = cols(m.F, 11552, ndim, FD)
    ssq, rstd, expo = m.stat[:, 0:ndim], m.statb[:, 0:ndim], cols(m.F, 15648, ndim)
    small = [cols(m.F, 15712 + 32 * i, TT, FH) for i in range(12)]
    z, e, den, s1, s2, acc, tot, pre, cum, ez, one_c, _ = small
    ones = cols(m.F, 16096, P)
    upper = cols(m.F, 16224, P)
    q_t = [cols(m.F, 5376 + i * T, T) for i in range(2)]
    k_t = [cols(m.F, 5376 + (2 + i) * T, T) for i in range(2)]
    p_buf = [cols(m.F, 11552 + i * T, T) for i in range(2)]
    pt_buf = [cols(m.F, 11552 + (2 + i) * T, T) for i in range(2)]
    W0 = 2 * KD * T
    m.br_hi = cols(m.R, W0, 6, T)
    m.br_lo = cols(m.R, W0 + 6 * T, 6, T)
    sq_done, ms_done, rstd_done, const, z_done, e_done, log_done, sum_done, prep = (
        m.sem(f"fox_{n}") for n in ("sq", "ms", "rstd", "const", "z", "e", "log", "sum", "prep"))
    gq, gk, fb = m.rowg[:, 192:256], m.rowg[:, 256:320], m.rowg[:, 320:324]

    def ready(pe):
        pe.wait_ge(prep, 1)
    fill = GateFill(m, "fox", 0, FOX_UNITS, 3)
    UNIT = 2 * GateFill.PER_HALF
    att = attention(m, "fox", KA, lambda h, t: aug[:, t, h, :], lambda h, t: aug[:, t, FH + h, :],
                    lambda h, j: m.fvf[:, j, h * FD:(h + 1) * FD], q_t, k_t, p_buf, pt_buf, 1, ready, fill, (FOX_UNITS - 3) * UNIT)

    with nc.Block() as block:
        @block.sync
        def _(sp):
            fill.sync(sp)

        @block.gpsimd
        def _(pool):
            m.pool_step.on(pool)
            nc.gpsimd.memset(expo, -0.5).then_inc(const, 1)
            nc.gpsimd.memset(ones, 1.0).then_inc(const, 1)
            pool.wait_ge(const, 2)
            nc.gpsimd.affine_select(out=upper, in_=ones, compare_op=ALU.is_ge, fill=0.0, base=0,
                                    pattern=[[1, P]], channel_multiplier=-1).then_inc(const, 1)
            pool.wait_ge(ms_done, 1)
            nc.gpsimd.tensor_tensor(rstd, ssq, expo, ALU.pow).then_inc(rstd_done, 1)

        @block.scalar
        def _(act):
            fill.scalar(act, UNIT // 2)
            act.wait_ge(z_done, 1)
            nc.scalar.activation(e, ez, ACT.Exp).then_inc(e_done, 1)
            nc.scalar.activation(sq, qk, ACT.Square).then_inc(sq_done, 1)
            fill.scalar(act, 3 * UNIT - UNIT // 2)
            att.scalar(act)
            fill.finish(act)

        @block.tensor
        def _(pe):
            fill.tensor(pe, UNIT)
            pe.wait_ge(const, 3)
            pe.wait_ge(log_done, 1)
            nc.tensor.matmul(m.ps[:, 5, 0:32], upper, z.rearrange("p t h -> p (t h)"), start=True, stop=True)
            nc.tensor.matmul(m.ps[:, 5, 32:64], ones, z.rearrange("p t h -> p (t h)"), start=True, stop=True).then_inc(sum_done, 1)
            fill.tensor(pe, 2 * UNIT)
            att.tensor(pe)

        @block.vector
        def _(dve):
            step = m.dve_step.on(dve)
            V = nc.vector
            step(V.tensor_tensor(z, m.fvf[:, :, 256:260], fb.unsqueeze(1).to_broadcast([P, TT, FH]), ALU.add))
            V.scalar_tensor_tensor(out=ez, in0=z, scalar=-1.0, in1=z, op0=ALU.mult, op1=ALU.min).then_inc(z_done, 1)
            step(V.tensor_scalar(gq, gq, float(FD) ** -0.5, None, ALU.mult))
            fill.vector(dve, UNIT)
            dve.wait_ge(e_done, 1)
            step(V.tensor_scalar(den, e, 2.0, None, ALU.add))
            step(V.reciprocal(den, den))
            step(V.tensor_tensor(s1, e, den, ALU.mult))
            step(V.tensor_tensor(s2, s1, s1, ALU.mult))
            step(V.tensor_scalar(acc, s2, 2.0 / 17, 2.0 / 15, ALU.mult, ALU.add))
            for k in (13, 11, 9, 7, 5, 3, 1):
                step(V.tensor_tensor(acc, acc, s2, ALU.mult))
                step(V.tensor_scalar(acc, acc, 2.0 / k, None, ALU.add))
            step(V.tensor_tensor(acc, acc, s1, ALU.mult))
            V.scalar_tensor_tensor(out=z, in0=z, scalar=0.0, in1=acc, op0=ALU.min, op1=ALU.subtract).then_inc(log_done, 1)
            fill.vector(dve, UNIT)
            dve.wait_ge(sq_done, 1)
            step(V.tensor_reduce(ssq, sq, AX.X, ALU.add))
            V.tensor_scalar(ssq, ssq, 1.0 / FD, EPS, ALU.mult, ALU.add).then_inc(ms_done, 1)
            dve.wait_ge(sum_done, 1)
            step(V.tensor_copy(tot.rearrange("p t h -> p (t h)"), m.ps[:, 5, 32:64]))
            step(V.memset(pre[:, 0, :], 0.0))
            for t in range(1, TT):
                step(V.tensor_tensor(pre[:, t, :], pre[:, t - 1, :], tot[:, t - 1, :], ALU.add))
            step(V.tensor_tensor(cum, m.ps[:, 5, 0:32].rearrange("p (t h) -> p t h", h=FH), pre, ALU.add))
            step(V.memset(aug[:, :, 0:FH, FD:FD + 1], 1.0))
            step(V.tensor_copy(aug[:, :, 0:FH, FD + 1], cum))
            step(V.tensor_scalar(aug[:, :, FH:2 * FH, FD], cum, -1.0, None, ALU.mult))
            step(V.memset(aug[:, :, FH:2 * FH, FD + 1:FD + 2], 1.0))
            fill.vector(dve, UNIT)
            dve.wait_ge(rstd_done, 1)
            step(V.tensor_tensor(sq, qk, rstd.unsqueeze(2).to_broadcast([P, ndim, FD]), ALU.mult))
            sqv = sq.rearrange("p (t g) d -> p t g d", g=2 * FH)
            step(V.tensor_tensor(aug[:, :, 0:FH, 0:FD], sqv[:, :, 0:FH, :],
                                 gq.unsqueeze(1).unsqueeze(1).to_broadcast([P, TT, FH, FD]), ALU.mult))
            V.tensor_tensor(aug[:, :, FH:2 * FH, 0:FD], sqv[:, :, FH:2 * FH, :],
                            gk.unsqueeze(1).unsqueeze(1).to_broadcast([P, TT, FH, FD]), ALU.mult).then_inc(prep, 1)
            att.vector(dve)


INV_FREQ = [float(f) for f in (np.float32(10000.0) ** (-np.arange(0, ROPE, 2, dtype=np.float32) / np.float32(ROPE)))]
TWO_PI = 2 * math.pi
PI_A = 6.28125
PI_B = float(np.float32(round((TWO_PI - PI_A) * 2 ** 22) / 2 ** 22))
PI_C = TWO_PI - PI_A - PI_B
ROUND = 1.5 * 2 ** 23
PI32 = 3.1415925


def reduced(nc, step, ang, turns, absang):
    V = nc.vector
    step(V.tensor_scalar(turns, ang, 1.0 / TWO_PI, ROUND, ALU.mult, ALU.add))
    step(V.tensor_scalar(turns, turns, ROUND, None, ALU.subtract))
    for part in (PI_A, PI_B, PI_C):
        step(V.scalar_tensor_tensor(out=ang, in0=turns, scalar=-part, in1=ang, op0=ALU.mult, op1=ALU.add))
    step(V.tensor_scalar(ang, ang, PI32, -PI32, ALU.min, ALU.max))
    step(V.scalar_tensor_tensor(out=absang, in0=ang, scalar=-1.0, in1=ang, op0=ALU.mult, op1=ALU.min))
    return V.tensor_scalar(absang, absang, math.pi / 2, None, ALU.add)


def stage_mla(m):
    nc = m.nc
    lat = cols(m.F, 0, TT, 672)
    lat_t = cols(m.F, 7168, 5, T)
    w_uq = cols(m.F, 15360, 3, H * QK)
    w_ukv = cols(m.F, 16512, 2, H * 2 * NOPE)
    q = cols(m.F, 12288, TT, H, QK)
    kv = cols(m.F, 0, TT, H, 2 * NOPE)
    k = cols(m.F, 7168, TT, H, QK)
    v = cols(m.F, 10240, TT, H, VD)
    lsq = cols(m.F, 12288, TT, Q_RANK)
    sq = cols(m.F, 0, TT * H, QK)
    ang, sin, cos, turns, t1 = (cols(m.F, 5376 + i * 128, TT, ROPE // 2) for i in range(5))
    pos_i, pos8, kr = cols(m.F, 6016, P), cols(m.F, 6144, P), cols(m.F, 6272, TT, ROPE)
    pos_f, inv_freq = cols(m.F, 6528, TT), cols(m.F, 6536, ROPE // 2)
    tmp = [cols(m.F, 15360 + i * 512, TT, H, ROPE // 2) for i in range(2)]
    q_t = [cols(m.F, i * T, T) for i in range(2)]
    k_t = [cols(m.F, (2 + i) * T, T) for i in range(2)]
    p_buf = [cols(m.F, 4096, T), cols(m.F, 15360, T)]
    pt_buf = [cols(m.F, 5120 + i * T, T) for i in range(2)]
    ssq, rstd, expo = m.stat[:, 0:48], m.statb[:, 0:48], cols(m.F, 6560, 48)
    gq, gk = m.rowg[:, 0:QK], m.rowg[:, QK:2 * QK]

    lat_in, w_in, pos_in, const, pos_t, sq_done, ms_done, rstd_done, ang_done, rope_done, scaled, filled, copied, q_prod, kv_prod, q_out, kv_out, prep = (
        m.sem(f"mla_{n}") for n in ("lat_in", "w_in", "pos_in", "const", "pos_t", "sq", "ms", "rstd", "ang", "sincos", "scaled",
                                    "filled", "copied", "q_prod", "kv_prod", "q_out", "kv_out", "prep"))

    pos_t_done = m.sem("mla_pos_t_done")

    def ready(pe):
        pe.wait_ge(prep, 1)
    fill = GateFill(m, "mla", FOX_UNITS, MLA_UNITS, MLA_PREP_UNITS)
    UNIT = 2 * GateFill.PER_HALF
    att = attention(m, "mlaa", QK, lambda h, t: q[:, t, h, :], lambda h, t: k[:, t, h, :],
                    lambda h, j: v[:, j, h, :], q_t, k_t, p_buf, pt_buf, 0, ready, fill,
                    (MLA_UNITS - MLA_PREP_UNITS) * UNIT)
    NQF = 3 * 2
    with nc.Block() as block:
        @block.sync
        def _(sp):
            sp.dma_start(lat.rearrange("p a b -> p (a b)"), m.scr_lat).then_inc(lat_in, 16)
            sp.dma_start(w_uq, m.ins["w_uq"][0].rearrange("(k p) h d -> p k (h d)", p=P)).then_inc(w_in, 16)
            sp.dma_start(w_ukv, m.ins["w_ukv"][0].rearrange("(k p) h d -> p k (h d)", p=P)).then_inc(w_in, 16)
            sp.dma_start(pos_i.bitcast(I32)[0:TT, :], m.ins["positions"][0].rearrange("(i p) -> i p", p=P)).then_inc(pos_in, 16)
            sp.wait_ge(kv_out, TT)
            fill.sync(sp)

        @block.gpsimd
        def _(pool):
            nc.gpsimd.memset(expo, -0.5).then_inc(const, 1)
            for j, f in enumerate(INV_FREQ):
                nc.gpsimd.memset(inv_freq[:, j:j + 1], f).then_inc(const, 1)
            pool.wait_ge(const, 1 + len(INV_FREQ))
            for n, (a, b) in enumerate(((0, 16), (16, 48), (16, 48))):
                pool.wait_ge(ms_done, n + 1)
                if n == 2:
                    a, b = 16, 48
                nc.gpsimd.tensor_tensor(rstd[:, a:b], ssq[:, a:b], expo[:, a:b], ALU.pow).then_inc(rstd_done, 1)

        @block.scalar
        def _(act):
            act.wait_ge(ang_done, 1)
            nc.scalar.activation(sin, ang, ACT.Sin).then_inc(rope_done, 1)
            nc.scalar.activation(cos, turns, ACT.Sin).then_inc(rope_done, 1)
            for f in range(10):
                act.wait_ge(filled, f + 1)
                r, half = divmod(f, 2)
                g = m.g_qlat[:, r:r + 1] if r < 3 else m.g_kvlat[:, r - 3:r - 2]
                nc.scalar.activation(lat_t[:, r, half * BANK:(half + 1) * BANK], m.ps[:, f % 4, :], ACT.Copy, scale=g).then_inc(copied, 1)
            for t in range(TT):
                act.wait_ge(q_prod, t + 1)
                nc.scalar.activation(q[:, t].rearrange("p h d -> p (h d)"), m.ps[:, t % 4, 0:H * QK], ACT.Copy).then_inc(q_out, 1)
            fill.scalar(act, MLA_PREP_UNITS * UNIT)
            att.scalar(act)
            fill.finish(act)

        @block.tensor
        def _(pe):
            pe.wait_ge(pos_t, 1)
            nc.tensor.transpose(m.ps[:, 7, 0:TT], pos8[0:TT, :], m.ident[0:TT, 0:TT]).then_inc(pos_t_done, 1)
            pe.wait_ge(scaled, 2)
            f = 0
            for r in range(5):
                for half in range(2):
                    if f >= 4:
                        pe.wait_ge(copied, f - 3)
                    for j in range(4):
                        tr = nc.tensor.transpose(m.ps[:, f % 4, j * P:(j + 1) * P], lat[:, 4 * half + j, r * P:(r + 1) * P], m.ident[:])
                    tr.then_inc(filled, 1)
                    f += 1
            pe.wait_ge(copied, 10)
            pe.wait_ge(w_in, 32)
            for t in range(TT):
                if t >= 4:
                    pe.wait_ge(q_out, t - 3)
                for r in range(3):
                    mm = nc.tensor.matmul(m.ps[:, t % 4, 0:H * QK], lat_t[:, r, t * P:(t + 1) * P], w_uq[:, r, :], start=(r == 0), stop=(r == 2))
                mm.then_inc(q_prod, 1)
                if t >= 2:
                    pe.wait_ge(kv_out, t - 1)
                for r in range(2):
                    mm = nc.tensor.matmul(m.ps[:, 4 + t % 2, :], lat_t[:, 3 + r, t * P:(t + 1) * P], w_ukv[:, r, :], start=(r == 0), stop=(r == 1))
                mm.then_inc(kv_prod, 1)
            fill.tensor(pe, MLA_PREP_UNITS * UNIT)
            att.tensor(pe)

        @block.vector
        def _(dve):
            step = m.dve_step.on(dve)
            V = nc.vector
            dve.wait_ge(pos_in, 16)
            V.tensor_copy(pos8[0:TT, :], pos_i.bitcast(I32)[0:TT, :]).then_inc(pos_t, 1)
            step(V.tensor_scalar(gq, gq, float(QK) ** -0.5, None, ALU.mult))
            dve.wait_ge(lat_in, 16)
            for n, (a, b) in enumerate(((0, Q_RANK), (Q_RANK, Q_RANK + KV_RANK))):
                part = lsq[:, :, 0:b - a]
                step(V.tensor_tensor(part, lat[:, :, a:b], lat[:, :, a:b], ALU.mult))
                step(V.tensor_reduce(ssq[:, 8 * n:8 * n + 8], part, AX.X, ALU.add))
                ins = V.tensor_scalar(ssq[:, 8 * n:8 * n + 8], ssq[:, 8 * n:8 * n + 8], 1.0 / (b - a), EPS, ALU.mult, ALU.add)
                ins.then_inc(ms_done, 1) if n else step(ins)
            dve.wait_ge(pos_t_done, 1)
            step(V.tensor_copy(pos_f, m.ps[:, 7, 0:TT]))
            dve.wait_ge(const, 1 + len(INV_FREQ))
            step(V.tensor_copy(t1, pos_f.unsqueeze(2).to_broadcast([P, TT, ROPE // 2])))
            step(V.tensor_tensor(ang, t1, inv_freq.unsqueeze(1).to_broadcast([P, TT, ROPE // 2]), ALU.mult))
            reduced(nc, step, ang, t1, turns).then_inc(ang_done, 1)
            dve.wait_ge(rstd_done, 1)
            for n, (a, b) in enumerate(((0, Q_RANK), (Q_RANK, Q_RANK + KV_RANK))):
                V.tensor_tensor(lat[:, :, a:b], lat[:, :, a:b], rstd[:, 8 * n:8 * n + 8].unsqueeze(2).to_broadcast([P, TT, b - a]),
                                ALU.mult).then_inc(scaled, 1)
            step(V.tensor_copy(kr, lat[:, :, C_KR:C_KR + ROPE]))
            for t in range(TT):
                dve.wait_ge(kv_prod, t + 1)
                V.tensor_copy(kv[:, t].rearrange("p h d -> p (h d)"), m.ps[:, 4 + t % 2, :]).then_inc(kv_out, 1)
            dve.wait_ge(kv_out, TT)
            step(V.tensor_copy(k[:, :, :, 0:NOPE], kv[:, :, :, 0:NOPE]))
            step(V.tensor_copy(k[:, :, :, NOPE:QK], kr.unsqueeze(2).to_broadcast([P, TT, H, ROPE])))
            step(V.tensor_copy(v, kv[:, :, :, NOPE:]))
            fill.vector(dve, UNIT)
            dve.wait_ge(q_out, TT)
            dve.wait_ge(rope_done, 2)
            for n, (a, g) in enumerate(((k, gk), (q, gq))):
                flat = a.rearrange("p t h d -> p (t h) d")
                step(V.tensor_tensor(sq, flat, flat, ALU.mult))
                fill.vector(dve, (MLA_PREP_UNITS - 1) // 2 * UNIT)
                step(V.tensor_reduce(ssq[:, 16:48], sq, AX.X, ALU.add))
                V.tensor_scalar(ssq[:, 16:48], ssq[:, 16:48], 1.0 / QK, EPS, ALU.mult, ALU.add).then_inc(ms_done, 1)
                dve.wait_ge(rstd_done, 2 + n)
                step(V.tensor_tensor(sq, flat, rstd[:, 16:48].unsqueeze(2).to_broadcast([P, TT * H, QK]), ALU.mult))
                step(V.tensor_tensor(flat, sq, g.unsqueeze(1).to_broadcast([P, TT * H, QK]), ALU.mult))
                x1, x2 = a[:, :, :, NOPE:NOPE + ROPE // 2], a[:, :, :, NOPE + ROPE // 2:QK]
                sb, cb = (z.unsqueeze(2).to_broadcast([P, TT, H, ROPE // 2]) for z in (sin, cos))
                step(V.tensor_tensor(tmp[0], x1, sb, ALU.mult))
                step(V.tensor_tensor(tmp[1], x2, sb, ALU.mult))
                step(V.tensor_tensor(x1, x1, cb, ALU.mult))
                step(V.tensor_tensor(x2, x2, cb, ALU.mult))
                step(V.tensor_tensor(x1, x1, tmp[1], ALU.subtract))
                last = V.tensor_tensor(x2, x2, tmp[0], ALU.add)
                step(last) if n == 0 else last.then_inc(prep, 1)
            att.vector(dve)


def stage_s5(m):
    nc = m.nc
    J = GR // 2
    u = cols(m.F, 0, GR, CH, GC)
    u_t = cols(m.F, 2048, GR, NCH)
    m_re = cols(m.F, 4096, J, 2, 9, GC)
    m_im = cols(m.F, 6400, J, 2, 9, GC)
    b_rep = [cols(m.F, 8704 + i * 1024, J, CH, GC) for i in range(2)]
    w = [cols(m.F, 10752 + i * 1024, J, CH, GC) for i in range(2)]
    w_t = [cols(m.F, 12800 + i * 1024, J, P) for i in range(2)]
    kk = cols(m.F, 14848, GR, CH * GC)
    toep = cols(m.F, 10752, GR, CH * GC)
    tab = [cols(m.F, 8704 + i * 1024, J, NCH) for i in range(2)]
    z_in = [cols(m.F, 14848 + i * 1024, J, NCH) for i in range(2)]
    z = [cols(m.F, 12800 + i * 1024, J, NCH) for i in range(2)]
    s_prev = [cols(m.F, 14848 + i * 1024, J, NCH) for i in range(2)]
    tmp, rho = cols(m.F, 0, J, NCH), cols(m.F, 1024, J, NCH)
    y = cols(m.F, 12800, CH, GR, GC)
    y_t = cols(m.F, 8704, 2, NCH, CH)
    w_glu = cols(m.F, 0, 2, GR * GC)
    sg = [cols(m.F, 512 + i * BANK, BANK) for i in range(2)]
    at = [16896]

    def small(*dims):
        n = math.prod(dims)
        at[0] += n
        assert at[0] <= FW
        return cols(m.F, at[0] - n, *dims)
    b = [small(J, GC), small(J, GC)]
    p9, a9, t9, e9, l_re, l_im = (small(J, 9) for _ in range(6))
    lre, lim, stp, a1, th, tt, ta, q_re, q_im, den, t8 = (small(J) for _ in range(11))
    ki, mask16 = small(9), small(GC)
    crow = [m.vecs[:, i * P:(i + 1) * P] for i in range(2)]
    rows = cols(m.F, 14848, 3 * P)
    bb = [cols(m.F, 15232 + i * 128, J, GC) for i in range(2)]
    cc = [cols(m.F, 15488 + i * 128, J, GC) for i in range(2)]
    d_row = cols(m.F, 15744, GR, GC)
    cidx = cols(m.F, 16000, NCH)
    pq = [cols(m.F, 16128 + i * 128, J, GC) for i in range(4)]
    names = ("u_in", "p_in", "r_in", "c_in", "step_b", "row_t", "row_c", "exp1", "cst", "ang9", "sc9", "w_rdy", "b_rdy", "w_ps",
             "w_cp", "u_ps", "u_cp", "k_ps", "k_cp", "toep_in", "x_ps", "tab_a", "tab_s", "s_rdy", "y_ps", "y_cp", "yt_ps", "yt_cp",
             "zero", "glu_in", "g_ps", "g_sg", "g_y", "g_hi", "g_lo", "cidx", "rho")
    s = {n: m.sem(f"s5_{n}") for n in names}
    ps = m.ps
    cidx_keep = m.cidx[:]

    def y_out(f):
        return cols(m.F, 1536 + f * BANK, BANK)

    with nc.Block() as block:
        @block.sync
        def _(sp):
            for i, v in enumerate((m.ins["s5_lambda_re"], m.ins["s5_lambda_im"])):
                sp.dma_start(rows[0:J, i * P:(i + 1) * P], v[0].rearrange("(j g) p -> j (g p)", g=2)).then_inc(s["r_in"], 16)
            sp.dma_start(stp[0:J, 0:2], m.ins["s5_log_step"][0].rearrange("(j g) -> j g", g=2)).then_inc(s["r_in"], 16)
            for i, v in enumerate((m.ins["s5_c_re"], m.ins["s5_c_im"])):
                vj = v[0].rearrange("(j g) h p -> g j h p", g=2)
                for g in range(2):
                    for j in range(J):
                        sp.dma_start(crow[i][j * GC:(j + 1) * GC, g * ST:(g + 1) * ST], vj[g, j]).then_inc(s["c_in"], 16)
            for i, v in enumerate((m.ins["s5_b_re"], m.ins["s5_b_im"])):
                vj = v[0].rearrange("(j g) p h -> g p j h", g=2)
                for g in range(2):
                    sp.dma_start(b[i][g * ST:(g + 1) * ST], vj[g]).then_inc(s["p_in"], 16)
            sp.dma_start(d_row.rearrange("p g h -> p (g h)"), m.ins["s5_d"][0].rearrange("g h -> (g h)").partition_broadcast(P)).then_inc(s["p_in"], 16)
            sp.dma_start(u.rearrange("p g s h -> p (g s h)"), m.scr_u).then_inc(s["u_in"], 16)
            sp.wait_ge(s["k_cp"], 4)
            sp.wait_ge(s["zero"], 1)
            for kap in range(CH):
                lag = (CH - 1 - kap) * GC
                r = slice(kap * GC, (kap + 1) * GC)
                sp.dma_start(toep[r, :, lag:], kk[r, :, 0:CH * GC - lag]).then_inc(s["toep_in"], 16)
            sp.wait_ge(s["s_rdy"], 1)
            sp.dma_start(w_glu, m.ins["s5_w_glu"][0].rearrange("(k p) n -> p k n", p=P)).then_inc(s["glu_in"], 16)

        @block.gpsimd
        def _(pool):
            nc.gpsimd.iota(ki.bitcast(I32), pattern=[[1, 9]], base=0, channel_multiplier=0).then_inc(s["cst"], 1)
            nc.gpsimd.iota(cidx.bitcast(I32), pattern=[[1, NCH]], base=0, channel_multiplier=0).then_inc(s["cst"], 1)
            nc.gpsimd.memset(m_re.rearrange("p a b c d -> p (a b c d)"), 0.0).then_inc(s["cst"], 1)
            nc.gpsimd.memset(m_im.rearrange("p a b c d -> p (a b c d)"), 0.0).then_inc(s["cst"], 1)

        @block.scalar
        def _(act):
            A = nc.scalar.activation
            act.wait_ge(s["row_c"], 3)
            A(stp, stp, ACT.Exp).then_inc(s["exp1"], 1)
            act.wait_ge(s["ang9"], 2)
            A(e9, a9, ACT.Exp).then_inc(s["sc9"], 1)
            A(l_im, p9, ACT.Sin).then_inc(s["sc9"], 1)
            A(l_re, t9, ACT.Sin).then_inc(s["sc9"], 1)
            for f in range(4):
                act.wait_ge(s["u_ps"], f + 1)
                A(u_t[:, 4 * f:4 * f + 4, :].rearrange("p g c -> p (g c)"), ps[:, f, :], ACT.Copy).then_inc(s["u_cp"], 1)
            for f in range(4):
                act.wait_ge(s["w_ps"], f + 1)
                A(w_t[f // 2][:, 4 * (f % 2):4 * (f % 2) + 4, :].rearrange("p j c -> p (j c)"), ps[:, 4 + f, :], ACT.Copy).then_inc(s["w_cp"], 1)
            act.wait_ge(s["tab_a"], 1)
            A(tab[1], tab[1], ACT.Sin).then_inc(s["tab_s"], 1)
            A(tab[0], tab[0], ACT.Sin).then_inc(s["tab_s"], 1)
            for f in range(4):
                act.wait_ge(s["y_ps"], f + 1)
                dst = y[:, :, 4 * f:4 * f + 4, :].rearrange("p s g h -> p g s h")
                A(dst, ps[:, 4 + f, :].rearrange("p (g s h) -> p g s h", g=4, s=CH), ACT.Gelu_apprx_tanh).then_inc(s["y_cp"], 1)
            for f in range(4):
                act.wait_ge(s["g_ps"], f + 1)
                mt, half = divmod(f, 2)
                if f >= 2:
                    act.wait_ge(s["g_y"], f - 1)
                A(sg[f % 2], ps[:, 4 + f, :], ACT.Sigmoid, bias=m.b_glu[:, mt:mt + 1]).then_inc(s["g_sg"], 1)
                act.wait_ge(s["g_y"], f + 1)
                A(m.br_hi[:, 4 + mt, half * BANK:(half + 1) * BANK], y_out(f), ACT.Copy).then_inc(s["g_hi"], 1)

        @block.tensor
        def _(pe):
            I = m.ident
            pe.wait_ge(s["step_b"], 1)
            pe.wait_ge(s["r_in"], 48)
            for i in range(3):
                tr = nc.tensor.transpose(ps[:, 7, i * J:(i + 1) * J], rows[0:J, i * P:(i + 1) * P], I[0:J, 0:J])
            tr.then_inc(s["row_t"], 1)
            pe.wait_ge(s["c_in"], 16 * 4 * J)
            nc.tensor.transpose(ps[:, 6, 0:P], crow[0], I[:])
            nc.tensor.transpose(ps[:, 6, P:2 * P], crow[1], I[:]).then_inc(s["row_t"], 1)
            pe.wait_ge(s["u_in"], 16)
            for g in range(GR):
                tr = nc.tensor.transpose(ps[:, g // 4, (g % 4) * P:(g % 4 + 1) * P], u[:, g].rearrange("p s h -> p (s h)"), I[:])
                if g % 4 == 3:
                    tr.then_inc(s["u_ps"], 1)
            pe.wait_ge(s["w_rdy"], 1)
            for n in range(2 * J):
                i, j = divmod(n, J)
                tr = nc.tensor.transpose(ps[:, 4 + n // 4, (n % 4) * P:(n % 4 + 1) * P], w[i][:, j].rearrange("p s h -> p (s h)"), I[:])
                if n % 4 == 3:
                    tr.then_inc(s["w_ps"], 1)
            pe.wait_ge(s["u_cp"], 4)
            pe.wait_ge(s["b_rdy"], 1)
            pe.wait_ge(s["w_cp"], 4)
            for g in range(GR):
                j, g2 = divmod(g, 2)
                o = ps[:, g // 4, (g % 4) * P:(g % 4 + 1) * P]
                nc.tensor.matmul(o, b_rep[0][:, j].rearrange("p s h -> p (s h)"), m_re[:, j, g2, 0:8, :].rearrange("p k h -> p (k h)"), start=True, stop=False)
                mm = nc.tensor.matmul(o, b_rep[1][:, j].rearrange("p s h -> p (s h)"), m_im[:, j, g2, 0:8, :].rearrange("p k h -> p (k h)"), start=False, stop=True)
                if g % 4 == 3:
                    mm.then_inc(s["k_ps"], 1)
            for i in range(2):
                for j in range(J):
                    for g2 in range(2):
                        mm = nc.tensor.matmul(ps[g2 * ST:(g2 + 1) * ST, 4 + 2 * i + j // 4, (j % 4) * P:(j % 4 + 1) * P],
                                              w_t[i][:, j, g2 * ST:(g2 + 1) * ST], u_t[:, 2 * j + g2, :], start=True, stop=True)
                mm.then_inc(s["x_ps"], 1)
            pe.wait_ge(s["toep_in"], 16 * CH)
            pe.wait_ge(s["s_rdy"], 1)
            for g in range(GR):
                j, g2 = divmod(g, 2)
                o = ps[:, 4 + g // 4, (g % 4) * P:(g % 4 + 1) * P]
                nc.tensor.matmul(o, u_t[:, g, :], toep[:, g, :], start=True, stop=False)
                nc.tensor.matmul(o, s_prev[0][:, j, :], m_re[:, j, g2, 1:9, :].rearrange("p k h -> p (k h)"), start=False, stop=False)
                mm = nc.tensor.matmul(o, s_prev[1][:, j, :], m_im[:, j, g2, 1:9, :].rearrange("p k h -> p (k h)"), start=False, stop=True)
                if g % 4 == 3:
                    mm.then_inc(s["y_ps"], 1)
            pe.wait_ge(s["y_cp"], 4)
            for f in range(4):
                mt, half = divmod(f, 2)
                for q in range(4):
                    st = 4 * half + q
                    tr = nc.tensor.transpose(ps[:, f, q * P:(q + 1) * P], y[:, st, 8 * mt:8 * mt + 8, :].rearrange("p g h -> p (g h)"), I[:])
                tr.then_inc(s["yt_ps"], 1)
            pe.wait_ge(s["yt_cp"], 4)
            pe.wait_ge(s["glu_in"], 16)
            for f in range(4):
                mt, half = divmod(f, 2)
                for k in range(2):
                    rhs = y_t[:, k].rearrange("p c s -> p (c s)")[:, half * BANK:(half + 1) * BANK]
                    mm = nc.tensor.matmul(ps[:, 4 + f, :], w_glu[:, k, mt * P:(mt + 1) * P], rhs, start=(k == 0), stop=(k == 1))
                mm.then_inc(s["g_ps"], 1)

        @block.vector
        def _(dve):
            step = m.dve_step.on(dve)
            V = nc.vector
            TTo, TS, STT = V.tensor_tensor, V.tensor_scalar, V.scalar_tensor_tensor
            dve.wait_ge(s["r_in"], 48)
            V.tensor_copy(rows[0:J, 2 * P:3 * P].rearrange("j (g p) -> j g p", g=2),
                          stp[0:J, 0:2].unsqueeze(2).to_broadcast([J, 2, ST])).then_inc(s["step_b"], 1)
            dve.wait_ge(s["row_t"], 1)
            for i, dst in enumerate((lre, lim, stp)):
                V.tensor_copy(dst, ps[:, 7, i * J:(i + 1) * J]).then_inc(s["row_c"], 1)
            dve.wait_ge(s["row_c"], 3)
            dve.wait_ge(s["row_t"], 2)
            for i in range(2):
                step(V.tensor_copy(cc[i].rearrange("p j h -> p (j h)"), ps[:, 6, i * P:(i + 1) * P]))
            dve.wait_ge(s["cst"], 4)
            step(V.tensor_copy(ki, ki.bitcast(I32)))
            step(V.tensor_copy(cidx_keep, cidx.bitcast(I32)))
            dve.wait_ge(s["exp1"], 1)
            step(TTo(a1, lre, stp, ALU.mult))
            step(TTo(th, lim, stp, ALU.mult))
            step(reduced(nc, step, th, tt, ta))
            kb = ki.unsqueeze(1).to_broadcast([P, J, 9])
            step(TTo(a9, kb, a1.unsqueeze(2).to_broadcast([P, J, 9]), ALU.mult))
            step(TTo(p9, kb, th.unsqueeze(2).to_broadcast([P, J, 9]), ALU.mult))
            reduced(nc, step, p9, e9, t9).then_inc(s["ang9"], 1)
            dve.wait_ge(s["ang9"], 1)
            V.tensor_copy(t8, p9[:, :, 8]).then_inc(s["ang9"], 1)
            dve.wait_ge(s["sc9"], 3)
            step(TTo(l_re, l_re, e9, ALU.mult))
            step(TTo(l_im, l_im, e9, ALU.mult))
            step(TTo(den, lre, lre, ALU.mult))
            step(TTo(tt, lim, lim, ALU.mult))
            step(TTo(den, den, tt, ALU.add))
            step(V.reciprocal(den, den))
            step(TS(ta, l_re[:, :, 1], -1.0, None, ALU.add))
            step(TTo(q_re, ta, lre, ALU.mult))
            step(TTo(tt, l_im[:, :, 1], lim, ALU.mult))
            step(TTo(q_re, q_re, tt, ALU.add))
            step(TTo(q_re, q_re, den, ALU.mult))
            step(TTo(q_im, l_im[:, :, 1], lre, ALU.mult))
            step(TTo(tt, ta, lim, ALU.mult))
            step(TTo(q_im, q_im, tt, ALU.subtract))
            step(TTo(q_im, q_im, den, ALU.mult))
            dve.wait_ge(s["p_in"], 80)

            def cmul(o_re, o_im, xr, xi, yr, yi, t0, t1, neg_im=False):
                step(TTo(t0, xr, yr, ALU.mult))
                step(TTo(t1, xi, yi, ALU.mult))
                step(TTo(o_re, t0, t1, ALU.subtract))
                step(TTo(t0, xr, yi, ALU.mult))
                step(TTo(t1, xi, yr, ALU.mult))
                if neg_im:
                    step(STT(out=o_im, in0=t0, scalar=-1.0, in1=t1, op0=ALU.mult, op1=ALU.subtract))
                else:
                    step(TTo(o_im, t0, t1, ALU.add))

            def over(a, n):
                return a.unsqueeze(2).to_broadcast([P, J, n])
            cmul(bb[0], bb[1], over(q_re, GC), over(q_im, GC), b[0], b[1], pq[0], pq[1])
            nine = [J, 9, GC]
            t0, t1 = cols(m.F, 10752, J, 9, GC), cols(m.F, 11904, J, 9, GC)
            lr, li = (a.unsqueeze(3).to_broadcast([P] + nine) for a in (l_re, l_im))
            cr, ci = (a.unsqueeze(2).to_broadcast([P] + nine) for a in cc)
            step(TTo(t0, lr, cr, ALU.mult))
            step(TTo(t1, li, ci, ALU.mult))
            for g2 in range(2):
                r = slice(g2 * ST, (g2 + 1) * ST)
                step(TTo(m_re[r, :, g2], t0[r], t1[r], ALU.subtract))
            step(TTo(t0, lr, ci, ALU.mult))
            step(TTo(t1, li, cr, ALU.mult))
            step(TTo(t0, t0, t1, ALU.add))
            for g2 in range(2):
                r = slice(g2 * ST, (g2 + 1) * ST)
                ins = TS(m_im[r, :, g2], t0[r], -1.0, None, ALU.mult)
                step(ins) if g2 == 0 else ins.then_inc(s["b_rdy"], 1)
            four = [P, J, CH, GC]
            lr, li = (a[:, :, 0:CH].unsqueeze(3).to_broadcast(four) for a in (l_re, l_im))
            br, bi = (a.unsqueeze(2).to_broadcast(four) for a in bb)
            cmul(w[0], w[1], lr, li, br, bi, b_rep[0], b_rep[1])
            step(V.tensor_copy(b_rep[0], br))
            V.tensor_copy(b_rep[1], bi).then_inc(s["w_rdy"], 1)
            step(V.tensor_reduce(mask16, m.ident[:].rearrange("p (a h) -> p h a", h=GC), AX.X, ALU.add))
            dmat = m.vecs[:, 0:GR * GC].rearrange("p (g h) -> p g h", h=GC)
            dve.wait_ge(s["b_rdy"], 1)
            step(TTo(dmat, d_row, mask16.unsqueeze(1).to_broadcast([P, GR, GC]), ALU.mult))
            dve.wait_ge(s["w_ps"], 4)
            V.memset(toep, 0.0).then_inc(s["zero"], 1)
            for f in range(4):
                dve.wait_ge(s["k_ps"], f + 1)
                o = kk[:, 4 * f:4 * f + 4, :]
                src = ps[:, f, :].rearrange("p (g n) -> p g n", g=4)
                step(V.tensor_copy(o[:, :, GC:], src[:, :, GC:]))
                TTo(o[:, :, 0:GC], src[:, :, 0:GC], dmat[:, 4 * f:4 * f + 4, :], ALU.add).then_inc(s["k_cp"], 1)
            step(TTo(tab[1], t8.unsqueeze(2).to_broadcast([P, J, NCH]), cidx_keep.unsqueeze(1).to_broadcast([P, J, NCH]), ALU.mult))
            reduced(nc, step, tab[1], rho, tab[0]).then_inc(s["tab_a"], 1)
            dve.wait_ge(s["tab_a"], 1)
            step(V.tensor_copy(rho, e9[:, :, 8:9].to_broadcast([P, J, NCH])))
            step(V.memset(rho[:, :, 0:1], 0.0))
            dve.wait_ge(s["tab_s"], 2)
            dve.wait_ge(s["x_ps"], 2)
            dve.wait_ge(s["toep_in"], 16 * CH)
            x = [ps[:, 4 + 2 * i:6 + 2 * i, :].rearrange("p b (j c) -> p (b j) c", c=NCH) for i in range(2)]
            step(TTo(z_in[0], x[0], tab[0], ALU.mult))
            step(TTo(tmp, x[1], tab[1], ALU.mult))
            step(TTo(z_in[0], z_in[0], tmp, ALU.add))
            step(TTo(z_in[1], x[1], tab[0], ALU.mult))
            step(TTo(tmp, x[0], tab[1], ALU.mult))
            step(TTo(z_in[1], z_in[1], tmp, ALU.subtract))
            for i in range(2):
                flat = (a.rearrange("p j c -> p (j c)") for a in (z[i], rho, z_in[i]))
                o, d0, d1 = flat
                step(V.tensor_tensor_scan(o, d0, d1, 0.0, ALU.mult, ALU.add))
            n1 = NCH - 1
            zc = [a[:, :, 0:n1] for a in z]
            cs, sn = tab[0][:, :, 0:n1], tab[1][:, :, 0:n1]
            o_re, o_im = (a[:, :, 1:] for a in s_prev)
            step(V.memset(s_prev[0][:, :, 0:1], 0.0))
            step(V.memset(s_prev[1][:, :, 0:1], 0.0))
            step(TTo(o_re, zc[0], cs, ALU.mult))
            step(TTo(tmp[:, :, 0:n1], zc[1], sn, ALU.mult))
            step(TTo(o_re, o_re, tmp[:, :, 0:n1], ALU.subtract))
            step(TTo(o_im, zc[0], sn, ALU.mult))
            step(TTo(tmp[:, :, 0:n1], zc[1], cs, ALU.mult))
            TTo(o_im, o_im, tmp[:, :, 0:n1], ALU.add).then_inc(s["s_rdy"], 1)
            for f in range(4):
                mt, half = divmod(f, 2)
                dve.wait_ge(s["yt_ps"], f + 1)
                V.tensor_copy(y_t[:, mt, :, 4 * half:4 * half + 4].rearrange("p c s -> p s c"),
                              ps[:, f, :].rearrange("p (s c) -> p s c", s=4)).then_inc(s["yt_cp"], 1)
            dve.wait_ge(s["yt_cp"], 4)
            for f in range(4):
                mt, half = divmod(f, 2)
                cut = slice(half * BANK, (half + 1) * BANK)
                dve.wait_ge(s["g_sg"], f + 1)
                TTo(y_out(f), y_t[:, mt].rearrange("p c s -> p (c s)")[:, cut], sg[f % 2], ALU.mult).then_inc(s["g_y"], 1)
                dve.wait_ge(s["g_hi"], f + 1)
                TTo(m.br_lo[:, 4 + mt, cut], y_out(f), f32(m.br_hi[:, 4 + mt, cut]), ALU.subtract).then_inc(s["g_lo"], 1)


def after(eng, sem, value):
    if isinstance(value, int) and value <= 0:
        return
    eng.wait_ge(sem, value)


def looped(eng, first, last, body):
    body(0)
    with eng.Fori(first, last) as i:
        body(i)


def stage_combine_out(m):
    nc, ps = m.nc, m.ps
    NB = 3
    UNITS = 2 * NB
    ITERS = KD // 2
    ALL = ITERS * UNITS
    A0, A1 = 2 * KD * T, 2 * KD * T + 12 * T
    rows = cols(m.F, 0, TT, D)
    gate = [cols(m.F, i * T, T) for i in range(UNITS)]
    raw = [cols(m.F, 10240 + i * 2 * P, 2, P) for i in range(2)]
    part = [cols(m.F, 10752 + i * T, T) for i in range(NB)]
    total = [cols(m.F, 13824 + i * T, T) for i in range(2)]
    wo_raw = [cols(m.F, at, D) for at in (15872, 16896, 10752, 11776, 12800)]
    slot = (0, 1, 0, 1, 2, 3, 4, 0)
    freed_by = (None, None, 1, 2, None, None, None, 3)
    wo_hi = [cols(m.R, A1 + 2 * k * D if k < 2 else A0 + 2 * (k - 2) * D, D) for k in range(KD)]
    wo_lo = [cols(m.R, (A1 + 2 * k * D if k < 2 else A0 + 2 * (k - 2) * D) + D, D) for k in range(KD)]
    w_hi = [cols(m.R, A1 + 4 * D + 2 * i * 2 * P, 2, P) for i in range(2)]
    w_lo = [cols(m.R, A1 + 4 * D + (2 * i + 1) * 2 * P, 2, P) for i in range(2)]
    scaled_to = cols(m.F, TT * D, TT, D)
    nrm = NormAndTurn(m, "ffnn", m.g_ffn, lambda i: scaled_to[:, i, :], scaled_to)
    w_in = [m.sem(f"branch_w_in{i}") for i in range(2)]
    gate_in = [m.sem(f"gate_in{i}") for i in range(UNITS)]
    wo_in = [m.sem(f"out_w_in{k}") for k in range(KD)]
    hi_done, lo_done, proj_mm, sig_done, mul_done, add_done, sum_done, mg_hi, mg_lo = (
        m.sem(f"gates_{n}") for n in ("w_hi", "w_lo", "proj", "sigmoid", "mul", "add", "sum", "merged_hi", "merged_lo"))
    wo_hi_done, wo_lo_done, out_mm, x_add, x_in = (m.sem(f"out_{n}") for n in ("w_hi", "w_lo", "mm", "add", "x_in"))
    branch_src = m.ins["w_branch"][0].rearrange("b (k p) n -> b p k n", p=P)
    gate_src = m.scr_gate.rearrange("(d n) p t -> n p d t", n=NB)
    proj_ps = [ps[:, 2 * i:2 * i + 2, :].rearrange("p b n -> p (b n)") for i in range(2)]

    def tile_of(it, u):
        return it * 2 + u // NB, u % NB

    with nc.Block() as block:
        @block.sync
        def _(sp):
            def body(it):
                for u in range(UNITS):
                    d, n = tile_of(it, u)
                    after(sp, mul_done, it * UNITS + u - (UNITS - 1))
                    sp.dma_start(gate[u], gate_src[n][:, bass.ds(d, 1), :].rearrange("p a t -> p (a t)")).then_inc(gate_in[u], 16)
                    after(sp, lo_done, it * UNITS + u - 1)
                    sp.dma_start(raw[u % 2], branch_src[n][:, :, bass.ds(d * P, P)]).then_inc(w_in[u % 2], 16)
                    if isinstance(it, int) and u == 1:
                        for k in range(2):
                            sp.dma_start(wo_raw[slot[k]], m.ins["w_out"][0, k * P:(k + 1) * P, :]).then_inc(wo_in[k], 16)
            looped(sp, 1, ITERS, body)
            sp.wait_ge(mul_done, ALL)
            sp.dma_start(rows, m.ins["x"][0].rearrange("(i p) d -> p i d", p=P)).then_inc(x_in, 16)
            for k in range(2, KD):
                if freed_by[k]:
                    sp.wait_ge(wo_lo_done, freed_by[k])
                if k == 4:
                    sp.wait_ge(sum_done, KD)
                sp.dma_start(wo_raw[slot[k]], m.ins["w_out"][0, k * P:(k + 1) * P, :]).then_inc(wo_in[k], 16)

        @block.scalar
        def _(act):
            def split(it, u):
                if u >= UNITS:
                    it, u = it + 1, u - UNITS
                after(act, w_in[u % 2], (it * (UNITS // 2) + u // 2 + 1) * 16)
                after(act, proj_mm, it * UNITS + u - 1)
                nc.scalar.activation(w_hi[u % 2], raw[u % 2], ACT.Copy).then_inc(hi_done, 1)

            def merged_hi(d, u):
                after(act, sum_done, d + 1)
                nc.scalar.activation(m.R[:, bass.ds(d * T, T)], total[u // NB % 2], ACT.Copy).then_inc(mg_hi, 1)

            def body(it, first=False, last=False):
                for u in range(UNITS):
                    if not (last and u == UNITS - 1):
                        split(it, u + 1)
                    d, n = tile_of(it, u)
                    after(act, gate_in[u], it * 16 + 16)
                    nc.scalar.activation(gate[u], gate[u], ACT.Sigmoid).then_inc(sig_done, 1)
                    if n == 0 and not (first and u == 0):
                        merged_hi(d - 1, u + NB)
            split(0, 0)
            body(0, first=True)
            with act.Fori(1, ITERS - 1) as it:
                body(it)
            body(ITERS - 1, last=True)

            def out_split(k):
                act.wait_ge(wo_in[k], 16)
                nc.scalar.activation(wo_hi[k], wo_raw[slot[k]], ACT.Copy).then_inc(wo_hi_done, 1)
            out_split(0), out_split(1)
            merged_hi(KD - 1, NB)
            act.wait_ge(proj_mm, ALL)
            for k in range(2, KD):
                out_split(k)
            for i in range(TT):
                act.wait_ge(x_add, 2 * i + 2)
                nrm.square(act, i)
            nrm.hi(act, 0)
            nrm.hi(act, 1)

        @block.vector
        def _(dve):
            def split(it, u):
                if u >= UNITS:
                    it, u = it + 1, u - UNITS
                after(dve, hi_done, it * UNITS + u + 1)
                nc.vector.tensor_tensor(w_lo[u % 2], raw[u % 2], f32(w_hi[u % 2]), ALU.subtract).then_inc(lo_done, 1)

            def sum_up(d, u):
                after(dve, add_done, d + 1)
                after(dve, mul_done, d * NB + NB)
                nc.vector.tensor_tensor(total[u // NB % 2], part[0], part[2], ALU.add).then_inc(sum_done, 1)
                after(dve, sum_done, d + 1)

            def merged_lo(d, u):
                after(dve, mg_hi, d + 1)
                nc.vector.tensor_tensor(m.R[:, bass.ds(d * T + KD * T, T)], total[u // NB % 2], f32(m.R[:, bass.ds(d * T, T)]),
                                        ALU.subtract).then_inc(mg_lo, 1)

            def body(it, first=False, last=False):
                for u in range(UNITS):
                    d, n = tile_of(it, u)
                    if n == 0 and not (first and u == 0):
                        sum_up(d - 1, u + NB)
                    if not (last and u == UNITS - 1):
                        split(it, u + 1)
                    after(dve, proj_mm, it * UNITS + u + 1)
                    after(dve, sig_done, it * UNITS + u + 1)
                    nc.vector.tensor_tensor(part[n], proj_ps[u % 2], gate[u], ALU.mult).then_inc(mul_done, 1)
                    if n == 1 and not (first and u == 1):
                        merged_lo(d - 1, u + NB)
            split(0, 0)
            body(0, first=True)
            with dve.Fori(1, ITERS - 1) as it:
                body(it)
            body(ITERS - 1, last=True)

            def out_split(k):
                dve.wait_ge(wo_hi_done, k + 1)
                nc.vector.tensor_tensor(wo_lo[k], wo_raw[slot[k]], f32(wo_hi[k]), ALU.subtract).then_inc(wo_lo_done, 1)
            out_split(0), out_split(1)
            sum_up(KD - 1, NB)
            merged_lo(KD - 1, NB)
            for k in range(2, KD):
                out_split(k)
            dve.wait_ge(x_in, 16)
            for t in range(TT):
                for half in range(2):
                    n = 2 * t + half
                    dve.wait_ge(out_mm, n + 1)
                    r = rows[:, t, half * BANK:(half + 1) * BANK]
                    nc.vector.tensor_tensor(r, ps[:, n % 8, :], r, ALU.add).then_inc(x_add, 1)
                nrm.mean(dve, t)
                if t:
                    nrm.scale(dve, t - 1)
            nrm.scale(dve, TT - 1)
            nrm.lo(dve, 0)
            nrm.lo(dve, 1)

        @block.gpsimd
        def _(pool):
            def body(it):
                for u in (1, NB + 1):
                    after(pool, mul_done, it * UNITS + u + 1)
                    nc.gpsimd.tensor_tensor(part[0], part[0], part[1], ALU.add).then_inc(add_done, 1)
            looped(pool, 1, ITERS, body)
            nrm.powers(pool)

        @block.tensor
        def _(pe):
            def body(it):
                for u in range(UNITS):
                    n = u % NB
                    hi, lo = w_hi[u % 2], w_lo[u % 2]
                    after(pe, lo_done, it * UNITS + u + 1)
                    after(pe, mul_done, it * UNITS + u - 1)
                    for k in range(2):
                        for w, src in ((hi, m.br_hi), (hi, m.br_lo), (lo, m.br_hi)):
                            for half in range(2):
                                cut = slice(half * BANK, (half + 1) * BANK)
                                mm = nc.tensor.matmul(proj_ps[u % 2][:, cut], w[:, k, :], src[:, 2 * n + k, cut], start=(k == 0 and w is hi and src is m.br_hi),
                                                      stop=(k == 1 and w is lo), skip_group_check=True)
                    mm.then_inc(proj_mm, 1)
            looped(pe, 1, ITERS, body)

            def out_product(n, k):
                t, half = divmod(n, 2)
                o, cut = ps[:, n % 8, :], slice(half * BANK, (half + 1) * BANK)
                hi, lo = (a[:, k, t * P:(t + 1) * P] for a in (m.h_hi, m.h_lo))
                nc.tensor.matmul(o, hi, wo_hi[k][:, cut], start=(k == 0), stop=False)
                nc.tensor.matmul(o, hi, wo_lo[k][:, cut], start=False, stop=False)
                mm = nc.tensor.matmul(o, lo, wo_hi[k][:, cut], start=False, stop=(k == KD - 1))
                if k == KD - 1:
                    mm.then_inc(out_mm, 1)
            pe.wait_ge(mul_done, ALL)
            for k in range(KD):
                pe.wait_ge(mg_lo, k + 1)
                pe.wait_ge(wo_lo_done, k + 1)
                for n in range(8):
                    out_product(n, k)
            for n in range(8, 2 * TT):
                pe.wait_ge(x_add, n - 7)
                for k in range(KD):
                    out_product(n, k)
            pe.wait_ge(x_add, 2 * TT - 4)
            nrm.turn(pe, 0)
            nrm.turn(pe, 1)


def stage_ffn(m):
    nc, ps = m.nc, m.ps
    FT = FF // P
    GROUPS = FT // 2
    rows = cols(m.F, 0, TT, D)
    raw = [cols(m.F, 8192 + i * T, KD, P) for i in range(4)]
    wd_raw = [cols(m.F, 12288 + i * D, D) for i in range(2)]
    conv = [cols(m.F, 14336 + i * T, T) for i in range(2)]
    gated = cols(m.F, 16384, T)
    W0 = 2 * KD * T
    w_hi = [cols(m.R, W0 + 2 * i * T, KD, P) for i in range(4)]
    w_lo = [cols(m.R, W0 + (2 * i + 1) * T, KD, P) for i in range(4)]
    a_hi, a_lo = cols(m.R, W0 + 8 * T, 2, T), cols(m.R, W0 + 10 * T, 2, T)
    d_hi, d_lo = cols(m.R, W0 + 12 * T, 2, D), cols(m.R, W0 + 14 * T, 2, D)
    w_in = [m.sem(f"up_in{i}") for i in range(4)]
    wd_in = [m.sem(f"down_in{i}") for i in range(2)]
    (hi_done, lo_done, up_mm, scaled, conv_mid, conv_done, silu_done, gated_done, a_hi_done, a_lo_done, d_hi_done, d_lo_done,
     down_mm, add_done, stored) = (m.sem(f"ffn_{n}") for n in (
         "w_hi", "w_lo", "up", "scaled", "conv_mid", "conv", "silu", "gated", "a_hi", "a_lo", "d_hi", "d_lo", "down", "add", "stored"))
    up_src = m.ins["w_up"][0].rearrange("(k p) n -> p k n", p=P)
    ups = [ps[:, 2 * i:2 * i + 2, :].rearrange("p b n -> p (b n)") for i in range(2)]
    ND = 2 * TT

    def feature(it, n):
        return it * (2 * P) + ((n // 2) * P + (n % 2) * FF)

    with nc.Block() as block:
        @block.sync
        def _(sp):
            def body(it):
                for n in range(4):
                    after(sp, lo_done, it * 4 + n - 3)
                    sp.dma_start(raw[n], up_src[:, :, bass.ds(feature(it, n), P)]).then_inc(w_in[n], 16)
                    if n % 2 == 1:
                        f = n // 2
                        after(sp, d_lo_done, it * 2 + f - 1)
                        sp.dma_start(wd_raw[f], m.ins["w_down"][0][bass.ds(it * (2 * P) + f * P, P), :]).then_inc(wd_in[f], 16)
            looped(sp, 1, GROUPS, body)
            for t in range(TT):
                sp.wait_ge(add_done, GROUPS * ND + 2 * t + 2)
                sp.dma_start(m.ins["out"][0, t * P:(t + 1) * P, :], rows[:, t, :]).then_inc(stored, 16)
            sp.wait_ge(stored, 16 * TT)

        def ahead(it, n, by=2):
            return (it, n + by) if n + by < 4 else (it + 1, n + by - 4)

        @block.scalar
        def _(act):
            def split(it, n):
                after(act, w_in[n], it * 16 + 16)
                after(act, up_mm, it * 4 + n - 3)
                nc.scalar.activation(w_hi[n], raw[n], ACT.Copy).then_inc(hi_done, 1)

            def body(it, last=False):
                for n in range(4):
                    f = n // 2
                    if not (last and n >= 2):
                        split(*ahead(it, n))
                    after(act, up_mm, it * 4 + n + 1)
                    after(act, gated_done, it * 2 + f)
                    nc.scalar.activation(conv[n % 2], ups[n % 2], ACT.Copy,
                                         scale=m.colv[:, bass.ds(2 * 44 + it * 2 + f + (n % 2) * FT, 1)]).then_inc(scaled, 1)
                    if n % 2 == 1:
                        after(act, conv_done, it * 4 + n)
                        nc.scalar.activation(conv[0], conv[0], ACT.Silu).then_inc(silu_done, 1)
                        after(act, wd_in[f], it * 16 + 16)
                        after(act, down_mm, it * ND)
                        nc.scalar.activation(d_hi[:, f, :], wd_raw[f], ACT.Copy).then_inc(d_hi_done, 1)
                        after(act, gated_done, it * 2 + f + 1)
                        nc.scalar.activation(a_hi[:, f, :], gated, ACT.Copy).then_inc(a_hi_done, 1)
            split(0, 0)
            split(0, 1)
            body(0)
            with act.Fori(1, GROUPS - 1) as it:
                body(it)
            body(GROUPS - 1, last=True)

        @block.vector
        def _(dve):
            V = nc.vector

            def split(it, n):
                after(dve, hi_done, it * 4 + n + 1)
                V.tensor_tensor(w_lo[n], raw[n], f32(w_hi[n]), ALU.subtract).then_inc(lo_done, 1)

            def adds(it):
                for n in range(ND):
                    t, half = divmod(n, 2)
                    after(dve, down_mm, it * ND + n + 1)
                    r = rows[:, t, half * BANK:(half + 1) * BANK]
                    after(dve, add_done, it * ND + n + 1)
                    V.tensor_tensor(r, ps[:, 4 + n % 4, :], r, ALU.add).then_inc(add_done, 1)

            def body(it, last=False, first=False):
                for n in range(4):
                    f = n // 2
                    if not (last and n >= 2):
                        split(*ahead(it, n))
                    after(dve, scaled, it * 4 + n + 1)
                    up, c = ups[n % 2], conv[n % 2]
                    V.scalar_tensor_tensor(out=c[:, 1:], in0=up[:, 0:T - 1], scalar=m.colv[:, bass.ds(44 + it * 2 + f + (n % 2) * FT, 1)],
                                           in1=c[:, 1:], op0=ALU.mult, op1=ALU.add).then_inc(conv_mid, 1)
                    after(dve, conv_mid, it * 4 + n + 1)
                    V.scalar_tensor_tensor(out=c[:, 2:], in0=up[:, 0:T - 2], scalar=m.colv[:, bass.ds(it * 2 + f + (n % 2) * FT, 1)],
                                           in1=c[:, 2:], op0=ALU.mult, op1=ALU.add).then_inc(conv_done, 1)
                    if n == 0 and not first:
                        adds(it - 1)
                    if n % 2 == 1:
                        after(dve, silu_done, it * 2 + f + 1)
                        after(dve, conv_done, it * 4 + n + 1)
                        after(dve, a_lo_done, it * 2 + f)
                        V.tensor_tensor(gated, conv[0], conv[1], ALU.mult).then_inc(gated_done, 1)
                        after(dve, d_hi_done, it * 2 + f + 1)
                        V.tensor_tensor(d_lo[:, f, :], wd_raw[f], f32(d_hi[:, f, :]), ALU.subtract).then_inc(d_lo_done, 1)
                        after(dve, a_hi_done, it * 2 + f + 1)
                        V.tensor_tensor(a_lo[:, f, :], gated, f32(a_hi[:, f, :]), ALU.subtract).then_inc(a_lo_done, 1)
            dve.sem_inc(add_done, ND)
            split(0, 0)
            split(0, 1)
            body(0, first=True)
            with dve.Fori(1, GROUPS - 1) as it:
                body(it)
            body(GROUPS - 1, last=True)
            adds(GROUPS - 1)

        @block.tensor
        def _(pe):
            def up(it, n):
                after(pe, lo_done, it * 4 + n + 1)
                after(pe, conv_done, it * 4 + n - 1)
                for k in range(KD):
                    for w, src in ((w_hi[n], m.h_hi), (w_hi[n], m.h_lo), (w_lo[n], m.h_hi)):
                        for half in range(2):
                            cut = slice(half * BANK, (half + 1) * BANK)
                            mm = nc.tensor.matmul(ups[n % 2][:, cut], w[:, k, :], src[:, k, cut], start=(k == 0 and w is w_hi[n] and src is m.h_hi),
                                                  stop=(k == KD - 1 and w is w_lo[n]), skip_group_check=True)
                mm.then_inc(up_mm, 1)

            def down(it):
                after(pe, a_lo_done, it * 2 + 2)
                after(pe, d_lo_done, it * 2 + 2)
                for n in range(ND):
                    t, half = divmod(n, 2)
                    after(pe, add_done, it * ND + ND + n - 3)
                    cut = slice(half * BANK, (half + 1) * BANK)
                    for f in range(2):
                        hi, lo = (a[:, f, t * P:(t + 1) * P] for a in (a_hi, a_lo))
                        o = ps[:, 4 + n % 4, :]
                        nc.tensor.matmul(o, hi, d_hi[:, f, cut], start=(f == 0), stop=False)
                        nc.tensor.matmul(o, hi, d_lo[:, f, cut], start=False, stop=False)
                        mm = nc.tensor.matmul(o, lo, d_hi[:, f, cut], start=False, stop=(f == 1))
                    mm.then_inc(down_mm, 1)

            def body(it, first=False):
                up(it, 0)
                if not first:
                    down(it - 1)
                for n in range(1, 4):
                    up(it, n)
            body(0, first=True)
            with pe.Fori(1, GROUPS) as it:
                body(it)
            down(GROUPS - 1)


def hybrid_trunk(nc, ins):
    with ExitStack() as ctx:
        m = setup(nc, ctx, ins)
        stage_load_norm_project(m)
        stage_fox(m)
        stage_mla(m)
        stage_s5(m)
        reuse_semaphores(m)
        stage_combine_out(m)
        stage_ffn(m)


_INS = ["x", "positions", "attn_norm_g", "w_in", "q_lat_norm_g", "w_uq", "kv_lat_norm_g", "w_ukv", "mla_q_norm_g", "mla_k_norm_g",
        "fox_q_norm_g", "fox_k_norm_g", "fox_f_bias", "s5_lambda_re", "s5_lambda_im", "s5_b_re", "s5_b_im", "s5_c_re", "s5_c_im",
        "s5_d", "s5_log_step", "s5_w_glu", "s5_b_glu", "w_branch", "w_out", "ffn_norm_g", "w_up", "ffn_conv_w", "w_down"]


def kernel(**inputs):
    import concourse.bacc as _bacc
    from concourse.bass_utils import run_bass_kernel_spmd as _run

    nc = _bacc.Bacc("TRN2", target_bir_lowering=False, num_devices=1)
    arrays, args = {}, {}
    for name in _INS:
        a = np.ascontiguousarray(inputs[name])
        arrays[f"in_{name}"] = a
        args[name] = nc.dram_tensor(f"in_{name}", a.shape, mybir.dt.from_np(a.dtype), kind="ExternalInput").ap()
    args["out"] = nc.dram_tensor("out_x", (1, T, D), F32, kind="ExternalOutput").ap()
    hybrid_trunk(nc, args)
    r = _run(nc, [arrays], core_ids=[0])
    return r.results[0]["out_x"]
```

```python
from contextlib import ExitStack
import math
import numpy as np

import concourse.bass as bass
from concourse import mybir

F32 = mybir.dt.float32
F32R = mybir.dt.float32r
BF16 = mybir.dt.bfloat16
I32 = mybir.dt.int32
ALU = mybir.AluOpType
ACT = mybir.ActivationFunctionType
AX = mybir.AxisListType

P = 128
T, D, KD = 1024, 1024, 8
TT = T // P
BANK = 512
Q_RANK, KV_RANK = 384, 256
H, NOPE, ROPE = 4, 64, 32
QK = NOPE + ROPE
VD = 64
FH, FD = 4, 64
GR, GC, ST = 16, 16, 64
CH = 8
NCH = T // CH
FF, CONV = 2816, 3
EPS = 1e-6
NEG = -1e30
C_Q, C_KV, C_KR = 0, Q_RANK, Q_RANK + KV_RANK
C_FQ = C_KR + ROPE
C_FK, C_FV = C_FQ + 256, C_FQ + 512
C_F = C_FQ + 768
C_U = C_F + FH
C_G = C_U + 256

RW = 128 * 256
FW = 74 * 256


class Chain:

    def __init__(self, sem):
        self.sem, self.n = sem, 0

    def on(self, eng, base=None):
        self.eng, self.base = eng, base
        return self

    def __call__(self, ins):
        ins.then_inc(self.sem, 1)
        self.n += 1
        self.eng.wait_ge(self.sem, self.n if self.base is None else self.base + self.n)
        return ins


class Memory:
    pass


class Programs:

    def __init__(self, scalar, vector, tensor, gpsimd=None, sync=None, done=None):
        self.scalar, self.vector, self.tensor = scalar, vector, tensor
        self.gpsimd, self.sync, self.done = gpsimd, sync, done


def cols(tensor, off, *dims):
    n = math.prod(dims)
    ap = tensor[:, off:off + n]
    if len(dims) == 1:
        return ap
    names = "abcd"[:len(dims)]
    return ap.rearrange(f"p ({' '.join(names)}) -> p {' '.join(names)}",
                        **{k: v for k, v in zip(names[1:], dims[1:])})


def setup(nc, ctx, ins):
    m = Memory()
    m.nc, m.ctx, m.ins = nc, ctx, ins
    m.sb = lambda name, shape, dt=F32: ctx.enter_context(nc.sbuf_tensor(name, shape, dt))
    m.scope, m.held = ctx.enter_context(ExitStack()), []

    def sem(name):
        m.held.append(m.scope.enter_context(nc.semaphore(name)))
        return m.held[-1]
    m.sem = sem
    m.R = m.sb("split_arena", [P, RW], F32R)
    m.F = m.sb("plain_arena", [P, FW], F32)
    m.ident = m.sb("ident", [P, P])
    m.identb = m.sb("identb", [P, P], BF16)
    m.maskb = m.sb("maskb", [P, P], BF16)
    m.vecs = m.sb("vecs", [P, 3 * P])
    m.colv = m.sb("colv", [P, 160])
    m.conv_w = m.colv[:, 0:132].rearrange("p (j f) -> p j f", j=CONV)
    m.g_attn, m.g_ffn = m.colv[:, 132:140], m.colv[:, 140:148]
    m.g_qlat, m.g_kvlat, m.b_glu = m.colv[:, 148:151], m.colv[:, 151:153], m.colv[:, 153:155]
    m.rowg = m.sb("rowg", [P, 2 * QK + 2 * FD + FH])
    m.stat = m.sb("stat", [P, 64])
    m.statb = m.sb("statb", [P, 64])
    m.cidx = m.sb("cidx", [P, P])
    m.ps = ctx.enter_context(nc.psum_tensor("ps", [P, 8, BANK], F32))
    m.h_hi = cols(m.R, 0, KD, T)
    m.h_lo = cols(m.R, KD * T, KD, T)
    m.dve_step, m.pool_step = (Chain(ctx.enter_context(nc.semaphore(n))) for n in ("dve_step", "pool_step"))
    m.scr_u = nc.dram_tensor("scr_u", (P, 8 * 256), F32, kind="Internal").ap()
    m.scr_gate = nc.dram_tensor("scr_gate", (3 * KD, P, T), F32, kind="Internal").ap()
    m.scr_lat = nc.dram_tensor("scr_lat", (P, TT * 672), F32, kind="Internal").ap()
    return m


def reuse_semaphores(m):
    with m.nc.Block() as block:
        @block.sync
        def _(sp):
            for s in m.held:
                sp.sem_clear(s)
    m.scope.close()
    m.scope, m.held = m.ctx.enter_context(ExitStack()), []


def f32(ap):
    return ap.bitcast(F32)


class NormAndTurn:

    def __init__(self, m, tag, gain, squares_to, scaled_to):
        self.m, self.gain, self.squares_to, self.scaled_to = m, gain, squares_to, scaled_to
        self.rows = cols(m.F, 0, TT, D)
        self.sq_done, self.ms_done, self.rstd_done, self.scaled, self.turned, self.hi_done, self.done = (
            m.sem(f"{tag}_{n}") for n in ("sq", "ms", "rstd", "scaled", "turned", "hi", "lo"))
        self.ssq, self.rstd, self.expo = m.stat[:, 0:TT], m.stat[:, 8:8 + TT], m.stat[:, 16:16 + TT]

    def square(self, act, i):
        self.m.nc.scalar.activation(self.squares_to(i), self.rows[:, i, :], ACT.Square,
                                    accum_out=self.ssq[:, i:i + 1]).then_inc(self.sq_done, 1)
        act.wait_ge(self.sq_done, i + 1)

    def mean(self, dve, i):
        dve.wait_ge(self.sq_done, i + 1)
        self.m.nc.vector.tensor_scalar(self.ssq[:, i:i + 1], self.ssq[:, i:i + 1], 1.0 / D, EPS, ALU.mult, ALU.add).then_inc(self.ms_done, 1)

    def powers(self, pool):
        m = self.m
        m.pool_step.on(pool)
        m.pool_step(m.nc.gpsimd.memset(self.expo, -0.5))
        for i in range(TT):
            pool.wait_ge(self.ms_done, i + 1)
            m.nc.gpsimd.tensor_tensor(self.rstd[:, i:i + 1], self.ssq[:, i:i + 1], self.expo[:, i:i + 1], ALU.pow).then_inc(self.rstd_done, 1)

    def scale(self, dve, i):
        dve.wait_ge(self.rstd_done, i + 1)
        self.m.nc.vector.tensor_scalar(self.scaled_to[:, i, :], self.rows[:, i, :], self.rstd[:, i:i + 1], None, ALU.mult).then_inc(self.scaled, 1)

    def turn(self, pe, fills):
        for n in fills:
            half, k = divmod(n, KD)
            if k == 0:
                pe.wait_ge(self.scaled, 4 * half + 4)
            if n >= 4:
                pe.wait_ge(self.done, n - 3)
            for j in range(4):
                t = self.m.nc.tensor.transpose(self.m.ps[:, n % 4, j * P:(j + 1) * P],
                                               self.scaled_to[:, 4 * half + j, k * P:(k + 1) * P], self.m.ident[:])
            t.then_inc(self.turned, 1)

    def hi(self, act, fills):
        for n in fills:
            half, k = divmod(n, KD)
            act.wait_ge(self.turned, n + 1)
            self.m.nc.scalar.activation(self.m.h_hi[:, k, half * BANK:(half + 1) * BANK], self.m.ps[:, n % 4, :],
                                        ACT.Copy, scale=self.gain[:, k:k + 1]).then_inc(self.hi_done, 1)

    def lo(self, dve, fills):
        for n in fills:
            half, k = divmod(n, KD)
            cut = slice(half * BANK, (half + 1) * BANK)
            dve.wait_ge(self.hi_done, n + 1)
            self.m.nc.vector.scalar_tensor_tensor(out=self.m.h_lo[:, k, cut], in0=self.m.ps[:, n % 4, :], scalar=self.gain[:, k:k + 1],
                                                  in1=f32(self.m.h_hi[:, k, cut]), op0=ALU.mult, op1=ALU.subtract).then_inc(self.done, 1)


def stage_load_norm_project(m):
    nc = m.nc
    vec_in, row_in, vec_turned, vec_done, const = (m.sem(n) for n in ("vec_in", "row_in", "vec_turned", "vec_done", "const"))
    nrm = NormAndTurn(m, "attn", m.g_attn, lambda i: m.ps[:, 6:8, :].rearrange("p a b -> p (a b)"), cols(m.F, 0, TT, D))
    x_in = [m.sem(f"x_in{i}") for i in range(TT)]

    chunks = [(0, 192), (192, 192), (C_KV, 288), (C_FQ, 256), (C_FK, 256), (C_FV, 260), (C_U, 256)]
    NW = 288
    m.lat = cols(m.F, 0, TT, 672)
    m.fqk = cols(m.F, 5376, TT, 512)
    m.fvf = cols(m.F, 5376 + 4096, TT, 260)
    m.u = cols(m.F, 11552, GR, CH, GC)
    raw = [cols(m.F, 13600 + i * 4 * NW, 4, NW) for i in range(2)]
    W0 = 2 * KD * T
    w_hi = [cols(m.R, W0 + i * 2 * KD * NW, KD, NW) for i in range(2)]
    w_lo = [cols(m.R, W0 + (2 * i + 1) * KD * NW, KD, NW) for i in range(2)]
    raw_in = [m.sem(f"pw_in{i}") for i in range(2)]
    w_hi_done, w_lo_done, prod, out_act, out_dve = (m.sem(n) for n in ("pw_hi", "pw_lo", "p_prod", "p_act", "p_dve"))
    spill = m.spill = m.sem("spill")
    w_src = m.ins["w_in"][0].rearrange("(k p) n -> p k n", p=P)

    def dest(c, t):
        first, n = chunks[c]
        if first < C_FQ:
            return m.lat[:, t, first:first + n]
        if first < C_FV:
            return m.fqk[:, t, first - C_FQ:first - C_FQ + n]
        if first == C_FV:
            return m.fvf[:, t, :]
        return m.u[:, :, 7 - t, :]

    def made(n):
        width = chunks[n // TT][1]
        src = m.ps[:, 4 + n % 4, 0:width]
        return src.rearrange("p (g h) -> p g h", h=GC) if chunks[n // TT][0] == C_U else src

    nch = len(chunks)
    m.gate_fill = GateFill(m, GATE_PLAN)
    with nc.Block() as block:
        @block.sync
        def _(sp):
            for i in range(TT):
                sp.dma_start(nrm.rows[:, i, :], m.ins["x"][0, i * P:(i + 1) * P, :]).then_inc(x_in[i], 16)
            at = 0
            for v in (m.ins["mla_q_norm_g"], m.ins["mla_k_norm_g"], m.ins["fox_q_norm_g"], m.ins["fox_k_norm_g"], m.ins["fox_f_bias"]):
                n = v.shape[1]
                sp.dma_start(m.rowg[:, at:at + n], v[0].partition_broadcast(P)).then_inc(row_in, 16)
                at += n
            for c, (first, n) in enumerate(chunks):
                for half in range(2):
                    if c >= 1:
                        sp.wait_ge(w_lo_done, 2 * (c - 1) + half + 1)
                    sp.dma_start(raw[half][:, :, 0:n], w_src[:, 4 * half:4 * half + 4, first:first + n]).then_inc(raw_in[half], 16)
            m.gate_fill.load(sp)
            sp.wait_ge(out_act, 3 * TT // 2)
            sp.wait_ge(out_dve, 3 * TT // 2)
            sp.dma_start(m.scr_lat, m.lat.rearrange("p a b -> p (a b)")).then_inc(spill, 16)
            sp.wait_ge(out_act, nch * TT // 2)
            sp.wait_ge(out_dve, nch * TT // 2)
            sp.dma_start(m.scr_u, m.u.rearrange("p g s h -> p (g s h)")).then_inc(spill, 16)
            m.gate_fill.load(sp)

        @block.gpsimd
        def _(pool):
            m.pool_step.on(pool)
            m.pool_step(nc.gpsimd.memset(m.ident[:], 0.0))
            m.pool_step(nc.gpsimd.affine_select(out=m.ident[:], in_=m.ident[:], compare_op=ALU.not_equal, fill=1.0,
                                                base=0, pattern=[[-1, P]], channel_multiplier=1))
            m.pool_step(nc.gpsimd.tensor_copy(m.identb[:], m.ident[:]))
            m.pool_step(nc.gpsimd.memset(m.maskb[:], 0.0))
            nc.gpsimd.affine_select(out=m.maskb[:], in_=m.maskb[:], compare_op=ALU.is_ge, fill=NEG,
                                    base=0, pattern=[[-1, P]], channel_multiplier=1).then_inc(const, 1)
            pool.wait_ge(const, 1)
            nrm.powers(pool)
            m.gate_fill.gpsimd(pool, 1)

        @block.tensor
        def _(pe):
            pe.wait_ge(const, 1)
            pe.wait_ge(vec_in, 96)
            for j in range(CONV):
                nc.tensor.transpose(m.ps[:, 5, j * P:j * P + 44], m.vecs[0:44, j * P:(j + 1) * P], m.ident[0:44, 0:44])
            nc.tensor.transpose(m.ps[:, 5, 3 * P:3 * P + 67], m.vecs[0:67, 0:P], m.ident[0:67, 0:67]).then_inc(vec_turned, 1)
            nrm.turn(pe, range(KD))
            pe.wait_ge(nrm.done, KD)
            n = 0
            for c, (first, width) in enumerate(chunks):
                pe.wait_ge(w_lo_done, 2 * c + 2)
                for t in range(TT):
                    bank = 4 + n % 4
                    if n < 4:
                        nrm.turn(pe, range(KD + 2 * n, KD + 2 * n + 2))
                    elif n == 4:
                        pe.wait_ge(nrm.done, 2 * KD)
                    if n >= 4:
                        pe.wait_ge(out_act if n % 2 == 0 else out_dve, n // 2 - 1)
                    for k in range(KD):
                        if first == C_U:
                            hi, lo = (a[:, k, :].rearrange("p (c s) -> p c s", s=8)[:, :, t] for a in (m.h_hi, m.h_lo))
                        else:
                            hi, lo = (a[:, k, t * P:(t + 1) * P] for a in (m.h_hi, m.h_lo))
                        wh, wl = w_hi[c % 2][:, k, 0:width], w_lo[c % 2][:, k, 0:width]
                        o = m.ps[:, bank, 0:width]
                        nc.tensor.matmul(o, hi, wh, start=(k == 0), stop=False)
                        nc.tensor.matmul(o, hi, wl, start=False, stop=False)
                        mm = nc.tensor.matmul(o, lo, wh, start=False, stop=(k == KD - 1))
                    mm.then_inc(prod, 1)
                    n += 1

        @block.scalar
        def _(act):
            cw = m.ins["ffn_conv_w"][0]
            act.dma_start(m.vecs[0:44, :].rearrange("f (j c) -> f j c", j=CONV),
                         cw.rearrange("j (f c) -> f j c", c=P)).then_inc(vec_in, 16)
            at = 44
            for v in (m.ins["attn_norm_g"], m.ins["ffn_norm_g"], m.ins["q_lat_norm_g"], m.ins["kv_lat_norm_g"], m.ins["s5_b_glu"]):
                n = v.shape[1] // P
                act.dma_start(m.vecs[at:at + n, 0:P], v[0].rearrange("(r c) -> r c", c=P)).then_inc(vec_in, 16)
                at += n
            for i in range(TT):
                act.wait_ge(x_in[i], 16)
                nrm.square(act, i)
            act.wait_ge(vec_done, 2)
            nrm.hi(act, range(KD))

            def split(c, half):
                n = chunks[c][1]
                act.wait_ge(raw_in[half], 16 * (c + 1))
                if c >= 2:
                    act.wait_ge(prod, (c - 1) * TT)
                nc.scalar.activation(w_hi[c % 2][:, 4 * half:4 * half + 4, 0:n], raw[half][:, :, 0:n], ACT.Copy).then_inc(w_hi_done, 1)
            split(0, 0), split(0, 1)
            for n in range(nch * TT):
                if n < 4:
                    nrm.hi(act, range(KD + 2 * n, KD + 2 * n + 2))
                elif n == 4:
                    split(1, 0), split(1, 1)
                if n % 2 == 0:
                    act.wait_ge(prod, n + 1)
                    nc.scalar.activation(dest(n // TT, n % TT), made(n), ACT.Copy).then_inc(out_act, 1)
                if n % TT == TT - 1 and n // TT + 2 < nch:
                    split(n // TT + 2, 0), split(n // TT + 2, 1)
            m.gate_fill.split_hi(act, 0)

        @block.vector
        def _(dve):
            nrm.mean(dve, 0)
            for i in range(TT):
                if i + 1 < TT:
                    nrm.mean(dve, i + 1)
                nrm.scale(dve, i)
            dve.wait_ge(vec_turned, 1)
            nc.vector.tensor_copy(m.conv_w, m.ps[:, 5, 0:3 * P].rearrange("p (j c) -> p j c", j=CONV)[:, :, 0:44]).then_inc(vec_done, 1)
            nc.vector.tensor_copy(m.colv[:, 132:155], m.ps[:, 5, 3 * P + 44:3 * P + 67]).then_inc(vec_done, 1)
            dve.wait_ge(vec_done, 2)
            nrm.lo(dve, range(KD))

            def split(c, half):
                n = chunks[c][1]
                dve.wait_ge(w_hi_done, 2 * c + half + 1)
                hi = w_hi[c % 2][:, 4 * half:4 * half + 4, 0:n]
                nc.vector.tensor_tensor(w_lo[c % 2][:, 4 * half:4 * half + 4, 0:n], raw[half][:, :, 0:n], f32(hi),
                                        ALU.subtract).then_inc(w_lo_done, 1)
            split(0, 0), split(0, 1)
            for n in range(nch * TT):
                if n < 4:
                    nrm.lo(dve, range(KD + 2 * n, KD + 2 * n + 2))
                elif n == 4:
                    split(1, 0), split(1, 1)
                if n % 2 == 1:
                    dve.wait_ge(prod, n + 1)
                    nc.vector.tensor_copy(dest(n // TT, n % TT), made(n)).then_inc(out_dve, 1)
                if n % TT == TT - 1 and n // TT + 2 < nch:
                    split(n // TT + 2, 0), split(n // TT + 2, 1)
            dve.wait_ge(row_in, 80)


class GateFill:

    PER_HALF = 3 * KD

    def __init__(self, m, plan):
        self.m = m
        self.banks = [banks[i % len(banks)] for units, banks in plan for i in range(2 * units)]
        self.count = len(self.banks) // 2
        at = 2 * KD * T
        self.raw, self.stage = cols(m.F, 17920, KD, P), cols(m.F, 17408, BANK)
        at += 12 * T
        self.w_hi = [cols(m.R, at + 2 * i * T, KD, P) for i in range(2)]
        self.w_lo = [cols(m.R, at + (2 * i + 1) * T, KD, P) for i in range(2)]
        self.w_in, self.hi, self.lo, self.half_mm, self.out, self.stored = (
            m.sem(f"gate_{n}") for n in ("w_in", "hi", "lo", "mm", "out", "stored"))
        self.at = {"pe": 0, "act": 0}
        self.copied = self.split = self.loaded = self.saved = 0
        self.w_src = m.ins["w_in"][0].rearrange("(k p) n -> p k n", p=P)

    def load(self, sp):
        u, self.loaded = self.loaded, self.loaded + 1
        if u < self.count:
            d, n = divmod(u, 3)
            if u:
                sp.wait_ge(self.lo, u)
            sp.dma_start(self.raw, self.w_src[:, :, C_G + n * D + d * P:C_G + n * D + (d + 1) * P]).then_inc(self.w_in, 16)

    def sync(self, sp, units):
        for _ in range(units):
            u, self.saved = self.saved, self.saved + 1
            self.load(sp)
            for half in range(2):
                sp.wait_ge(self.out, 2 * u + half + 1)
                sp.dma_start(self.m.scr_gate[u][:, half * BANK:(half + 1) * BANK], self.stage).then_inc(self.stored, 16)

    def all_stored(self, eng):
        eng.wait_ge(self.stored, 32 * self.count)

    def tensor(self, pe, n):
        m, nc = self.m, self.m.nc
        for i in range(self.at["pe"], self.at["pe"] + n):
            half, j = divmod(i, self.PER_HALF)
            u, h = divmod(half, 2)
            k, which = divmod(j, 3)
            if j == 0:
                pe.wait_ge(self.lo, u + 1)
                before = [b for b in range(half) if self.banks[b] == self.banks[half]]
                if before:
                    pe.wait_ge(self.out, before[-1] + 1)
            w = (self.w_hi, self.w_hi, self.w_lo)[which][u % 2]
            src = (m.h_hi, m.h_lo, m.h_hi)[which]
            mm = nc.tensor.matmul(m.ps[:, self.banks[half], :], w[:, k, :], src[:, k, h * BANK:(h + 1) * BANK], start=(j == 0), stop=(j == self.PER_HALF - 1))
            if j == self.PER_HALF - 1:
                mm.then_inc(self.half_mm, 1)
        self.at["pe"] += n

    def scalar(self, act, n):
        m, nc = self.m, self.m.nc
        for i in range(self.at["act"], self.at["act"] + n):
            half, j = divmod(i, self.PER_HALF)
            if j:
                continue
            if self.copied < half:
                self.copy_out(act)
            if half % 2 == 0:
                self.split_hi(act, half // 2 + 1)
        self.at["act"] += n

    def split_hi(self, act, u):
        if u < self.count:
            act.wait_ge(self.w_in, 16 * (u + 1))
            if u >= 2:
                act.wait_ge(self.half_mm, 2 * (u - 1))
            self.m.nc.scalar.activation(self.w_hi[u % 2], self.raw, ACT.Copy).then_inc(self.hi, 1)

    def copy_made(self, act):
        while (self.copied + 1) * self.PER_HALF <= self.at["act"]:
            self.copy_out(act)

    def copy_out(self, act):
        act.wait_ge(self.half_mm, self.copied + 1)
        if self.copied:
            act.wait_ge(self.stored, 16 * self.copied)
        self.m.nc.scalar.activation(self.stage, self.m.ps[:, self.banks[self.copied], :], ACT.Copy).then_inc(self.out, 1)
        self.copied += 1

    def gpsimd(self, pool, n):
        for u in range(self.split, min(self.split + n, self.count)):
            pool.wait_ge(self.hi, u + 1)
            self.m.nc.gpsimd.tensor_tensor(self.w_lo[u % 2], self.raw, f32(self.w_hi[u % 2]), ALU.subtract).then_inc(self.lo, 1)
        self.split += n


FOX_PREP, MLA_FIRST, MLA_PREP, S5_FIRST, S5_SECOND = 4, 2, 5, 3, 2
ATT_FILL = (12, 12, 8, 4, 4, 4, 2, 2)
FOX_UNITS = FOX_PREP + H
MLA_UNITS = MLA_FIRST + MLA_PREP + H
S5_UNITS = S5_FIRST + S5_SECOND
assert FOX_UNITS + MLA_UNITS + S5_UNITS == 3 * KD
UNIT = 2 * GateFill.PER_HALF
GATE_PLAN = ((FOX_PREP, (6, 7)), (H, (7,)), (MLA_FIRST + MLA_PREP, (6, 7)), (H, (7,)), (S5_UNITS, (0, 1)))
ATT_STEPS = H * TT


def attention(m, tag, kd, q_of, k_of, v_of, q_t, k_t, p_buf, pt_buf, branch, ready, fill):
    nc, ps = m.nc, m.ps
    scores, negmax, exped, normed, filled, copied, pv, o_hi, o_lo, rs = (
        m.sem(f"{tag}_{n}") for n in ("scores", "negmax", "exp", "norm", "filled", "copied", "pv", "o_hi", "o_lo", "recip"))
    nmax, rsum, rinv = m.stat[:, 0:2], m.stat[:, 2:4], m.stat[:, 4:6]
    S = [m.ps[:, 0:2, :].rearrange("p b n -> p (b n)"), m.ps[:, 2:4, :].rearrange("p b n -> p (b n)")]

    fills = []
    order = []
    if q_of is not None:
        order.append(("qk", 0))
    nb = len(q_t)
    for s in range(ATT_STEPS + 2):
        if s < ATT_STEPS:
            order.append(("s", s))
        if 1 <= s <= ATT_STEPS:
            order.append(("t", s - 1))
        if s < ATT_STEPS:
            order.append(("f", ATT_FILL[s % TT]))
        if s >= 2:
            order.append(("v", s - 2))
        if q_of is not None and s % TT == 5 and s // TT + 1 < H:
            order.append(("qk", s // TT + 1))
    qk_until, t_until = {}, {}
    for what, n in order:
        if what == "qk":
            fills += [("qk", n, w, half) for w in range(2) for half in range(2)]
            qk_until[n] = len(fills)
        elif what == "t":
            tiles = n % TT + 1
            fills += [("p", n, a, min(4, tiles - a)) for a in range(0, tiles, 4)]
            t_until[n] = len(fills)

    def tensor(pe):
        ready(pe)
        f = 0
        for what, n in order:
            h, i = divmod(n, TT)
            if what == "f":
                fill.tensor(pe, n)
            elif what == "qk":
                h = n
                for w, (src, _) in enumerate(((q_of, q_t), (k_of, k_t))):
                    for half in range(2):
                        if f >= 2:
                            pe.wait_ge(copied, f - 1)
                        for j in range(4):
                            tr = nc.tensor.transpose(ps[0:kd, 4 + f % 2, j * P:(j + 1) * P], src(h, 4 * half + j), m.ident[:])
                        tr.then_inc(filled, 1)
                        f += 1
            elif what == "s":
                if i == 0 and q_of is not None:
                    pe.wait_ge(copied, qk_until[h])
                if n >= 2:
                    pe.wait_ge(exped, n - 1)
                keys = (i + 1) * P
                for a in range(0, keys, BANK):
                    b = min(keys, a + BANK)
                    diag = b == keys
                    mm = nc.tensor.matmul(S[n % 2][:, a:b], q_t[h % nb][0:kd, i * P:(i + 1) * P], k_t[h % nb][0:kd, a:b],
                                          start=True, stop=not diag)
                mm = nc.tensor.matmul(S[n % 2][:, keys - P:keys], m.identb[:], m.maskb[:], start=False, stop=True)
                mm.then_inc(scores, 1)
            elif what == "t":
                pe.wait_ge(normed, n + 1)
                for a in range(0, i + 1, 4):
                    if f >= 2:
                        pe.wait_ge(copied, f - 1)
                    for j in range(a, min(a + 4, i + 1)):
                        tr = nc.tensor.transpose(ps[:, 4 + f % 2, (j - a) * P:(j - a + 1) * P],
                                                 p_buf[n % 2][:, j * P:(j + 1) * P], m.ident[:])
                    tr.then_inc(filled, 1)
                    f += 1
            else:
                pe.wait_ge(copied, t_until[n])
                g = n // 4
                if i % 4 == 0 and g >= 1:
                    pe.wait_ge(o_lo, g)
                rows = slice(64 * (h % 2), 64 * (h % 2) + 64)
                for j in range(i + 1):
                    mm = nc.tensor.matmul(ps[rows, 6, (i % 4) * P:(i % 4 + 1) * P], v_of(h, j),
                                          pt_buf[n % 2][:, j * P:(j + 1) * P], start=(j == 0), stop=(j == i))
                mm.then_inc(pv, 1)

    def out_rows(g):
        h, half = divmod(g, 2)
        rows = slice(64 * (h % 2), 64 * (h % 2) + 64)
        k = 2 * branch + h // 2
        return rows, k, slice(half * BANK, (half + 1) * BANK)

    def scalar(act):
        f = 0
        for what, n in order:
            if what == "f":
                fill.scalar(act, n)
                continue
            if what == "s":
                keys = (n % TT + 1) * P
                fill.copy_made(act)
                act.wait_ge(negmax, n + 1)
                if n >= 2:
                    act.wait_ge(filled, t_until[n - 2])
                    act.wait_ge(rs, n - 1)
                nc.scalar.activation(p_buf[n % 2][:, 0:keys], S[n % 2][:, 0:keys], ACT.Exp, bias=nmax[:, n % 2:n % 2 + 1],
                                     accum_out=rsum[:, n % 2:n % 2 + 1]).then_inc(exped, 1)
                continue
            if what in ("qk", "t"):
                while f < len(fills) and fills[f][0] == ("qk" if what == "qk" else "p") and fills[f][1] == n:
                    act.wait_ge(filled, f + 1)
                    if what == "qk":
                        _, h, w, half = fills[f]
                        if half == 0 and w == 0 and h >= 2:
                            act.wait_ge(scores, (h - 1) * TT)
                        dst = (q_t, k_t)[w][h % 2][0:kd, half * BANK:(half + 1) * BANK]
                        nc.scalar.activation(dst, ps[0:kd, 4 + f % 2, :], ACT.Copy).then_inc(copied, 1)
                    else:
                        _, s, a, c = fills[f]
                        if a == 0 and s >= 2:
                            act.wait_ge(pv, s - 1)
                        nc.scalar.activation(pt_buf[s % 2][:, a * P:(a + c) * P], ps[:, 4 + f % 2, 0:c * P], ACT.Copy).then_inc(copied, 1)
                    f += 1
            if what == "v" and n % 4 == 3:
                g = n // 4
                rows, k, cut = out_rows(g)
                act.wait_ge(pv, n + 1)
                nc.scalar.activation(m.br_hi[rows, k, cut], ps[rows, 6, :], ACT.Copy).then_inc(o_hi, 1)

    def vector(dve):
        for what, n in order:
            if what == "s":
                keys = (n % TT + 1) * P
                dve.wait_ge(scores, n + 1)
                if n >= 2:
                    dve.wait_ge(exped, n - 1)
                nc.vector.tensor_reduce(nmax[:, n % 2:n % 2 + 1], S[n % 2][:, 0:keys], AX.X, ALU.max, negate=True).then_inc(negmax, 1)
                dve.wait_ge(exped, n + 1)
                nc.vector.reciprocal(rinv[:, n % 2:n % 2 + 1], rsum[:, n % 2:n % 2 + 1]).then_inc(rs, 1)
                dve.wait_ge(rs, n + 1)
                nc.vector.tensor_scalar(p_buf[n % 2][:, 0:keys], p_buf[n % 2][:, 0:keys], rinv[:, n % 2:n % 2 + 1], None,
                                        ALU.mult).then_inc(normed, 1)
            elif what == "v" and n % 4 == 3:
                g = n // 4
                rows, k, cut = out_rows(g)
                dve.wait_ge(o_hi, g + 1)
                nc.vector.tensor_tensor(m.br_lo[rows, k, cut], ps[rows, 6, :], f32(m.br_hi[rows, k, cut]),
                                        ALU.subtract).then_inc(o_lo, 1)
    return Programs(scalar, vector, tensor)


def stage_fox(m):
    nc = m.nc
    ndim = 2 * TT * FH
    qk = m.fqk.rearrange("p t (g d) -> p (t g) d", d=FD)
    KA = FD + 2
    aug = cols(m.F, 0, TT, 2 * FH, KA)
    sq = cols(m.F, 11552, ndim, FD)
    ssq, rstd, expo = m.stat[:, 0:ndim], m.statb[:, 0:ndim], cols(m.F, 15648, ndim)
    small = [cols(m.F, 15712 + 32 * i, TT, FH) for i in range(12)]
    z, e, den, s1, s2, acc, tot, pre, cum, ez, one_c, _ = small
    ones = cols(m.F, 16096, P)
    upper = cols(m.F, 16224, P)
    q_t = [cols(m.F, 5376 + i * T, T) for i in range(2)]
    k_t = [cols(m.F, 5376 + (2 + i) * T, T) for i in range(2)]
    p_buf = [cols(m.F, 11552 + i * T, T) for i in range(2)]
    pt_buf = [cols(m.F, 11552 + (2 + i) * T, T) for i in range(2)]
    W0 = 2 * KD * T
    m.br_hi = cols(m.R, W0, 6, T)
    m.br_lo = cols(m.R, W0 + 6 * T, 6, T)
    sq_done, ms_done, rstd_done, const, z_done, e_done, log_done, sum_done, prep = (
        m.sem(f"fox_{n}") for n in ("sq", "ms", "rstd", "const", "z", "e", "log", "sum", "prep"))
    gq, gk, fb = m.rowg[:, 192:256], m.rowg[:, 256:320], m.rowg[:, 320:324]

    def ready(pe):
        pe.wait_ge(prep, 1)
    fill = m.gate_fill
    att = attention(m, "fox", KA, lambda h, t: aug[:, t, h, :], lambda h, t: aug[:, t, FH + h, :],
                    lambda h, j: m.fvf[:, j, h * FD:(h + 1) * FD], q_t, k_t, p_buf, pt_buf, 1, ready, fill)

    with nc.Block() as block:
        @block.sync
        def _(sp):
            fill.sync(sp, FOX_UNITS)

        @block.gpsimd
        def _(pool):
            m.pool_step.on(pool)
            nc.gpsimd.memset(expo, -0.5).then_inc(const, 1)
            nc.gpsimd.memset(ones, 1.0).then_inc(const, 1)
            pool.wait_ge(const, 2)
            nc.gpsimd.affine_select(out=upper, in_=ones, compare_op=ALU.is_ge, fill=0.0, base=0,
                                    pattern=[[1, P]], channel_multiplier=-1).then_inc(const, 1)
            fill.gpsimd(pool, 2)
            pool.wait_ge(ms_done, 1)
            nc.gpsimd.tensor_tensor(rstd, ssq, expo, ALU.pow).then_inc(rstd_done, 1)
            fill.gpsimd(pool, FOX_UNITS - 2)

        @block.scalar
        def _(act):
            act.wait_ge(z_done, 1)
            nc.scalar.activation(e, ez, ACT.Exp).then_inc(e_done, 1)
            act.wait_ge(m.spill, 32)
            nc.scalar.activation(sq, qk, ACT.Square).then_inc(sq_done, 1)
            fill.scalar(act, FOX_PREP * UNIT)
            att.scalar(act)
            fill.copy_made(act)

        @block.tensor
        def _(pe):
            fill.tensor(pe, UNIT)
            pe.wait_ge(const, 3)
            pe.wait_ge(log_done, 1)
            nc.tensor.matmul(m.ps[:, 5, 0:32], upper, z.rearrange("p t h -> p (t h)"), start=True, stop=True)
            nc.tensor.matmul(m.ps[:, 5, 32:64], ones, z.rearrange("p t h -> p (t h)"), start=True, stop=True).then_inc(sum_done, 1)
            fill.tensor(pe, (FOX_PREP - 1) * UNIT)
            att.tensor(pe)

        @block.vector
        def _(dve):
            step = m.dve_step.on(dve)
            V = nc.vector
            step(V.tensor_tensor(z, m.fvf[:, :, 256:260], fb.unsqueeze(1).to_broadcast([P, TT, FH]), ALU.add))
            V.scalar_tensor_tensor(out=ez, in0=z, scalar=-1.0, in1=z, op0=ALU.mult, op1=ALU.min).then_inc(z_done, 1)
            step(V.tensor_scalar(gq, gq, float(FD) ** -0.5, None, ALU.mult))
            dve.wait_ge(e_done, 1)
            step(V.tensor_scalar(den, e, 2.0, None, ALU.add))
            step(V.reciprocal(den, den))
            step(V.tensor_tensor(s1, e, den, ALU.mult))
            step(V.tensor_tensor(s2, s1, s1, ALU.mult))
            step(V.tensor_scalar(acc, s2, 2.0 / 17, 2.0 / 15, ALU.mult, ALU.add))
            for k in (13, 11, 9, 7, 5, 3, 1):
                step(V.tensor_tensor(acc, acc, s2, ALU.mult))
                step(V.tensor_scalar(acc, acc, 2.0 / k, None, ALU.add))
            step(V.tensor_tensor(acc, acc, s1, ALU.mult))
            V.scalar_tensor_tensor(out=z, in0=z, scalar=0.0, in1=acc, op0=ALU.min, op1=ALU.subtract).then_inc(log_done, 1)
            dve.wait_ge(sq_done, 1)
            step(V.tensor_reduce(ssq, sq, AX.X, ALU.add))
            V.tensor_scalar(ssq, ssq, 1.0 / FD, EPS, ALU.mult, ALU.add).then_inc(ms_done, 1)
            dve.wait_ge(sum_done, 1)
            step(V.tensor_copy(tot.rearrange("p t h -> p (t h)"), m.ps[:, 5, 32:64]))
            step(V.memset(pre[:, 0, :], 0.0))
            for t in range(1, TT):
                step(V.tensor_tensor(pre[:, t, :], pre[:, t - 1, :], tot[:, t - 1, :], ALU.add))
            step(V.tensor_tensor(cum, m.ps[:, 5, 0:32].rearrange("p (t h) -> p t h", h=FH), pre, ALU.add))
            step(V.memset(aug[:, :, 0:FH, FD:FD + 1], 1.0))
            step(V.tensor_copy(aug[:, :, 0:FH, FD + 1], cum))
            step(V.tensor_scalar(aug[:, :, FH:2 * FH, FD], cum, -1.0, None, ALU.mult))
            step(V.memset(aug[:, :, FH:2 * FH, FD + 1:FD + 2], 1.0))
            dve.wait_ge(rstd_done, 1)
            step(V.tensor_tensor(sq, qk, rstd.unsqueeze(2).to_broadcast([P, ndim, FD]), ALU.mult))
            sqv = sq.rearrange("p (t g) d -> p t g d", g=2 * FH)
            step(V.tensor_tensor(aug[:, :, 0:FH, 0:FD], sqv[:, :, 0:FH, :],
                                 gq.unsqueeze(1).unsqueeze(1).to_broadcast([P, TT, FH, FD]), ALU.mult))
            V.tensor_tensor(aug[:, :, FH:2 * FH, 0:FD], sqv[:, :, FH:2 * FH, :],
                            gk.unsqueeze(1).unsqueeze(1).to_broadcast([P, TT, FH, FD]), ALU.mult).then_inc(prep, 1)
            att.vector(dve)


INV_FREQ = [float(f) for f in (np.float32(10000.0) ** (-np.arange(0, ROPE, 2, dtype=np.float32) / np.float32(ROPE)))]
TWO_PI = 2 * math.pi
PI_A = 6.28125
PI_B = float(np.float32(round((TWO_PI - PI_A) * 2 ** 22) / 2 ** 22))
PI_C = TWO_PI - PI_A - PI_B
ROUND = 1.5 * 2 ** 23
PI32 = 3.1415925


def reduced(nc, step, ang, turns, absang):
    V = nc.vector
    step(V.tensor_scalar(turns, ang, 1.0 / TWO_PI, ROUND, ALU.mult, ALU.add))
    step(V.tensor_scalar(turns, turns, ROUND, None, ALU.subtract))
    for part in (PI_A, PI_B, PI_C):
        step(V.scalar_tensor_tensor(out=ang, in0=turns, scalar=-part, in1=ang, op0=ALU.mult, op1=ALU.add))
    step(V.tensor_scalar(ang, ang, PI32, -PI32, ALU.min, ALU.max))
    step(V.scalar_tensor_tensor(out=absang, in0=ang, scalar=-1.0, in1=ang, op0=ALU.mult, op1=ALU.min))
    return V.tensor_scalar(absang, absang, math.pi / 2, None, ALU.add)


def stage_mla(m):
    nc = m.nc
    lat = cols(m.F, 0, TT, 672)
    lat_t = cols(m.F, 7168, 5, T)
    w_uq = cols(m.F, 15360, 3, H * QK)
    w_ukv = [cols(m.F, at, H * 2 * NOPE) for at in (16512, 6608)]
    q = cols(m.F, 12288, TT, H, QK)
    kv = cols(m.F, 0, TT, H, 2 * NOPE)
    k = cols(m.F, 7168, TT, H, QK)
    v = cols(m.F, 10240, TT, H, VD)
    lsq = cols(m.F, 12288, TT, Q_RANK)
    sq = cols(m.F, 0, TT * H, QK)
    ang, sin, cos, turns, t1 = (cols(m.F, 5376 + i * 128, TT, ROPE // 2) for i in range(5))
    pos_i, pos8, kr = cols(m.F, 6016, P), cols(m.F, 6144, P), cols(m.F, 6272, TT, ROPE)
    pos_f, inv_freq = cols(m.F, 6528, TT), cols(m.F, 6536, ROPE // 2)
    tmp = [cols(m.F, 15360 + i * 512, TT, H, ROPE // 2) for i in range(2)]
    q_t = [cols(m.F, i * T, T) for i in range(2)]
    k_t = [cols(m.F, (2 + i) * T, T) for i in range(2)]
    p_buf = [cols(m.F, 4096, T), cols(m.F, 15360, T)]
    pt_buf = [cols(m.F, 5120 + i * T, T) for i in range(2)]
    ssq, rstd, expo = m.stat[:, 0:48], m.statb[:, 0:48], cols(m.F, 6560, 48)
    gq, gk = m.rowg[:, 0:QK], m.rowg[:, QK:2 * QK]

    lat_in, w_in, pos_in, const, pos_t, sq_done, ms_done, rstd_done, ang_done, rope_done, scaled, filled, copied, q_prod, kv_prod, q_out, kv_out, prep = (
        m.sem(f"mla_{n}") for n in ("lat_in", "w_in", "pos_in", "const", "pos_t", "sq", "ms", "rstd", "ang", "sincos", "scaled",
                                    "filled", "copied", "q_prod", "kv_prod", "q_out", "kv_out", "prep"))

    pos_t_done = m.sem("mla_pos_t_done")

    def ready(pe):
        pe.wait_ge(prep, 1)
    fill = m.gate_fill
    att = attention(m, "mlaa", QK, lambda h, t: q[:, t, h, :], lambda h, t: k[:, t, h, :],
                    lambda h, j: v[:, j, h, :], q_t, k_t, p_buf, pt_buf, 0, ready, fill)
    J = GR // 2
    m.s5_rows = [m.vecs[0:J, 2 * P:3 * P], m.cidx[0:J, :]]
    m.s5_log_step = m.statb[0:J, 60:62]
    m.s5_c = [m.vecs[:, i * P:(i + 1) * P] for i in range(2)]
    m.s5_b = [cols(m.F, 17152 + i * P, J, GC) for i in range(2)]
    m.s5_rows_in, m.s5_c_in, m.s5_b_in = (m.sem(f"s5_{n}_in") for n in ("rows", "c", "b"))
    with nc.Block() as block:
        @block.sync
        def _(sp):
            sp.dma_start(pos_i.bitcast(I32)[0:TT, :], m.ins["positions"][0].rearrange("(i p) -> i p", p=P)).then_inc(pos_in, 16)
            sp.wait_ge(m.spill, 32)
            sp.dma_start(lat.rearrange("p a b -> p (a b)"), m.scr_lat).then_inc(lat_in, 16)
            sp.dma_start(w_uq, m.ins["w_uq"][0].rearrange("(k p) h d -> p k (h d)", p=P)).then_inc(w_in, 16)
            for r in range(2):
                sp.dma_start(w_ukv[r], m.ins["w_ukv"][0, r * P:(r + 1) * P].rearrange("p h d -> p (h d)")).then_inc(w_in, 16)
            for i, v in enumerate((m.ins["s5_lambda_re"], m.ins["s5_lambda_im"])):
                sp.dma_start(m.s5_rows[i], v[0].rearrange("(j g) p -> j (g p)", g=2)).then_inc(m.s5_rows_in, 16)
            sp.dma_start(m.s5_log_step, m.ins["s5_log_step"][0].rearrange("(j g) -> j g", g=2)).then_inc(m.s5_rows_in, 16)
            for i, v in enumerate((m.ins["s5_c_re"], m.ins["s5_c_im"])):
                vj = v[0].rearrange("(j g) h p -> g j h p", g=2)
                for g in range(2):
                    for j in range(GR // 2):
                        sp.dma_start(m.s5_c[i][j * GC:(j + 1) * GC, g * ST:(g + 1) * ST], vj[g, j]).then_inc(m.s5_c_in, 16)
            for i, v in enumerate((m.ins["s5_b_re"], m.ins["s5_b_im"])):
                vj = v[0].rearrange("(j g) p h -> g p j h", g=2)
                for g in range(2):
                    sp.dma_start(m.s5_b[i][g * ST:(g + 1) * ST], vj[g]).then_inc(m.s5_b_in, 16)
            fill.sync(sp, MLA_UNITS)

        @block.gpsimd
        def _(pool):
            nc.gpsimd.memset(expo, -0.5).then_inc(const, 1)
            for j, f in enumerate(INV_FREQ):
                nc.gpsimd.memset(inv_freq[:, j:j + 1], f).then_inc(const, 1)
            pool.wait_ge(const, 1 + len(INV_FREQ))
            fill.gpsimd(pool, 1)
            for n, (a, b) in enumerate(((0, 16), (16, 48), (16, 48))):
                pool.wait_ge(ms_done, n + 1)
                nc.gpsimd.tensor_tensor(rstd[:, a:b], ssq[:, a:b], expo[:, a:b], ALU.pow).then_inc(rstd_done, 1)
                fill.gpsimd(pool, (MLA_FIRST, 2, MLA_UNITS - MLA_FIRST - 3)[n])

        @block.scalar
        def _(act):
            fill.scalar(act, MLA_FIRST * UNIT)
            act.wait_ge(ang_done, 1)
            nc.scalar.activation(sin, ang, ACT.Sin).then_inc(rope_done, 1)
            nc.scalar.activation(cos, turns, ACT.Sin).then_inc(rope_done, 1)
            for f in range(10):
                act.wait_ge(filled, f + 1)
                r, half = divmod(f, 2)
                g = m.g_qlat[:, r:r + 1] if r < 3 else m.g_kvlat[:, r - 3:r - 2]
                nc.scalar.activation(lat_t[:, r, half * BANK:(half + 1) * BANK], m.ps[:, f % 4, :], ACT.Copy, scale=g).then_inc(copied, 1)
            for t in range(TT):
                act.wait_ge(q_prod, t + 1)
                nc.scalar.activation(q[:, t].rearrange("p h d -> p (h d)"), m.ps[:, t % 4, 0:H * QK], ACT.Copy).then_inc(q_out, 1)
            fill.scalar(act, MLA_PREP * UNIT)
            att.scalar(act)
            fill.copy_made(act)

        @block.tensor
        def _(pe):
            fill.tensor(pe, UNIT)
            pe.wait_ge(pos_t, 1)
            nc.tensor.transpose(m.ps[:, 5, 0:TT], pos8[0:TT, :], m.ident[0:TT, 0:TT]).then_inc(pos_t_done, 1)
            fill.tensor(pe, (MLA_FIRST - 1) * UNIT)
            pe.wait_ge(scaled, 2)
            f = 0
            for r in range(5):
                for half in range(2):
                    if f >= 4:
                        pe.wait_ge(copied, f - 3)
                    for j in range(4):
                        tr = nc.tensor.transpose(m.ps[:, f % 4, j * P:(j + 1) * P], lat[:, 4 * half + j, r * P:(r + 1) * P], m.ident[:])
                    tr.then_inc(filled, 1)
                    f += 1
            pe.wait_ge(copied, 10)
            pe.wait_ge(w_in, 48)
            for t in range(TT):
                if t >= 4:
                    pe.wait_ge(q_out, t - 3)
                for r in range(3):
                    mm = nc.tensor.matmul(m.ps[:, t % 4, 0:H * QK], lat_t[:, r, t * P:(t + 1) * P], w_uq[:, r, :], start=(r == 0), stop=(r == 2))
                mm.then_inc(q_prod, 1)
                if t >= 2:
                    pe.wait_ge(kv_out, t - 1)
                for r in range(2):
                    mm = nc.tensor.matmul(m.ps[:, 4 + t % 2, :], lat_t[:, 3 + r, t * P:(t + 1) * P], w_ukv[r], start=(r == 0), stop=(r == 1))
                mm.then_inc(kv_prod, 1)
            fill.tensor(pe, MLA_PREP * UNIT)
            att.tensor(pe)

        @block.vector
        def _(dve):
            step = m.dve_step.on(dve)
            V = nc.vector
            dve.wait_ge(pos_in, 16)
            V.tensor_copy(pos8[0:TT, :], pos_i.bitcast(I32)[0:TT, :]).then_inc(pos_t, 1)
            step(V.tensor_scalar(gq, gq, float(QK) ** -0.5, None, ALU.mult))
            dve.wait_ge(lat_in, 16)
            for n, (a, b) in enumerate(((0, Q_RANK), (Q_RANK, Q_RANK + KV_RANK))):
                part = lsq[:, :, 0:b - a]
                step(V.tensor_tensor(part, lat[:, :, a:b], lat[:, :, a:b], ALU.mult))
                step(V.tensor_reduce(ssq[:, 8 * n:8 * n + 8], part, AX.X, ALU.add))
                ins = V.tensor_scalar(ssq[:, 8 * n:8 * n + 8], ssq[:, 8 * n:8 * n + 8], 1.0 / (b - a), EPS, ALU.mult, ALU.add)
                ins.then_inc(ms_done, 1) if n else step(ins)
            dve.wait_ge(pos_t_done, 1)
            step(V.tensor_copy(pos_f, m.ps[:, 5, 0:TT]))
            dve.wait_ge(const, 1 + len(INV_FREQ))
            step(V.tensor_copy(t1, pos_f.unsqueeze(2).to_broadcast([P, TT, ROPE // 2])))
            step(V.tensor_tensor(ang, t1, inv_freq.unsqueeze(1).to_broadcast([P, TT, ROPE // 2]), ALU.mult))
            reduced(nc, step, ang, t1, turns).then_inc(ang_done, 1)
            dve.wait_ge(rstd_done, 1)
            for n, (a, b) in enumerate(((0, Q_RANK), (Q_RANK, Q_RANK + KV_RANK))):
                V.tensor_tensor(lat[:, :, a:b], lat[:, :, a:b], rstd[:, 8 * n:8 * n + 8].unsqueeze(2).to_broadcast([P, TT, b - a]),
                                ALU.mult).then_inc(scaled, 1)
            step(V.tensor_copy(kr, lat[:, :, C_KR:C_KR + ROPE]))
            for t in range(TT):
                dve.wait_ge(kv_prod, t + 1)
                V.tensor_copy(kv[:, t].rearrange("p h d -> p (h d)"), m.ps[:, 4 + t % 2, :]).then_inc(kv_out, 1)
            dve.wait_ge(kv_out, TT)
            step(V.tensor_copy(k[:, :, :, 0:NOPE], kv[:, :, :, 0:NOPE]))
            step(V.tensor_copy(k[:, :, :, NOPE:QK], kr.unsqueeze(2).to_broadcast([P, TT, H, ROPE])))
            step(V.tensor_copy(v, kv[:, :, :, NOPE:]))
            dve.wait_ge(q_out, TT)
            dve.wait_ge(rope_done, 2)
            for n, (a, g) in enumerate(((k, gk), (q, gq))):
                flat = a.rearrange("p t h d -> p (t h) d")
                step(V.tensor_tensor(sq, flat, flat, ALU.mult))
                step(V.tensor_reduce(ssq[:, 16:48], sq, AX.X, ALU.add))
                V.tensor_scalar(ssq[:, 16:48], ssq[:, 16:48], 1.0 / QK, EPS, ALU.mult, ALU.add).then_inc(ms_done, 1)
                dve.wait_ge(rstd_done, 2 + n)
                step(V.tensor_tensor(sq, flat, rstd[:, 16:48].unsqueeze(2).to_broadcast([P, TT * H, QK]), ALU.mult))
                step(V.tensor_tensor(flat, sq, g.unsqueeze(1).to_broadcast([P, TT * H, QK]), ALU.mult))
                x1, x2 = a[:, :, :, NOPE:NOPE + ROPE // 2], a[:, :, :, NOPE + ROPE // 2:QK]
                sb, cb = (z.unsqueeze(2).to_broadcast([P, TT, H, ROPE // 2]) for z in (sin, cos))
                step(V.tensor_tensor(tmp[0], x1, sb, ALU.mult))
                step(V.tensor_tensor(tmp[1], x2, sb, ALU.mult))
                step(V.tensor_tensor(x1, x1, cb, ALU.mult))
                step(V.tensor_tensor(x2, x2, cb, ALU.mult))
                step(V.tensor_tensor(x1, x1, tmp[1], ALU.subtract))
                last = V.tensor_tensor(x2, x2, tmp[0], ALU.add)
                step(last) if n == 0 else last.then_inc(prep, 1)
            att.vector(dve)


def stage_s5(m):
    nc = m.nc
    J = GR // 2
    u = cols(m.F, 0, GR, CH, GC)
    u_t = cols(m.F, 2048, GR, NCH)
    m_re = cols(m.F, 4096, J, 2, 9, GC)
    m_im = cols(m.F, 6400, J, 2, 9, GC)
    b_rep = [cols(m.F, 8704 + i * 1024, J, CH, GC) for i in range(2)]
    w = [cols(m.F, 10752 + i * 1024, J, CH, GC) for i in range(2)]
    w_t = [cols(m.F, 12800 + i * 1024, J, P) for i in range(2)]
    kk = cols(m.F, 14848, GR, CH * GC)
    toep = cols(m.F, 10752, GR, CH * GC)
    tab = [cols(m.F, 8704 + i * 1024, J, NCH) for i in range(2)]
    z_in = [cols(m.F, 14848 + i * 1024, J, NCH) for i in range(2)]
    z = [cols(m.F, 12800 + i * 1024, J, NCH) for i in range(2)]
    s_prev = [cols(m.F, 14848 + i * 1024, J, NCH) for i in range(2)]
    tmp, rho = cols(m.F, 0, J, NCH), cols(m.F, 1024, J, NCH)
    y = cols(m.F, 12800, CH, GR, GC)
    y_t = cols(m.F, 8704, 2, NCH, CH)
    w_glu = cols(m.F, 0, 2, GR * GC)
    sg = [cols(m.F, 512 + i * BANK, BANK) for i in range(2)]
    at = [16640]

    def small(*dims):
        n = math.prod(dims)
        at[0] += n
        assert at[0] <= 17152
        return cols(m.F, at[0] - n, *dims)
    p9, a9, t9, e9, l_re, l_im = (small(J, 9) for _ in range(6))
    lre, lim, stp, a1, th, tt, ta, q_re, q_im, den = (small(J) for _ in range(10))
    t8, ki, mask16 = m.stat[:, 0:J], m.stat[:, J:J + 9], m.stat[:, 32:32 + GC]
    b, crow = m.s5_b, m.s5_c
    rows = m.s5_rows + [cols(m.F, 14848, P)[0:J]]
    bb = [cols(m.F, 15232 + i * 128, J, GC) for i in range(2)]
    cc = [cols(m.F, 15488 + i * 128, J, GC) for i in range(2)]
    d_row = cols(m.F, 15744, GR, GC)
    cidx = cols(m.F, 16000, NCH)
    pq = [cols(m.F, 16128 + i * 128, J, GC) for i in range(4)]
    names = ("u_in", "d_in", "step_b", "row_t", "row_c", "exp1", "cst", "ang9", "sc9", "w_rdy", "b_rdy", "w_ps",
             "w_cp", "u_ps", "u_cp", "k_ps", "k_cp", "toep_in", "x_ps", "tab_a", "tab_s", "s_rdy", "y_ps", "y_cp", "yt_ps", "yt_cp",
             "zero", "glu_in", "g_ps", "g_sg", "g_y", "g_hi", "g_lo", "cidx", "rho")
    s = {n: m.sem(f"s5_{n}") for n in names}
    ps = m.ps
    cidx_keep = m.cidx[:]

    def y_out(f):
        return cols(m.F, 1536 + f * BANK, BANK)

    fill = m.gate_fill
    with nc.Block() as block:
        @block.sync
        def _(sp):
            sp.dma_start(d_row.rearrange("p g h -> p (g h)"), m.ins["s5_d"][0].rearrange("g h -> (g h)").partition_broadcast(P)).then_inc(s["d_in"], 16)
            sp.dma_start(u.rearrange("p g s h -> p (g s h)"), m.scr_u).then_inc(s["u_in"], 16)
            fill.sync(sp, S5_FIRST)
            sp.wait_ge(s["k_cp"], 4)
            sp.wait_ge(s["zero"], 1)
            for kap in range(CH):
                lag = (CH - 1 - kap) * GC
                r = slice(kap * GC, (kap + 1) * GC)
                sp.dma_start(toep[r, :, lag:], kk[r, :, 0:CH * GC - lag]).then_inc(s["toep_in"], 16)
            fill.sync(sp, S5_SECOND)
            fill.all_stored(sp)
            sp.wait_ge(s["s_rdy"], 1)
            sp.dma_start(w_glu, m.ins["s5_w_glu"][0].rearrange("(k p) n -> p k n", p=P)).then_inc(s["glu_in"], 16)

        @block.gpsimd
        def _(pool):
            nc.gpsimd.iota(ki.bitcast(I32), pattern=[[1, 9]], base=0, channel_multiplier=0).then_inc(s["cst"], 1)
            nc.gpsimd.iota(cidx.bitcast(I32), pattern=[[1, NCH]], base=0, channel_multiplier=0).then_inc(s["cst"], 1)
            nc.gpsimd.memset(m_re.rearrange("p a b c d -> p (a b c d)"), 0.0).then_inc(s["cst"], 1)
            nc.gpsimd.memset(m_im.rearrange("p a b c d -> p (a b c d)"), 0.0).then_inc(s["cst"], 1)
            fill.gpsimd(pool, S5_UNITS - 1)

        @block.scalar
        def _(act):
            A = nc.scalar.activation
            fill.scalar(act, UNIT // 2)
            act.wait_ge(s["row_c"], 3)
            A(stp, stp, ACT.Exp).then_inc(s["exp1"], 1)
            act.wait_ge(s["ang9"], 2)
            A(e9, a9, ACT.Exp).then_inc(s["sc9"], 1)
            A(l_im, p9, ACT.Sin).then_inc(s["sc9"], 1)
            A(l_re, t9, ACT.Sin).then_inc(s["sc9"], 1)
            for f in range(4):
                act.wait_ge(s["u_ps"], f + 1)
                A(u_t[:, 4 * f:4 * f + 4, :].rearrange("p g c -> p (g c)"), ps[:, 2 + f, :], ACT.Copy).then_inc(s["u_cp"], 1)
            fill.scalar(act, S5_FIRST * UNIT - UNIT // 2)
            fill.copy_made(act)
            for f in range(4):
                act.wait_ge(s["w_ps"], f + 1)
                A(w_t[f // 2][:, 4 * (f % 2):4 * (f % 2) + 4, :].rearrange("p j c -> p (j c)"), ps[:, 4 + f, :], ACT.Copy).then_inc(s["w_cp"], 1)
            act.wait_ge(s["tab_a"], 1)
            A(tab[1], tab[1], ACT.Sin).then_inc(s["tab_s"], 1)
            A(tab[0], tab[0], ACT.Sin).then_inc(s["tab_s"], 1)
            fill.scalar(act, S5_SECOND * UNIT)
            fill.copy_made(act)
            for f in range(4):
                act.wait_ge(s["y_ps"], f + 1)
                dst = y[:, :, 4 * f:4 * f + 4, :].rearrange("p s g h -> p g s h")
                A(dst, ps[:, 4 + f, :].rearrange("p (g s h) -> p g s h", g=4, s=CH), ACT.Gelu_apprx_tanh).then_inc(s["y_cp"], 1)
            for f in range(4):
                act.wait_ge(s["g_ps"], f + 1)
                mt, half = divmod(f, 2)
                if f >= 2:
                    act.wait_ge(s["g_y"], f - 1)
                A(sg[f % 2], ps[:, 4 + f, :], ACT.Sigmoid, bias=m.b_glu[:, mt:mt + 1]).then_inc(s["g_sg"], 1)
                act.wait_ge(s["g_y"], f + 1)
                A(m.br_hi[:, 4 + mt, half * BANK:(half + 1) * BANK], y_out(f), ACT.Copy).then_inc(s["g_hi"], 1)

        @block.tensor
        def _(pe):
            I = m.ident
            fill.tensor(pe, UNIT // 2)
            pe.wait_ge(s["step_b"], 1)
            pe.wait_ge(m.s5_rows_in, 48)
            for i in range(3):
                tr = nc.tensor.transpose(ps[:, 7, i * J:(i + 1) * J], rows[i], I[0:J, 0:J])
            tr.then_inc(s["row_t"], 1)
            pe.wait_ge(m.s5_c_in, 16 * 4 * J)
            nc.tensor.transpose(ps[:, 6, 0:P], crow[0], I[:])
            nc.tensor.transpose(ps[:, 6, P:2 * P], crow[1], I[:]).then_inc(s["row_t"], 1)
            pe.wait_ge(s["u_in"], 16)
            for g in range(GR):
                tr = nc.tensor.transpose(ps[:, 2 + g // 4, (g % 4) * P:(g % 4 + 1) * P], u[:, g].rearrange("p s h -> p (s h)"), I[:])
                if g % 4 == 3:
                    tr.then_inc(s["u_ps"], 1)
            fill.tensor(pe, S5_FIRST * UNIT - UNIT // 2)
            pe.wait_ge(s["u_cp"], 4)
            pe.wait_ge(s["w_rdy"], 1)
            for n in range(2 * J):
                i, j = divmod(n, J)
                tr = nc.tensor.transpose(ps[:, 4 + n // 4, (n % 4) * P:(n % 4 + 1) * P], w[i][:, j].rearrange("p s h -> p (s h)"), I[:])
                if n % 4 == 3:
                    tr.then_inc(s["w_ps"], 1)
            pe.wait_ge(s["u_cp"], 4)
            pe.wait_ge(s["b_rdy"], 1)
            pe.wait_ge(s["w_cp"], 4)
            pe.wait_ge(fill.out, 2 * (FOX_UNITS + MLA_UNITS + S5_FIRST))
            for g in range(GR):
                j, g2 = divmod(g, 2)
                o = ps[:, g // 4, (g % 4) * P:(g % 4 + 1) * P]
                nc.tensor.matmul(o, b_rep[0][:, j].rearrange("p s h -> p (s h)"), m_re[:, j, g2, 0:8, :].rearrange("p k h -> p (k h)"), start=True, stop=False)
                mm = nc.tensor.matmul(o, b_rep[1][:, j].rearrange("p s h -> p (s h)"), m_im[:, j, g2, 0:8, :].rearrange("p k h -> p (k h)"), start=False, stop=True)
                if g % 4 == 3:
                    mm.then_inc(s["k_ps"], 1)
            for i in range(2):
                for j in range(J):
                    for g2 in range(2):
                        mm = nc.tensor.matmul(ps[g2 * ST:(g2 + 1) * ST, 4 + 2 * i + j // 4, (j % 4) * P:(j % 4 + 1) * P],
                                              w_t[i][:, j, g2 * ST:(g2 + 1) * ST], u_t[:, 2 * j + g2, :], start=True, stop=True)
                mm.then_inc(s["x_ps"], 1)
            pe.wait_ge(s["k_cp"], 4)
            fill.tensor(pe, S5_SECOND * UNIT)
            pe.wait_ge(s["toep_in"], 16 * CH)
            pe.wait_ge(s["s_rdy"], 1)
            for g in range(GR):
                j, g2 = divmod(g, 2)
                o = ps[:, 4 + g // 4, (g % 4) * P:(g % 4 + 1) * P]
                nc.tensor.matmul(o, u_t[:, g, :], toep[:, g, :], start=True, stop=False)
                nc.tensor.matmul(o, s_prev[0][:, j, :], m_re[:, j, g2, 1:9, :].rearrange("p k h -> p (k h)"), start=False, stop=False)
                mm = nc.tensor.matmul(o, s_prev[1][:, j, :], m_im[:, j, g2, 1:9, :].rearrange("p k h -> p (k h)"), start=False, stop=True)
                if g % 4 == 3:
                    mm.then_inc(s["y_ps"], 1)
            pe.wait_ge(s["y_cp"], 4)
            pe.wait_ge(fill.out, 6 * KD)
            for f in range(4):
                mt, half = divmod(f, 2)
                for q in range(4):
                    st = 4 * half + q
                    tr = nc.tensor.transpose(ps[:, f, q * P:(q + 1) * P], y[:, st, 8 * mt:8 * mt + 8, :].rearrange("p g h -> p (g h)"), I[:])
                tr.then_inc(s["yt_ps"], 1)
            pe.wait_ge(s["yt_cp"], 4)
            pe.wait_ge(s["glu_in"], 16)
            for f in range(4):
                mt, half = divmod(f, 2)
                for k in range(2):
                    rhs = y_t[:, k].rearrange("p c s -> p (c s)")[:, half * BANK:(half + 1) * BANK]
                    mm = nc.tensor.matmul(ps[:, 4 + f, :], w_glu[:, k, mt * P:(mt + 1) * P], rhs, start=(k == 0), stop=(k == 1))
                mm.then_inc(s["g_ps"], 1)

        @block.vector
        def _(dve):
            step = m.dve_step.on(dve)
            V = nc.vector
            TTo, TS, STT = V.tensor_tensor, V.tensor_scalar, V.scalar_tensor_tensor
            dve.wait_ge(m.s5_rows_in, 48)
            V.tensor_copy(rows[2].rearrange("j (g p) -> j g p", g=2),
                          m.s5_log_step.unsqueeze(2).to_broadcast([J, 2, ST])).then_inc(s["step_b"], 1)
            dve.wait_ge(s["row_t"], 1)
            for i, dst in enumerate((lre, lim, stp)):
                V.tensor_copy(dst, ps[:, 7, i * J:(i + 1) * J]).then_inc(s["row_c"], 1)
            dve.wait_ge(s["row_c"], 3)
            dve.wait_ge(s["row_t"], 2)
            for i in range(2):
                step(V.tensor_copy(cc[i].rearrange("p j h -> p (j h)"), ps[:, 6, i * P:(i + 1) * P]))
            dve.wait_ge(s["cst"], 4)
            step(V.tensor_copy(ki, ki.bitcast(I32)))
            step(V.tensor_copy(cidx_keep, cidx.bitcast(I32)))
            dve.wait_ge(s["exp1"], 1)
            step(TTo(a1, lre, stp, ALU.mult))
            step(TTo(th, lim, stp, ALU.mult))
            step(reduced(nc, step, th, tt, ta))
            kb = ki.unsqueeze(1).to_broadcast([P, J, 9])
            step(TTo(a9, kb, a1.unsqueeze(2).to_broadcast([P, J, 9]), ALU.mult))
            step(TTo(p9, kb, th.unsqueeze(2).to_broadcast([P, J, 9]), ALU.mult))
            reduced(nc, step, p9, e9, t9).then_inc(s["ang9"], 1)
            dve.wait_ge(s["ang9"], 1)
            V.tensor_copy(t8, p9[:, :, 8]).then_inc(s["ang9"], 1)
            dve.wait_ge(s["sc9"], 3)
            step(TTo(l_re, l_re, e9, ALU.mult))
            step(TTo(l_im, l_im, e9, ALU.mult))
            step(TTo(den, lre, lre, ALU.mult))
            step(TTo(tt, lim, lim, ALU.mult))
            step(TTo(den, den, tt, ALU.add))
            step(V.reciprocal(den, den))
            step(TS(ta, l_re[:, :, 1], -1.0, None, ALU.add))
            step(TTo(q_re, ta, lre, ALU.mult))
            step(TTo(tt, l_im[:, :, 1], lim, ALU.mult))
            step(TTo(q_re, q_re, tt, ALU.add))
            step(TTo(q_re, q_re, den, ALU.mult))
            step(TTo(q_im, l_im[:, :, 1], lre, ALU.mult))
            step(TTo(tt, ta, lim, ALU.mult))
            step(TTo(q_im, q_im, tt, ALU.subtract))
            step(TTo(q_im, q_im, den, ALU.mult))
            dve.wait_ge(m.s5_b_in, 64)

            def cmul(o_re, o_im, xr, xi, yr, yi, t0, t1, neg_im=False):
                step(TTo(t0, xr, yr, ALU.mult))
                step(TTo(t1, xi, yi, ALU.mult))
                step(TTo(o_re, t0, t1, ALU.subtract))
                step(TTo(t0, xr, yi, ALU.mult))
                step(TTo(t1, xi, yr, ALU.mult))
                if neg_im:
                    step(STT(out=o_im, in0=t0, scalar=-1.0, in1=t1, op0=ALU.mult, op1=ALU.subtract))
                else:
                    step(TTo(o_im, t0, t1, ALU.add))

            def over(a, n):
                return a.unsqueeze(2).to_broadcast([P, J, n])
            cmul(bb[0], bb[1], over(q_re, GC), over(q_im, GC), b[0], b[1], pq[0], pq[1])
            nine = [J, 9, GC]
            t0, t1 = cols(m.F, 10752, J, 9, GC), cols(m.F, 11904, J, 9, GC)
            lr, li = (a.unsqueeze(3).to_broadcast([P] + nine) for a in (l_re, l_im))
            cr, ci = (a.unsqueeze(2).to_broadcast([P] + nine) for a in cc)
            step(TTo(t0, lr, cr, ALU.mult))
            step(TTo(t1, li, ci, ALU.mult))
            for g2 in range(2):
                r = slice(g2 * ST, (g2 + 1) * ST)
                step(TTo(m_re[r, :, g2], t0[r], t1[r], ALU.subtract))
            step(TTo(t0, lr, ci, ALU.mult))
            step(TTo(t1, li, cr, ALU.mult))
            step(TTo(t0, t0, t1, ALU.add))
            for g2 in range(2):
                r = slice(g2 * ST, (g2 + 1) * ST)
                ins = TS(m_im[r, :, g2], t0[r], -1.0, None, ALU.mult)
                step(ins) if g2 == 0 else ins.then_inc(s["b_rdy"], 1)
            four = [P, J, CH, GC]
            lr, li = (a[:, :, 0:CH].unsqueeze(3).to_broadcast(four) for a in (l_re, l_im))
            br, bi = (a.unsqueeze(2).to_broadcast(four) for a in bb)
            cmul(w[0], w[1], lr, li, br, bi, b_rep[0], b_rep[1])
            step(V.tensor_copy(b_rep[0], br))
            V.tensor_copy(b_rep[1], bi).then_inc(s["w_rdy"], 1)
            step(V.tensor_reduce(mask16, m.ident[:].rearrange("p (a h) -> p h a", h=GC), AX.X, ALU.add))
            dmat = m.vecs[:, 0:GR * GC].rearrange("p (g h) -> p g h", h=GC)
            dve.wait_ge(s["b_rdy"], 1)
            dve.wait_ge(s["d_in"], 16)
            step(TTo(dmat, d_row, mask16.unsqueeze(1).to_broadcast([P, GR, GC]), ALU.mult))
            dve.wait_ge(s["w_ps"], 4)
            V.memset(toep, 0.0).then_inc(s["zero"], 1)
            for f in range(4):
                dve.wait_ge(s["k_ps"], f + 1)
                o = kk[:, 4 * f:4 * f + 4, :]
                src = ps[:, f, :].rearrange("p (g n) -> p g n", g=4)
                step(V.tensor_copy(o[:, :, GC:], src[:, :, GC:]))
                TTo(o[:, :, 0:GC], src[:, :, 0:GC], dmat[:, 4 * f:4 * f + 4, :], ALU.add).then_inc(s["k_cp"], 1)
            step(TTo(tab[1], t8.unsqueeze(2).to_broadcast([P, J, NCH]), cidx_keep.unsqueeze(1).to_broadcast([P, J, NCH]), ALU.mult))
            reduced(nc, step, tab[1], rho, tab[0]).then_inc(s["tab_a"], 1)
            dve.wait_ge(s["tab_a"], 1)
            step(V.tensor_copy(rho, e9[:, :, 8:9].to_broadcast([P, J, NCH])))
            step(V.memset(rho[:, :, 0:1], 0.0))
            dve.wait_ge(s["tab_s"], 2)
            dve.wait_ge(s["x_ps"], 2)
            dve.wait_ge(s["toep_in"], 16 * CH)
            x = [ps[:, 4 + 2 * i:6 + 2 * i, :].rearrange("p b (j c) -> p (b j) c", c=NCH) for i in range(2)]
            step(TTo(z_in[0], x[0], tab[0], ALU.mult))
            step(TTo(tmp, x[1], tab[1], ALU.mult))
            step(TTo(z_in[0], z_in[0], tmp, ALU.add))
            step(TTo(z_in[1], x[1], tab[0], ALU.mult))
            step(TTo(tmp, x[0], tab[1], ALU.mult))
            step(TTo(z_in[1], z_in[1], tmp, ALU.subtract))
            for i in range(2):
                flat = (a.rearrange("p j c -> p (j c)") for a in (z[i], rho, z_in[i]))
                o, d0, d1 = flat
                step(V.tensor_tensor_scan(o, d0, d1, 0.0, ALU.mult, ALU.add))
            n1 = NCH - 1
            zc = [a[:, :, 0:n1] for a in z]
            cs, sn = tab[0][:, :, 0:n1], tab[1][:, :, 0:n1]
            o_re, o_im = (a[:, :, 1:] for a in s_prev)
            step(V.memset(s_prev[0][:, :, 0:1], 0.0))
            step(V.memset(s_prev[1][:, :, 0:1], 0.0))
            step(TTo(o_re, zc[0], cs, ALU.mult))
            step(TTo(tmp[:, :, 0:n1], zc[1], sn, ALU.mult))
            step(TTo(o_re, o_re, tmp[:, :, 0:n1], ALU.subtract))
            step(TTo(o_im, zc[0], sn, ALU.mult))
            step(TTo(tmp[:, :, 0:n1], zc[1], cs, ALU.mult))
            TTo(o_im, o_im, tmp[:, :, 0:n1], ALU.add).then_inc(s["s_rdy"], 1)
            for f in range(4):
                mt, half = divmod(f, 2)
                dve.wait_ge(s["yt_ps"], f + 1)
                V.tensor_copy(y_t[:, mt, :, 4 * half:4 * half + 4].rearrange("p c s -> p s c"),
                              ps[:, f, :].rearrange("p (s c) -> p s c", s=4)).then_inc(s["yt_cp"], 1)
            dve.wait_ge(s["yt_cp"], 4)
            for f in range(4):
                mt, half = divmod(f, 2)
                cut = slice(half * BANK, (half + 1) * BANK)
                dve.wait_ge(s["g_sg"], f + 1)
                TTo(y_out(f), y_t[:, mt].rearrange("p c s -> p (c s)")[:, cut], sg[f % 2], ALU.mult).then_inc(s["g_y"], 1)
                dve.wait_ge(s["g_hi"], f + 1)
                TTo(m.br_lo[:, 4 + mt, cut], y_out(f), f32(m.br_hi[:, 4 + mt, cut]), ALU.subtract).then_inc(s["g_lo"], 1)


def after(eng, sem, value):
    if isinstance(value, int) and value <= 0:
        return
    eng.wait_ge(sem, value)


def looped(eng, first, last, body):
    body(0)
    with eng.Fori(first, last) as i:
        body(i)


def stage_combine_out(m):
    nc, ps = m.nc, m.ps
    NB = 3
    UNITS = 2 * NB
    ITERS = KD // 2
    ALL = ITERS * UNITS
    A0, A1 = 2 * KD * T, 2 * KD * T + 12 * T
    rows = cols(m.F, 0, TT, D)
    gate = [cols(m.F, i * T, T) for i in range(UNITS)]
    raw = [cols(m.F, 10240 + i * 2 * P, 2, P) for i in range(2)]
    part = [cols(m.F, 10752 + i * T, T) for i in range(NB)]
    total = [cols(m.F, 13824 + i * T, T) for i in range(2)]
    wo_raw = [cols(m.F, at, D) for at in (15872, 16896, 10752, 11776, 12800)]
    slot = (0, 1, 0, 1, 2, 3, 4, 0)
    freed_by = (None, None, 1, 2, None, None, None, 3)
    wo_hi = [cols(m.R, A1 + 2 * k * D if k < 2 else A0 + 2 * (k - 2) * D, D) for k in range(KD)]
    wo_lo = [cols(m.R, (A1 + 2 * k * D if k < 2 else A0 + 2 * (k - 2) * D) + D, D) for k in range(KD)]
    w_hi = [cols(m.R, (KD - 1) * T + 2 * i * 2 * P, 2, P) for i in range(2)]
    w_lo = [cols(m.R, (KD - 1) * T + (2 * i + 1) * 2 * P, 2, P) for i in range(2)]
    scaled_to = cols(m.F, TT * D, TT, D)
    nrm = NormAndTurn(m, "ffnn", m.g_ffn, lambda i: scaled_to[:, i, :], scaled_to)
    w_in = [m.sem(f"branch_w_in{i}") for i in range(2)]
    gate_in = [m.sem(f"gate_in{i}") for i in range(UNITS)]
    wo_in = [m.sem(f"out_w_in{k}") for k in range(KD)]
    hi_done, lo_done, proj_mm, sig_done, mul_done, add_done, sum_done, mg_hi, mg_lo = (
        m.sem(f"gates_{n}") for n in ("w_hi", "w_lo", "proj", "sigmoid", "mul", "add", "sum", "merged_hi", "merged_lo"))
    wo_hi_done, wo_lo_done, out_mm, x_add, x_in = (m.sem(f"out_{n}") for n in ("w_hi", "w_lo", "mm", "add", "x_in"))
    branch_src = m.ins["w_branch"][0].rearrange("b (k p) n -> b p k n", p=P)
    gate_src = m.scr_gate.rearrange("(d n) p t -> n p d t", n=NB)
    proj_ps = [ps[:, 2 * i:2 * i + 2, :].rearrange("p b n -> p (b n)") for i in range(2)]

    def tile_of(it, u):
        return it * 2 + u // NB, u % NB

    with nc.Block() as block:
        @block.sync
        def _(sp):
            def body(it):
                for u in range(UNITS):
                    d, n = tile_of(it, u)
                    after(sp, mul_done, it * UNITS + u - (UNITS - 1))
                    sp.dma_start(gate[u], gate_src[n][:, bass.ds(d, 1), :].rearrange("p a t -> p (a t)")).then_inc(gate_in[u], 16)
                    after(sp, lo_done, it * UNITS + u - 1)
                    sp.dma_start(raw[u % 2], branch_src[n][:, :, bass.ds(d * P, P)]).then_inc(w_in[u % 2], 16)
                    if isinstance(it, int) and u == 1:
                        for k in range(2):
                            sp.dma_start(wo_raw[slot[k]], m.ins["w_out"][0, k * P:(k + 1) * P, :]).then_inc(wo_in[k], 16)
            looped(sp, 1, ITERS, body)
            sp.wait_ge(mul_done, ALL)
            sp.dma_start(rows, m.ins["x"][0].rearrange("(i p) d -> p i d", p=P)).then_inc(x_in, 16)
            for k in range(2, KD):
                if freed_by[k]:
                    sp.wait_ge(wo_lo_done, freed_by[k])
                if k == 4:
                    sp.wait_ge(sum_done, KD)
                sp.dma_start(wo_raw[slot[k]], m.ins["w_out"][0, k * P:(k + 1) * P, :]).then_inc(wo_in[k], 16)

        @block.scalar
        def _(act):
            def split(it, u):
                if u >= UNITS:
                    it, u = it + 1, u - UNITS
                after(act, w_in[u % 2], (it * (UNITS // 2) + u // 2 + 1) * 16)
                after(act, proj_mm, it * UNITS + u - 1)
                nc.scalar.activation(w_hi[u % 2], raw[u % 2], ACT.Copy).then_inc(hi_done, 1)

            def merged_hi(d, u):
                after(act, sum_done, d + 1)
                nc.scalar.activation(m.R[:, bass.ds(d * T, T)], total[u // NB % 2], ACT.Copy).then_inc(mg_hi, 1)

            def body(it, first=False, last=False):
                for u in range(UNITS):
                    if not (last and u == UNITS - 1):
                        split(it, u + 1)
                    d, n = tile_of(it, u)
                    after(act, gate_in[u], it * 16 + 16)
                    nc.scalar.activation(gate[u], gate[u], ACT.Sigmoid).then_inc(sig_done, 1)
                    if n == 0 and not (first and u == 0):
                        merged_hi(d - 1, u + NB)
            split(0, 0)
            body(0, first=True)
            with act.Fori(1, ITERS - 1) as it:
                body(it)
            body(ITERS - 1, last=True)

            def out_split(k):
                act.wait_ge(wo_in[k], 16)
                nc.scalar.activation(wo_hi[k], wo_raw[slot[k]], ACT.Copy).then_inc(wo_hi_done, 1)
            out_split(0), out_split(1)
            merged_hi(KD - 1, NB)
            act.wait_ge(proj_mm, ALL)
            for k in range(2, KD):
                out_split(k)
            for i in range(TT):
                act.wait_ge(x_add, 2 * i + 2)
                nrm.square(act, i)
            nrm.hi(act, range(2 * KD))

        @block.vector
        def _(dve):
            def split(it, u):
                if u >= UNITS:
                    it, u = it + 1, u - UNITS
                after(dve, hi_done, it * UNITS + u + 1)
                nc.vector.tensor_tensor(w_lo[u % 2], raw[u % 2], f32(w_hi[u % 2]), ALU.subtract).then_inc(lo_done, 1)

            def sum_up(d, u):
                after(dve, add_done, d + 1)
                after(dve, mul_done, d * NB + NB)
                nc.vector.tensor_tensor(total[u // NB % 2], part[0], part[2], ALU.add).then_inc(sum_done, 1)
                after(dve, sum_done, d + 1)

            def merged_lo(d, u):
                after(dve, mg_hi, d + 1)
                nc.vector.tensor_tensor(m.R[:, bass.ds(d * T + KD * T, T)], total[u // NB % 2], f32(m.R[:, bass.ds(d * T, T)]),
                                        ALU.subtract).then_inc(mg_lo, 1)

            def body(it, first=False, last=False):
                for u in range(UNITS):
                    d, n = tile_of(it, u)
                    if n == 0 and not (first and u == 0):
                        sum_up(d - 1, u + NB)
                    if not (last and u == UNITS - 1):
                        split(it, u + 1)
                    after(dve, proj_mm, it * UNITS + u + 1)
                    after(dve, sig_done, it * UNITS + u + 1)
                    nc.vector.tensor_tensor(part[n], proj_ps[u % 2], gate[u], ALU.mult).then_inc(mul_done, 1)
                    if n == 1 and not (first and u == 1):
                        merged_lo(d - 1, u + NB)
            split(0, 0)
            body(0, first=True)
            with dve.Fori(1, ITERS - 1) as it:
                body(it)
            body(ITERS - 1, last=True)

            def out_split(k):
                dve.wait_ge(wo_hi_done, k + 1)
                nc.vector.tensor_tensor(wo_lo[k], wo_raw[slot[k]], f32(wo_hi[k]), ALU.subtract).then_inc(wo_lo_done, 1)
            out_split(0), out_split(1)
            sum_up(KD - 1, NB)
            merged_lo(KD - 1, NB)
            for k in range(2, KD):
                out_split(k)
            dve.wait_ge(x_in, 16)
            for t in range(TT):
                for half in range(2):
                    n = 2 * t + half
                    dve.wait_ge(out_mm, n + 1)
                    r = rows[:, t, half * BANK:(half + 1) * BANK]
                    nc.vector.tensor_tensor(r, ps[:, n % 8, :], r, ALU.add).then_inc(x_add, 1)
                nrm.mean(dve, t)
                if t:
                    nrm.scale(dve, t - 1)
            nrm.scale(dve, TT - 1)
            nrm.lo(dve, range(2 * KD))

        @block.gpsimd
        def _(pool):
            def body(it):
                for u in (1, NB + 1):
                    after(pool, mul_done, it * UNITS + u + 1)
                    nc.gpsimd.tensor_tensor(part[0], part[0], part[1], ALU.add).then_inc(add_done, 1)
            looped(pool, 1, ITERS, body)
            nrm.powers(pool)

        @block.tensor
        def _(pe):
            def body(it):
                for u in range(UNITS):
                    n = u % NB
                    hi, lo = w_hi[u % 2], w_lo[u % 2]
                    after(pe, lo_done, it * UNITS + u + 1)
                    after(pe, mul_done, it * UNITS + u - 1)
                    for k in range(2):
                        for w, src in ((hi, m.br_hi), (hi, m.br_lo), (lo, m.br_hi)):
                            for half in range(2):
                                cut = slice(half * BANK, (half + 1) * BANK)
                                mm = nc.tensor.matmul(proj_ps[u % 2][:, cut], w[:, k, :], src[:, 2 * n + k, cut], start=(k == 0 and w is hi and src is m.br_hi),
                                                      stop=(k == 1 and w is lo), skip_group_check=True)
                    mm.then_inc(proj_mm, 1)
            looped(pe, 1, ITERS, body)

            def out_product(n, k):
                t, half = divmod(n, 2)
                o, cut = ps[:, n % 8, :], slice(half * BANK, (half + 1) * BANK)
                hi, lo = (a[:, k, t * P:(t + 1) * P] for a in (m.h_hi, m.h_lo))
                nc.tensor.matmul(o, hi, wo_hi[k][:, cut], start=(k == 0), stop=False)
                nc.tensor.matmul(o, hi, wo_lo[k][:, cut], start=False, stop=False)
                mm = nc.tensor.matmul(o, lo, wo_hi[k][:, cut], start=False, stop=(k == KD - 1))
                if k == KD - 1:
                    mm.then_inc(out_mm, 1)
            pe.wait_ge(mul_done, ALL)
            for k in range(KD):
                pe.wait_ge(mg_lo, k + 1)
                pe.wait_ge(wo_lo_done, k + 1)
                for n in range(8):
                    out_product(n, k)
            for n in range(8, 2 * TT):
                pe.wait_ge(x_add, n - 7)
                for k in range(KD):
                    out_product(n, k)
            pe.wait_ge(x_add, 2 * TT - 4)
            nrm.turn(pe, range(2 * KD))


def stage_ffn(m):
    nc, ps = m.nc, m.ps
    FT = FF // P
    GROUPS = FT // 2
    rows = cols(m.F, 0, TT, D)
    raw = [cols(m.F, 8192 + i * T, KD, P) for i in range(4)]
    wd_raw = [cols(m.F, 12288 + i * D, D) for i in range(2)]
    conv = [cols(m.F, 14336 + i * T, T) for i in range(2)]
    gated = cols(m.F, 16384, T)
    W0 = 2 * KD * T
    w_hi = [cols(m.R, W0 + 2 * i * T, KD, P) for i in range(4)]
    w_lo = [cols(m.R, W0 + (2 * i + 1) * T, KD, P) for i in range(4)]
    a_hi, a_lo = cols(m.R, W0 + 8 * T, 2, T), cols(m.R, W0 + 10 * T, 2, T)
    d_hi, d_lo = cols(m.R, W0 + 12 * T, 2, D), cols(m.R, W0 + 14 * T, 2, D)
    w_in = [m.sem(f"up_in{i}") for i in range(4)]
    wd_in = [m.sem(f"down_in{i}") for i in range(2)]
    (hi_done, lo_done, up_mm, scaled, conv_mid, conv_done, silu_done, gated_done, a_hi_done, a_lo_done, d_hi_done, d_lo_done,
     down_mm, add_done, stored) = (m.sem(f"ffn_{n}") for n in (
         "w_hi", "w_lo", "up", "scaled", "conv_mid", "conv", "silu", "gated", "a_hi", "a_lo", "d_hi", "d_lo", "down", "add", "stored"))
    up_src = m.ins["w_up"][0].rearrange("(k p) n -> p k n", p=P)
    ups = [ps[:, 2 * i:2 * i + 2, :].rearrange("p b n -> p (b n)") for i in range(2)]
    ND = 2 * TT

    def feature(it, n):
        return it * (2 * P) + ((n // 2) * P + (n % 2) * FF)

    with nc.Block() as block:
        @block.sync
        def _(sp):
            def body(it):
                for n in range(4):
                    after(sp, lo_done, it * 4 + n - 3)
                    sp.dma_start(raw[n], up_src[:, :, bass.ds(feature(it, n), P)]).then_inc(w_in[n], 16)
                    if n % 2 == 1:
                        f = n // 2
                        after(sp, d_lo_done, it * 2 + f - 1)
                        sp.dma_start(wd_raw[f], m.ins["w_down"][0][bass.ds(it * (2 * P) + f * P, P), :]).then_inc(wd_in[f], 16)
            looped(sp, 1, GROUPS, body)
            for t in range(TT):
                sp.wait_ge(add_done, GROUPS * ND + 2 * t + 2)
                sp.dma_start(m.ins["out"][0, t * P:(t + 1) * P, :], rows[:, t, :]).then_inc(stored, 16)
            sp.wait_ge(stored, 16 * TT)

        def ahead(it, n, by=2):
            return (it, n + by) if n + by < 4 else (it + 1, n + by - 4)

        @block.scalar
        def _(act):
            def split(it, n):
                after(act, w_in[n], it * 16 + 16)
                after(act, up_mm, it * 4 + n - 3)
                nc.scalar.activation(w_hi[n], raw[n], ACT.Copy).then_inc(hi_done, 1)

            def body(it, last=False):
                for n in range(4):
                    f = n // 2
                    if not (last and n >= 2):
                        split(*ahead(it, n))
                    after(act, up_mm, it * 4 + n + 1)
                    after(act, gated_done, it * 2 + f)
                    nc.scalar.activation(conv[n % 2], ups[n % 2], ACT.Copy,
                                         scale=m.colv[:, bass.ds(2 * 44 + it * 2 + f + (n % 2) * FT, 1)]).then_inc(scaled, 1)
                    if n % 2 == 1:
                        after(act, conv_done, it * 4 + n)
                        nc.scalar.activation(conv[0], conv[0], ACT.Silu).then_inc(silu_done, 1)
                        after(act, wd_in[f], it * 16 + 16)
                        after(act, down_mm, it * ND)
                        nc.scalar.activation(d_hi[:, f, :], wd_raw[f], ACT.Copy).then_inc(d_hi_done, 1)
                        after(act, gated_done, it * 2 + f + 1)
                        nc.scalar.activation(a_hi[:, f, :], gated, ACT.Copy).then_inc(a_hi_done, 1)
            split(0, 0)
            split(0, 1)
            body(0)
            with act.Fori(1, GROUPS - 1) as it:
                body(it)
            body(GROUPS - 1, last=True)

        @block.vector
        def _(dve):
            V = nc.vector

            def split(it, n):
                after(dve, hi_done, it * 4 + n + 1)
                V.tensor_tensor(w_lo[n], raw[n], f32(w_hi[n]), ALU.subtract).then_inc(lo_done, 1)

            def adds(it):
                for n in range(ND):
                    t, half = divmod(n, 2)
                    after(dve, down_mm, it * ND + n + 1)
                    r = rows[:, t, half * BANK:(half + 1) * BANK]
                    after(dve, add_done, it * ND + n + 1)
                    V.tensor_tensor(r, ps[:, 4 + n % 4, :], r, ALU.add).then_inc(add_done, 1)

            def body(it, last=False, first=False):
                for n in range(4):
                    f = n // 2
                    if not (last and n >= 2):
                        split(*ahead(it, n))
                    after(dve, scaled, it * 4 + n + 1)
                    up, c = ups[n % 2], conv[n % 2]
                    V.scalar_tensor_tensor(out=c[:, 1:], in0=up[:, 0:T - 1], scalar=m.colv[:, bass.ds(44 + it * 2 + f + (n % 2) * FT, 1)],
                                           in1=c[:, 1:], op0=ALU.mult, op1=ALU.add).then_inc(conv_mid, 1)
                    after(dve, conv_mid, it * 4 + n + 1)
                    V.scalar_tensor_tensor(out=c[:, 2:], in0=up[:, 0:T - 2], scalar=m.colv[:, bass.ds(it * 2 + f + (n % 2) * FT, 1)],
                                           in1=c[:, 2:], op0=ALU.mult, op1=ALU.add).then_inc(conv_done, 1)
                    if n == 0 and not first:
                        adds(it - 1)
                    if n % 2 == 1:
                        after(dve, silu_done, it * 2 + f + 1)
                        after(dve, conv_done, it * 4 + n + 1)
                        after(dve, a_lo_done, it * 2 + f)
                        V.tensor_tensor(gated, conv[0], conv[1], ALU.mult).then_inc(gated_done, 1)
                        after(dve, d_hi_done, it * 2 + f + 1)
                        V.tensor_tensor(d_lo[:, f, :], wd_raw[f], f32(d_hi[:, f, :]), ALU.subtract).then_inc(d_lo_done, 1)
                        after(dve, a_hi_done, it * 2 + f + 1)
                        V.tensor_tensor(a_lo[:, f, :], gated, f32(a_hi[:, f, :]), ALU.subtract).then_inc(a_lo_done, 1)
            dve.sem_inc(add_done, ND)
            split(0, 0)
            split(0, 1)
            body(0, first=True)
            with dve.Fori(1, GROUPS - 1) as it:
                body(it)
            body(GROUPS - 1, last=True)
            adds(GROUPS - 1)

        @block.tensor
        def _(pe):
            def up(it, n):
                after(pe, lo_done, it * 4 + n + 1)
                after(pe, conv_done, it * 4 + n - 1)
                for k in range(KD):
                    for w, src in ((w_hi[n], m.h_hi), (w_hi[n], m.h_lo), (w_lo[n], m.h_hi)):
                        for half in range(2):
                            cut = slice(half * BANK, (half + 1) * BANK)
                            mm = nc.tensor.matmul(ups[n % 2][:, cut], w[:, k, :], src[:, k, cut], start=(k == 0 and w is w_hi[n] and src is m.h_hi),
                                                  stop=(k == KD - 1 and w is w_lo[n]), skip_group_check=True)
                mm.then_inc(up_mm, 1)

            def down(it):
                after(pe, a_lo_done, it * 2 + 2)
                after(pe, d_lo_done, it * 2 + 2)
                for n in range(ND):
                    t, half = divmod(n, 2)
                    after(pe, add_done, it * ND + ND + n - 3)
                    cut = slice(half * BANK, (half + 1) * BANK)
                    for f in range(2):
                        hi, lo = (a[:, f, t * P:(t + 1) * P] for a in (a_hi, a_lo))
                        o = ps[:, 4 + n % 4, :]
                        nc.tensor.matmul(o, hi, d_hi[:, f, cut], start=(f == 0), stop=False)
                        nc.tensor.matmul(o, hi, d_lo[:, f, cut], start=False, stop=False)
                        mm = nc.tensor.matmul(o, lo, d_hi[:, f, cut], start=False, stop=(f == 1))
                    mm.then_inc(down_mm, 1)

            def body(it, first=False):
                up(it, 0)
                if not first:
                    down(it - 1)
                for n in range(1, 4):
                    up(it, n)
            body(0, first=True)
            with pe.Fori(1, GROUPS) as it:
                body(it)
            down(GROUPS - 1)


def hybrid_trunk(nc, ins):
    with ExitStack() as ctx:
        m = setup(nc, ctx, ins)
        stage_load_norm_project(m)
        stage_fox(m)
        stage_mla(m)
        stage_s5(m)
        reuse_semaphores(m)
        stage_combine_out(m)
        stage_ffn(m)


_INS = ["x", "positions", "attn_norm_g", "w_in", "q_lat_norm_g", "w_uq", "kv_lat_norm_g", "w_ukv", "mla_q_norm_g", "mla_k_norm_g",
        "fox_q_norm_g", "fox_k_norm_g", "fox_f_bias", "s5_lambda_re", "s5_lambda_im", "s5_b_re", "s5_b_im", "s5_c_re", "s5_c_im",
        "s5_d", "s5_log_step", "s5_w_glu", "s5_b_glu", "w_branch", "w_out", "ffn_norm_g", "w_up", "ffn_conv_w", "w_down"]


def kernel(**inputs):
    import concourse.bacc as _bacc
    from concourse.bass_utils import run_bass_kernel_spmd as _run

    nc = _bacc.Bacc("TRN2", target_bir_lowering=False, num_devices=1)
    arrays, args = {}, {}
    for name in _INS:
        a = np.ascontiguousarray(inputs[name])
        arrays[f"in_{name}"] = a
        args[name] = nc.dram_tensor(f"in_{name}", a.shape, mybir.dt.from_np(a.dtype), kind="ExternalInput").ap()
    args["out"] = nc.dram_tensor("out_x", (1, T, D), F32, kind="ExternalOutput").ap()
    hybrid_trunk(nc, args)
    r = _run(nc, [arrays], core_ids=[0])
    return r.results[0]["out_x"]
```
